# Optimizing a Trainium2 kernel written in Bass

```python
import jax, jax.numpy as jnp
from jax import lax
import numpy as np

D_MODEL = 1024
BATCH = 1
SEQ = 1024
DEPTH = 1
DEC_BATCH = 8
DEC_SEQ = 1
PAST_LEN = 1024
PAGE_SIZE = 128

MIX_WIDTH = D_MODEL
HEAD_DIM = 64
GMLP_HEADS = MIX_WIDTH // (2 * HEAD_DIM)
GMLP_WIDTH = GMLP_HEADS * HEAD_DIM
NSA_HEADS = (MIX_WIDTH - GMLP_WIDTH) // HEAD_DIM
NSA_WIDTH = NSA_HEADS * HEAD_DIM
NSA_KV_HEADS = 2
NSA_GROUP = NSA_HEADS // NSA_KV_HEADS
KV_WIDTH = NSA_KV_HEADS * HEAD_DIM
CHUNK = 128
CMP_LEN = 32
CMP_STRIDE = 16
CMP_HID = 2 * HEAD_DIM
SEL_BLOCK = 64
N_SELECT = 8
N_LOCAL_BLOCKS = 2
WINDOW = 512
Q_BLOCK = 128
D_FF = -(-8 * D_MODEL // (3 * 256)) * 256
N_IN = 2 * GMLP_WIDTH + NSA_WIDTH + 6 * KV_WIDTH + 3 * NSA_HEADS
EPS = 1e-6

kernel_name = 'hymba_gmlp_nsa_alibi_decode_step'

def rmsnorm(x, g):
    xf = x.astype(jnp.float32)
    y = xf * lax.rsqrt(jnp.mean(xf * xf, axis=-1, keepdims=True) + EPS)
    return (y * g.astype(jnp.float32)).astype(x.dtype)

def alibi_slopes():
    h = jnp.arange(1, NSA_HEADS + 1, dtype=jnp.float32)
    return jnp.exp2(-8.0 * h / NSA_HEADS).reshape(NSA_KV_HEADS, NSA_GROUP)

def masked_softmax(s, mask):
    s = jnp.where(mask, s, -jnp.inf)
    m = jnp.max(s, axis=-1, keepdims=True)
    m = jnp.where(jnp.isfinite(m), m, 0.0)
    e = jnp.exp(s - m)
    return e / jnp.maximum(jnp.sum(e, axis=-1, keepdims=True), 1e-30)

def split_proj(h, w_in, gate_b):
    B, S, _ = h.shape
    z = h @ w_in
    u = z[..., :GMLP_WIDTH]
    v = z[..., GMLP_WIDTH:2 * GMLP_WIDTH]
    c = 2 * GMLP_WIDTH
    q = z[..., c:c + NSA_WIDTH].reshape(B, S, NSA_KV_HEADS, NSA_GROUP, HEAD_DIM)
    c += NSA_WIDTH
    kv_c = z[..., c:c + 2 * KV_WIDTH].reshape(B, S, 2, NSA_KV_HEADS, HEAD_DIM)
    c += 2 * KV_WIDTH
    kv_s = z[..., c:c + 2 * KV_WIDTH].reshape(B, S, 2, NSA_KV_HEADS, HEAD_DIM)
    c += 2 * KV_WIDTH
    kv_w = z[..., c:c + 2 * KV_WIDTH].reshape(B, S, 2, NSA_KV_HEADS, HEAD_DIM)
    c += 2 * KV_WIDTH
    gate = jax.nn.sigmoid((z[..., c:] + gate_b).astype(jnp.float32))
    gate = gate.reshape(B, S, NSA_KV_HEADS, NSA_GROUP, 3)
    return u, v, q, kv_c, kv_s, kv_w, gate

def gmlp_mix(u, v, ln_g, ln_b, w_s, b_s):
    B, L, _ = u.shape
    u = jax.nn.gelu(u).reshape(B, L, GMLP_HEADS, HEAD_DIM)
    vf = jax.nn.gelu(v).reshape(B, L, GMLP_HEADS, HEAD_DIM).astype(jnp.float32)
    mu = jnp.mean(vf, axis=-1, keepdims=True)
    var = jnp.mean(jnp.square(vf - mu), axis=-1, keepdims=True)
    vn = ((vf - mu) * lax.rsqrt(var + EPS) * ln_g + ln_b).astype(u.dtype)
    nc = -(-L // CHUNK)
    vp = jnp.pad(vn, ((0, 0), (0, nc * CHUNK - L), (0, 0), (0, 0)))
    vp = vp.reshape(B, nc, CHUNK, GMLP_HEADS, HEAD_DIM)
    causal = jnp.tril(jnp.ones((CHUNK, CHUNK), dtype=bool))
    ws = jnp.where(causal, w_s, 0)
    mixed = jnp.einsum('hts,bcshd->bcthd', ws, vp) + jnp.transpose(b_s)[None, None, :, :, None]
    mixed = mixed.reshape(B, nc * CHUNK, GMLP_HEADS, HEAD_DIM)[:, :L]
    out = (u * mixed).reshape(B, L, GMLP_WIDTH)
    last = ((L - 1) // CHUNK) * CHUNK
    return out, vn[:, last:]

def compress(k, pe, w1, b1, w2):
    B, T, G, Dh = k.shape
    n = (T - CMP_LEN) // CMP_STRIDE + 1
    idx = jnp.arange(n)[:, None] * CMP_STRIDE + jnp.arange(CMP_LEN)[None, :]
    blk = k[:, idx] + pe[None, None, :, None, :]
    blk = jnp.transpose(blk, (0, 1, 3, 2, 4)).reshape(B, n, G, CMP_LEN * Dh)
    return jax.nn.gelu(blk @ w1 + b1) @ w2

def nsa_context(kv_cmp, kv_slc, lp):
    k_c = compress(kv_cmp[:, :, 0], lp['cmp_pe_k'], lp['cmp_wk1'], lp['cmp_bk1'], lp['cmp_wk2'])
    v_c = compress(kv_cmp[:, :, 1], lp['cmp_pe_v'], lp['cmp_wv1'], lp['cmp_bv1'], lp['cmp_wv2'])
    n = k_c.shape[1]
    cmp_start = jnp.arange(n) * CMP_STRIDE
    cmp_end = cmp_start + CMP_LEN - 1
    B, T = kv_slc.shape[:2]
    ns = -(-T // SEL_BLOCK)
    kvp = jnp.pad(kv_slc, ((0, 0), (0, ns * SEL_BLOCK - T), (0, 0), (0, 0), (0, 0)))
    kvb = kvp.reshape(B, ns, SEL_BLOCK, 2, NSA_KV_HEADS, HEAD_DIM).transpose(3, 0, 4, 1, 2, 5)
    blk_lo = jnp.arange(ns) * SEL_BLOCK
    overlap = ((cmp_start[:, None] < blk_lo[None, :] + SEL_BLOCK)
               & (cmp_end[:, None] >= blk_lo[None, :])).astype(jnp.float32)
    return k_c, v_c, cmp_end, kvb[0], kvb[1], overlap

def nsa_attend(q, t, gate, k_c, v_c, cmp_end, k_sb, v_sb, overlap, k_w, v_w, w_pos):
    B, Sq = q.shape[:2]
    scale = HEAD_DIM ** -0.5
    slopes = alibi_slopes()[:, :, None, None]
    s = jnp.einsum('bqgrd,bngd->bgrqn', q, k_c, preferred_element_type=jnp.float32) * scale
    dist = t[:, None] - cmp_end[None, :]
    p_c = masked_softmax(s - slopes * dist.astype(jnp.float32), dist >= 0)
    o_c = jnp.einsum('bgrqn,bngd->bqgrd', p_c.astype(v_c.dtype), v_c)
    imp = jnp.einsum('bgqn,nj->bgqj', jnp.sum(p_c, axis=2), overlap)
    ns = overlap.shape[1]
    j = jnp.arange(ns)[None, :]
    cur = (t // SEL_BLOCK)[:, None]
    valid = j * SEL_BLOCK <= t[:, None]
    forced = (j == 0) | ((j <= cur) & (j > cur - N_LOCAL_BLOCKS))
    imp = jnp.where(valid, jnp.where(forced, jnp.inf, imp), -jnp.inf)
    n_sel = min(N_SELECT, ns)
    _, idx = lax.top_k(imp, n_sel)
    gather = jax.vmap(jax.vmap(lambda blocks, ids: blocks[ids]))
    k_g = gather(k_sb, idx)
    v_g = gather(v_sb, idx)
    pos = idx[..., None] * SEL_BLOCK + jnp.arange(SEL_BLOCK)
    dist = (t[None, None, :, None, None] - pos).reshape(B, NSA_KV_HEADS, 1, Sq, n_sel * SEL_BLOCK)
    s = jnp.einsum('bqgrd,bgqnkd->bgrqnk', q, k_g, preferred_element_type=jnp.float32) * scale
    s = s.reshape(B, NSA_KV_HEADS, NSA_GROUP, Sq, n_sel * SEL_BLOCK)
    p_s = masked_softmax(s - slopes * dist.astype(jnp.float32), dist >= 0)
    p_s = p_s.reshape(B, NSA_KV_HEADS, NSA_GROUP, Sq, n_sel, SEL_BLOCK)
    o_s = jnp.einsum('bgrqnk,bgqnkd->bqgrd', p_s.astype(v_g.dtype), v_g)
    s = jnp.einsum('bqgrd,bwgd->bgrqw', q, k_w, preferred_element_type=jnp.float32) * scale
    dist = t[:, None] - w_pos[None, :]
    mask = (dist >= 0) & (dist < WINDOW) & (w_pos[None, :] >= 0)
    p_w = masked_softmax(s - slopes * dist.astype(jnp.float32), mask)
    o_w = jnp.einsum('bgrqw,bwgd->bqgrd', p_w.astype(v_w.dtype), v_w)
    o = gate[..., 0, None] * o_c + gate[..., 1, None] * o_s + gate[..., 2, None] * o_w
    return o.astype(q.dtype).reshape(B, Sq, NSA_WIDTH)

def mix_prompt(h, lp):
    B, S, _ = h.shape
    u, v, q, kv_c, kv_s, kv_w, gate = split_proj(h, lp['w_in'], lp['gate_b'])
    o_a, v_rows = gmlp_mix(u, v, lp['gmlp_ln_g'], lp['gmlp_ln_b'], lp['gmlp_ws'], lp['gmlp_bs'])
    k_c, v_c, cmp_end, k_sb, v_sb, overlap = nsa_context(kv_c, kv_s, lp)
    qb = min(Q_BLOCK, S)
    kw_pad = jnp.pad(kv_w, ((0, 0), (WINDOW, 0), (0, 0), (0, 0), (0, 0)))

    def one_block(i):
        qs = i * qb
        t = qs + jnp.arange(qb)
        band = lax.dynamic_slice_in_dim(kw_pad, qs, WINDOW + qb, axis=1)
        w_pos = qs - WINDOW + jnp.arange(WINDOW + qb)
        return nsa_attend(lax.dynamic_slice_in_dim(q, qs, qb, axis=1), t,
                          lax.dynamic_slice_in_dim(gate, qs, qb, axis=1),
                          k_c, v_c, cmp_end, k_sb, v_sb, overlap,
                          band[:, :, 0], band[:, :, 1], w_pos)

    o_b = lax.map(one_block, jnp.arange(S // qb))
    o_b = jnp.transpose(o_b, (1, 0, 2, 3)).reshape(B, S, NSA_WIDTH)
    keep = min(WINDOW, S)
    return o_a, o_b, kv_c, kv_s, kv_w[:, S - keep:], v_rows

def mix_sample(h, cache_c, cache_s, win_state, page_table, lp):
    DB, DS, _ = h.shape
    past = page_table.shape[1] * cache_c.shape[1]
    u, v, q, kv_c, kv_s, kv_w, gate = split_proj(h, lp['w_in'], lp['gate_b'])
    o_a, v_rows = gmlp_mix(u, v, lp['gmlp_ln_g'], lp['gmlp_ln_b'], lp['gmlp_ws'], lp['gmlp_bs'])
    past_c = cache_c[page_table].reshape(DB, past, 2, NSA_KV_HEADS, HEAD_DIM)
    past_s = cache_s[page_table].reshape(DB, past, 2, NSA_KV_HEADS, HEAD_DIM)
    k_c, v_c, cmp_end, k_sb, v_sb, overlap = nsa_context(
        jnp.concatenate([past_c, kv_c], axis=1), jnp.concatenate([past_s, kv_s], axis=1), lp)
    t = past + jnp.arange(DS)
    wb = win_state.shape[1]
    win_all = jnp.concatenate([win_state, kv_w], axis=1)
    w_pos = past - wb + jnp.arange(wb + DS)
    o_b = nsa_attend(q, t, gate, k_c, v_c, cmp_end, k_sb, v_sb, overlap,
                     win_all[:, :, 0], win_all[:, :, 1], w_pos)
    return o_a, o_b, kv_c, kv_s, win_all[:, DS:], v_rows

def layer_tail(x, o_a, o_b, lp):
    o = jnp.concatenate([rmsnorm(o_a, lp['out_norm_a']), rmsnorm(o_b, lp['out_norm_b'])], axis=-1)
    x = x + o @ lp['w_out']
    h = rmsnorm(x, lp['norm2_g'])
    return x + (jax.nn.silu(h @ lp['w_gate']) * (h @ lp['w_up'])) @ lp['w_down']

def setup_inputs(seed: int = 0) -> dict:
    key = jax.random.key(seed)
    it = iter(list(jax.random.split(key, 32)))

    def nrm(shape, scale):
        return scale * jax.random.normal(next(it), shape, jnp.float32)

    n_pages = PAST_LEN // PAGE_SIZE
    n_used = DEC_BATCH * n_pages
    n_pool = (n_used * 5 + 3) // 4
    win_buf = min(WINDOW, PAST_LEN)
    kvs = (2, NSA_KV_HEADS, HEAD_DIM)
    x_prompt = nrm((BATCH, SEQ, D_MODEL), 1.0)
    x_sample = nrm((DEC_BATCH, DEC_SEQ, D_MODEL), 1.0)
    cache_kv_cmp = nrm((DEPTH, n_pool, PAGE_SIZE) + kvs, 1.0)
    cache_kv_slc = nrm((DEPTH, n_pool, PAGE_SIZE) + kvs, 1.0)
    state_win_kv = nrm((DEPTH, DEC_BATCH, win_buf) + kvs, 1.0)
    perm = jax.random.permutation(next(it), n_pool)
    page_table = perm[:n_used].reshape(DEC_BATCH, n_pages).astype(jnp.int32)
    return {
        'x_prompt': x_prompt,
        'x_sample': x_sample,
        'cache_kv_cmp': cache_kv_cmp,
        'cache_kv_slc': cache_kv_slc,
        'state_win_kv': state_win_kv,
        'page_table': page_table,
        'norm1_g': 1.0 + nrm((DEPTH, D_MODEL), 0.1),
        'w_in': nrm((DEPTH, D_MODEL, N_IN), D_MODEL ** -0.5),
        'gate_b': nrm((DEPTH, 3 * NSA_HEADS), 0.1),
        'gmlp_ln_g': 1.0 + nrm((DEPTH, GMLP_HEADS, HEAD_DIM), 0.1),
        'gmlp_ln_b': nrm((DEPTH, GMLP_HEADS, HEAD_DIM), 0.02),
        'gmlp_ws': nrm((DEPTH, GMLP_HEADS, CHUNK, CHUNK), 0.5 * CHUNK ** -0.5),
        'gmlp_bs': 1.0 + nrm((DEPTH, GMLP_HEADS, CHUNK), 0.1),
        'cmp_pe_k': nrm((DEPTH, CMP_LEN, HEAD_DIM), 0.1),
        'cmp_wk1': nrm((DEPTH, CMP_LEN * HEAD_DIM, CMP_HID), (CMP_LEN * HEAD_DIM) ** -0.5),
        'cmp_bk1': nrm((DEPTH, CMP_HID), 0.02),
        'cmp_wk2': nrm((DEPTH, CMP_HID, HEAD_DIM), CMP_HID ** -0.5),
        'cmp_pe_v': nrm((DEPTH, CMP_LEN, HEAD_DIM), 0.1),
        'cmp_wv1': nrm((DEPTH, CMP_LEN * HEAD_DIM, CMP_HID), (CMP_LEN * HEAD_DIM) ** -0.5),
        'cmp_bv1': nrm((DEPTH, CMP_HID), 0.02),
        'cmp_wv2': nrm((DEPTH, CMP_HID, HEAD_DIM), CMP_HID ** -0.5),
        'out_norm_a': 1.0 + nrm((DEPTH, GMLP_WIDTH), 0.1),
        'out_norm_b': 1.0 + nrm((DEPTH, NSA_WIDTH), 0.1),
        'w_out': nrm((DEPTH, MIX_WIDTH, D_MODEL), MIX_WIDTH ** -0.5),
        'norm2_g': 1.0 + nrm((DEPTH, D_MODEL), 0.1),
        'w_gate': nrm((DEPTH, D_MODEL, D_FF), D_MODEL ** -0.5),
        'w_up': nrm((DEPTH, D_MODEL, D_FF), D_MODEL ** -0.5),
        'w_down': nrm((DEPTH, D_FF, D_MODEL), D_FF ** -0.5),
        'final_norm_g': 1.0 + nrm((D_MODEL,), 0.1),
    }

def reference(x_prompt, x_sample, cache_kv_cmp, cache_kv_slc, state_win_kv, page_table,
              norm1_g, w_in, gate_b, gmlp_ln_g, gmlp_ln_b, gmlp_ws, gmlp_bs,
              cmp_pe_k, cmp_wk1, cmp_bk1, cmp_wk2, cmp_pe_v, cmp_wv1, cmp_bv1, cmp_wv2,
              out_norm_a, out_norm_b, w_out, norm2_g, w_gate, w_up, w_down, final_norm_g):
    xp, xs = x_prompt, x_sample
    p_cmp, p_slc, p_win, p_gv = [], [], [], []
    s_cmp, s_slc, s_win, s_gv = [], [], [], []
    for l in range(DEPTH):
        lp = {
            'w_in': w_in[l], 'gate_b': gate_b[l],
            'gmlp_ln_g': gmlp_ln_g[l], 'gmlp_ln_b': gmlp_ln_b[l],
            'gmlp_ws': gmlp_ws[l], 'gmlp_bs': gmlp_bs[l],
            'cmp_pe_k': cmp_pe_k[l], 'cmp_wk1': cmp_wk1[l], 'cmp_bk1': cmp_bk1[l], 'cmp_wk2': cmp_wk2[l],
            'cmp_pe_v': cmp_pe_v[l], 'cmp_wv1': cmp_wv1[l], 'cmp_bv1': cmp_bv1[l], 'cmp_wv2': cmp_wv2[l],
            'out_norm_a': out_norm_a[l], 'out_norm_b': out_norm_b[l], 'w_out': w_out[l],
            'norm2_g': norm2_g[l], 'w_gate': w_gate[l], 'w_up': w_up[l], 'w_down': w_down[l],
        }
        o_a, o_b, kc, ks, kw, gv = mix_prompt(rmsnorm(xp, norm1_g[l]), lp)
        xp = layer_tail(xp, o_a, o_b, lp)
        p_cmp.append(kc); p_slc.append(ks); p_win.append(kw); p_gv.append(gv)
        o_a, o_b, kc, ks, kw, gv = mix_sample(rmsnorm(xs, norm1_g[l]), cache_kv_cmp[l], cache_kv_slc[l],
                                              state_win_kv[l], page_table, lp)
        xs = layer_tail(xs, o_a, o_b, lp)
        s_cmp.append(kc); s_slc.append(ks); s_win.append(kw); s_gv.append(gv)
    y_prompt = rmsnorm(xp, final_norm_g)
    y_sample = rmsnorm(xs, final_norm_g)
    return (y_prompt, y_sample,
            jnp.stack(p_cmp), jnp.stack(p_slc), jnp.stack(p_win), jnp.stack(p_gv),
            jnp.stack(s_cmp), jnp.stack(s_slc), jnp.stack(s_win), jnp.stack(s_gv))


_drawn_inputs = setup_inputs


def setup_inputs(seed=0):
    import zlib

    import numpy as np

    out = dict(_drawn_inputs(seed))
    spreads = {}
    factors = {'gmlp_ln_b': 2.732, 'cmp_pe_k': 8.0, 'cmp_bk1': 52.98, 'cmp_bv1': 6.16}
    for name, (base, spread) in spreads.items():
        noise = np.random.default_rng([zlib.crc32(name.encode()), seed]).standard_normal(out[name].shape)
        drawn = base * np.exp(spread * noise) if base else spread * noise
        out[name] = __import__('jax').numpy.asarray(drawn.astype(out[name].dtype))
    for name, factor in factors.items():
        out[name] = (out[name] * factor).astype(out[name].dtype)
    return out
```

```python
from contextlib import ExitStack

import numpy as np
import concourse.bass as bass
from concourse import mybir

F32 = mybir.dt.float32
F32R = mybir.dt.float32r
BF16 = mybir.dt.bfloat16
I32 = mybir.dt.int32
ACT = mybir.ActivationFunctionType
ALU = mybir.AluOpType
AX = mybir.AxisListType.X

P = 128
D = 1024
KD = D // P
SEQ = 1024
NT = SEQ // P
NB = 8
PAST = 1024
PAGES = 8
DH = 64
GH = 8
NH = 8
NG = 2
NR = 4
KVW = 256
N_IN = 2328
FF = 2816
CMP_N = 63
NBLK = 16
SEL = 64
EPS = 1e-6
NEG = -1e30
FORCED = 1e30
PICKED = 3e38
XT = NT + 1
TOK = SEQ + NB
KAUG = 97


def rows(t):
    return P if t < NT else NB


def constants():
    bf = mybir.dt.np(BF16)
    f = np.float32
    slope = 2.0 ** -np.arange(1, NH + 1)
    t = np.arange(SEQ)
    q, k = np.arange(P)[:, None], np.arange(P)[None, :]
    c = {}
    c["ident"] = np.eye(P, dtype=f)
    c["ident_bf"] = np.eye(P).astype(bf)
    c["upper01"] = (q <= k).astype(f)
    c["mask_diag"] = np.where(k <= q, 0, NEG).astype(bf)
    c["mask_low"] = np.where(k > q, 0, NEG).astype(bf)
    end = 16 * np.arange(64) + 31
    cm = np.where((end[None, :] <= t[:, None]) & (np.arange(64) < CMP_N)[None, :], 0, NEG)
    c["mask_cmp"] = np.ascontiguousarray(cm.reshape(NT, P, 64).transpose(1, 0, 2)).astype(bf)

    def kaug(pos, second):
        a = np.zeros((33, len(pos)), f)
        a[16 * second + pos // SEL, np.arange(len(pos))] = 1
        a[32] = pos % SEL
        return a
    c["kaug"] = np.stack([kaug(t, 0), kaug(t, 0), kaug(t, 1), kaug(t, 1)], 1)
    c["kaug_cmp"] = np.stack([kaug(np.minimum(end, SEQ - 1), 1)] * 2, 1)
    qa = np.zeros((NT, 33, NG, NR, P), f)
    for i in range(NT):
        for g in range(NG):
            for r in range(NR):
                s = slope[g * NR + r]
                blk = s * (SEL * np.arange(NBLK) - P * i)
                qa[i, 0:16, g, r] = blk[:, None]
                qa[i, 16:32, g, r] = blk[:, None]
                qa[i, 32, g, r] = s
    c["qaug"] = qa.reshape(NT, 33, NH * P)
    j = np.arange(NBLK)[None, :]
    cur = (t // SEL)[:, None]
    forced = (j == 0) | ((j <= cur) & (j > cur - 2))
    add = np.where(j * SEL <= t[:, None], np.where(forced, FORCED, 0.0), NEG)
    c["imp_add"] = np.ascontiguousarray(add.reshape(NT, P, NBLK).transpose(1, 0, 2)).astype(f)
    row = np.arange(NB * NH)
    sl = slope[row % NH][:, None]
    c["same_group"] = ((row[:, None] // NR) == (row[None, :] // NR)).astype(f)
    c["seq_rows"] = (np.arange(NB)[:, None] == row[None, :] // NH).astype(f)
    c["rows_seq"] = np.ascontiguousarray(c["seq_rows"].T)
    c["head_pick"] = np.repeat((np.arange(NH)[None, :] == (row % NH)[:, None]), 3, 1).astype(f)
    c["t_slc"] = (-sl * (PAST - np.arange(PAST + 1))[None, :]).astype(f)
    w = np.arange(512).reshape(P, 4).T.reshape(-1)
    dist = 512 - w
    tw = np.where(dist[None, :] < 512, -sl * dist[None, :], NEG)
    c["t_win"] = np.concatenate([tw, np.zeros((64, 1))], 1).astype(f)
    c["t_cmp"] = (-sl * (PAST - end[None, :CMP_N])).astype(f)
    c["imp_add_s"] = np.broadcast_to(np.where(np.isin(np.arange(17), (0, 15, 16)), FORCED, 0.0), (64, 17)).astype(f)
    return {k_: np.ascontiguousarray(v) for k_, v in c.items()}


CONST_SHAPES = {k_: (v.shape, v.dtype) for k_, v in constants().items()}
RAW_INPUTS = ["x_prompt", "x_sample", "cache_kv_cmp", "cache_kv_slc", "state_win_kv", "page_table", "norm1_g", "w_in",
              "gate_b", "gmlp_ln_g", "gmlp_ln_b", "gmlp_ws", "gmlp_bs", "cmp_pe_k", "cmp_wk1", "cmp_bk1", "cmp_wk2",
              "cmp_pe_v", "cmp_wv1", "cmp_bv1", "cmp_wv2", "out_norm_a", "out_norm_b", "w_out", "norm2_g", "w_gate",
              "w_up", "w_down", "final_norm_g"]
OUTPUTS = [("y_prompt", (1, SEQ, D)), ("y_sample", (NB, 1, D)), ("p_kv_cmp", (1, 1, SEQ, 2, NG, DH)),
           ("p_kv_slc", (1, 1, SEQ, 2, NG, DH)), ("p_win_kv", (1, 1, 512, 2, NG, DH)),
           ("p_gmlp_v", (1, 1, P, GH, DH)), ("s_kv_cmp", (1, NB, 1, 2, NG, DH)), ("s_kv_slc", (1, NB, 1, 2, NG, DH)),
           ("s_win_kv", (1, NB, 512, 2, NG, DH)), ("s_gmlp_v", (1, NB, 1, GH, DH))]


def build_program(nc, A, C, O):
    ctx = ExitStack()

    sb_at = {}

    def sb(name, shape, dt=F32):
        sb_at[name] = -(-nc.sbuf_base // 32) * 32
        return ctx.enter_context(nc.sbuf_tensor(name, shape, dt))

    def rounded(name, shape, base, word=0):
        return nc.alloc_sbuf_tensor_at(name, shape, F32R, offset=sb_at[base] + 4 * word)

    def sem(name):
        return ctx.enter_context(nc.semaphore(name))

    bank = [ctx.enter_context(nc.psum_tensor(f"bankpair{i}", [P, 1024], F32)) for i in range(4)]

    def pb(i):
        return bank[i // 2][:, 512 * (i % 2):512 * (i % 2) + 512]

    x_all = sb("x_all", [P, XT, D])
    hT = sb("hT", [P, KD, TOK])
    hT_flat = hT[:, :, :].rearrange("p k n -> p (k n)")
    q_all = sb("q_all", [P, 4, TOK])
    kT_space = sb("kT_space", [P, 4 * SEQ])
    kT = kT_space[0:KAUG, :].rearrange("p (c n) -> p c n", c=4)
    v_all = sb("v_all", [P, NT, 2, P])
    oaT = sb("oaT", [P, 4, TOK])
    kcT_p = sb("kcT_p", [KAUG, NG, 64])
    vc_p = sb("vc_p", [64, P])
    ident = sb("ident", [P, P])
    ident_bf = sb("ident_bf", [P, P], BF16)
    mask_diag = sb("mask_diag", [P, P], BF16)
    mask_low = sb("mask_low", [P, P], BF16)
    mask_cmp = sb("mask_cmp", [P, NT, 64], BF16)
    imp_add = sb("imp_add", [P, NT, NBLK])
    norm_g = sb("norm_g", [P, D])
    normb_g = sb("normb_g", [P, 512])
    gate = sb("gate", [P, XT, 24])
    samp = sb("samp", [P, 1304])
    kv_new = samp[0:NB, 0:792]
    q_s = samp[0:NB, 792:1304]
    ob_s = sb("ob_s", [NB, 512])
    minus_half = sb("minus_half", [P, 8])
    small = sb("small", [P, 144])
    lnr = sb("lnr", [P, 3, GH])
    pages = ob_s[0:1, 0:NB * PAGES].bitcast(I32)
    regC = sb("regC", [P, 2770])
    arena = sb("arena", [P, 13824])

    def at(off, shape, base=None):
        n = int(np.prod(shape))
        v = (arena if base is None else base)[:, off:off + n]
        if len(shape) == 2:
            v = v.rearrange("p (a b) -> p a b", a=shape[0])
        elif len(shape) == 3:
            v = v.rearrange("p (a b c) -> p a b c", a=shape[0], b=shape[1])
        elif len(shape) == 4:
            v = v.rearrange("p (a b c d) -> p a b c d", a=shape[0], b=shape[1], c=shape[2])
        return v

    class Chain:

        def __init__(self, eng, s):
            self.eng, self.s, self.n = eng, s, 0

        def link(self, ins):
            self.n += 1
            ins.then_inc(self.s, 1)
            self.eng.wait_ge(self.s, self.n)

    vec_chain, act_chain, pool_chain = sem("vec_chain"), sem("act_chain"), sem("pool_chain")

    def inv_rms(pool, link, total, out, width):
        link(pool.tensor_scalar(out, total, 1.0 / width, EPS, ALU.mult, ALU.add))
        n = out.shape[1]
        return pool.tensor_tensor(out, out, minus_half[0:out.shape[0], 0:n], ALU.pow)

    def norm_rows(v):
        return v.rearrange("(a n) -> a n", a=1)

    wslot = [at(0, [KD, 512]), at(4096, [KD, 512])]
    kvst = at(8192, [2, 512])
    h_ring = at(9216, [2, D])
    sq_big = at(11264, [D])
    ws_raw = at(12288, [GH, P])
    vg = at(9216, [2, 512])
    u_sb = at(10240, [2, 512])
    oa = at(11264, [2, 512])
    sq = at(12288, [512])
    wsT = at(0, [GH, P], regC)
    ln_g = at(1024, [512], regC)
    ln_b = at(1536, [512], regC)
    norma_g = at(2048, [512], regC)
    gate_b = at(2560, [24], regC)
    bs_raw = at(2584, [P], regC)
    bsT = at(2712, [GH], regC)
    w00 = at(2720, [GH], regC)
    b00 = at(2728, [GH], regC)
    upper = at(13312, [P])
    ssx, ssa = small[:, 0:9], small[:, 9:18]
    rx, ra = small[:, 18:27], small[:, 27:36]

    CH = [(1536, 512), (2048, 280), (1024, 512), (0, 512), (512, 512)]

    x_in = [sem(f"x_in{t}") for t in range(XT)]
    ident_in, const_in = sem("ident_in"), sem("const_in")
    w_in_ready = [sem(f"w_in_ready{c}") for c in range(5)]
    zeroed = sem("zeroed")
    x_squared, x_scaled_by, h_ready = sem("x_squared"), sem("x_scaled_by"), sem("h_ready")
    h_turned, hT_low, hT_high = sem("h_turned"), sem("hT_low"), sem("hT_high")
    ws_turned, ws_masked = sem("ws_turned"), sem("ws_masked")
    z_ready, z_taken = sem("z_ready"), sem("z_taken")
    k_turned, kT_ready, v_kept = sem("k_turned"), sem("kT_ready"), sem("v_kept")
    kv_stored = [sem("kv_stored0"), sem("kv_stored1")]
    new_stored, gv_stored = sem("new_stored"), sem("gv_stored")
    gate_raw, gate_tanh, gate_ready = sem("gate_raw"), sem("gate_tanh"), sem("gate_ready")
    v_centered, v_squared, v_var, v_inv, vn_ready = (sem("v_centered"), sem("v_squared"), sem("v_var"),
                                                     sem("v_inv"), sem("vn_ready"))
    mixed, oa_ready, oa_squared, oa_inv = sem("mixed"), sem("oa_ready"), sem("oa_squared"), sem("oa_inv")
    oan_ready, oa_turned, oaT_ready = sem("oan_ready"), sem("oa_turned"), sem("oaT_ready")
    win_copied = sem("win_copied")

    loads1 = [
        (ident[:, :], C["ident"]), (norm_g[:, :], norm_rows(A["norm1_g"][0]).to_broadcast([P, D])), (upper, C["upper01"]),
        (ws_raw, A["gmlp_ws"][0].rearrange("h t s -> t h s")), (bs_raw[0:GH, :], A["gmlp_bs"][0]),
        (ln_g, norm_rows(A["gmlp_ln_g"][0].rearrange("h d -> (h d)")).to_broadcast([P, 512])),
        (ln_b, norm_rows(A["gmlp_ln_b"][0].rearrange("h d -> (h d)")).to_broadcast([P, 512])),
        (norma_g, norm_rows(A["out_norm_a"][0]).to_broadcast([P, 512])),
        (normb_g[:, :], norm_rows(A["out_norm_b"][0]).to_broadcast([P, 512])),
        (gate_b, norm_rows(A["gate_b"][0]).to_broadcast([P, 24])),
        (w00[0:NB, :], A["gmlp_ws"][0, :, 0, 0:1].rearrange("h o -> o h").to_broadcast([NB, GH])),
        (b00[0:NB, :], A["gmlp_bs"][0, :, 0:1].rearrange("h o -> o h").to_broadcast([NB, GH])),
        (ident_bf[:, :], C["ident_bf"]), (mask_diag[:, :], C["mask_diag"]), (mask_low[:, :], C["mask_low"]),
        (mask_cmp[:, :, :], C["mask_cmp"]), (imp_add[:, :, :], C["imp_add"]),
        (kT[64:KAUG, :, :], C["kaug"]), (kcT_p[64:KAUG, :, :], C["kaug_cmp"]), (pages[:, :], norm_rows(A["page_table"].rearrange("b p -> (b p)"))),
    ]

    def x_dram(t):
        return A["x_prompt"][0, P * t:P * t + P, :] if t < NT else A["x_sample"][:, 0, :]

    def load_w_in(sp, c):
        c0, w = CH[c]
        if c >= 2:
            sp.wait_ge(z_ready, 9 * (c - 1))
        sp.dma_start(wslot[c % 2][:, :, 0:w], A["w_in"][0].rearrange("(k p) n -> p k n", p=P)[:, :, c0:c0 + w])\
          .then_inc(w_in_ready[c], 16)

    def stage1_sync(sp):
        with nc.allow_non_contiguous_dma(reason="one value per head of the sample mixer"):
            sp.dma_start(x_all[:, 0, :], x_dram(0)).then_inc(x_in[0], 16)
            for dst, src in loads1[:2]:
                sp.dma_start(dst, src).then_inc(ident_in, 16)
            sp.dma_start(x_all[:, 1, :], x_dram(1)).then_inc(x_in[1], 16)
            load_w_in(sp, 0)
            for t in range(2, XT):
                sp.dma_start(x_all[0:rows(t), t, :], x_dram(t)).then_inc(x_in[t], 16)
            for dst, src in loads1[2:]:
                sp.dma_start(dst, src).then_inc(const_in, 16)
            load_w_in(sp, 1)
            sp.dma_start(O["s_win_kv"][0, :, 0:511].rearrange("b w k g d -> b (w k g d)"),
                         A["state_win_kv"][0, :, 1:512].rearrange("b w k g d -> b (w k g d)")).then_inc(win_copied, 16)
            for c in (2, 3, 4):
                load_w_in(sp, c)

    ALL_CONST = 16 * (len(loads1) - 2)

    def zn(c, t):
        return 9 * c + t if c < 3 else 27 + 2 * t + (c - 3)

    def stage1_tensor(pe):
        pe.wait_ge(ident_in, 32)

        def turn_ws():
            pe.wait_ge(const_in, ALL_CONST)
            for h in range(GH):
                ins = pe.transpose(pb(6 + h // 4)[:, P * (h % 4):P * (h % 4) + P], ws_raw[:, h, :], ident[:, :])
            ins.then_inc(ws_turned, 1)
            pe.transpose(pb(3)[:, 0:GH], bs_raw[0:GH, :], ident[0:GH, 0:GH]).then_inc(ws_turned, 1)

        def turn_h(t):
            n = rows(t)
            pe.wait_ge(h_ready, t + 1)
            if t >= 1:
                pe.wait_ge(hT_low, t)
                pe.wait_ge(hT_high, t)
            for k in range(KD):
                ins = pe.transpose(pb(4 + k // 4)[:, P * (k % 4):P * (k % 4) + n],
                                   h_ring[0:n, t % 2, P * k:P * k + P], ident[0:n, 0:n])
            ins.then_inc(h_turned, 1)

        def project(c, t):
            n, w, at_n = rows(t), CH[c][1], zn(c, t)
            pe.wait_ge(w_in_ready[c], 16)
            if c == 0:
                pe.wait_ge(hT_low, t + 1)
                pe.wait_ge(hT_high, t + 1)
            if at_n >= 4:
                pe.wait_ge(z_taken, at_n - 3)
            if at_n == 3:
                pe.wait_ge(ws_masked, 3)
            for k in range(KD):
                ins = pe.matmul(pb(at_n % 4)[0:n, 0:w], hT[:, k, P * t:P * t + n], wslot[c % 2][:, k, 0:w],
                                start=(k == 0), stop=(k == KD - 1))
            ins.then_inc(z_ready, 1)

        def turn_k(m):
            c, t = m // NT, m % NT
            pe.wait_ge(z_taken, zn(c, t) + 1)
            if m == 0:
                pe.wait_ge(ws_masked, 2)
            if m >= 2:
                pe.wait_ge(kT_ready, m - 1)
            col = 256 if c == 0 else 0
            for g in range(NG):
                ins = pe.transpose(pb(6 + m % 2)[0:DH, P * g:P * g + P], kvst[:, m % 2, col + DH * g:col + DH * g + DH],
                                   ident[:, :])
            ins.then_inc(k_turned, 1)

        turn_h(0)
        turn_h(1)
        for t in range(XT):
            project(0, t)
            if t >= 1:
                turn_k(t - 1)
            if t + 2 < XT:
                turn_h(t + 2)
            if t == 0:
                turn_ws()
        for t in range(XT):
            project(1, t)
            if t >= 1:
                turn_k(NT + t - 1)
        for t in range(XT):
            project(2, t)

        def mix(t):
            pe.wait_ge(vn_ready, t + 1)
            if t >= 2:
                pe.wait_ge(oa_ready, t - 1)
            else:
                pe.wait_ge(kT_ready, 2 * NT)
            for h in range(GH):
                ins = pe.matmul(pb(6 + t % 2)[:, DH * h:DH * h + DH], wsT[:, h, :], vg[:, t % 2, DH * h:DH * h + DH],
                                start=True, stop=True)
            ins.then_inc(mixed, 1)

        def turn_oa(t):
            n = rows(t)
            pe.wait_ge(oan_ready, t + 1)
            if t >= 2:
                pe.wait_ge(oaT_ready, t - 1)
            for k in range(4):
                ins = pe.transpose(pb(4 + t % 2)[:, P * k:P * k + n], oa[0:n, t % 2, P * k:P * k + P], ident[0:n, 0:n])
            ins.then_inc(oa_turned, 1)

        for t in range(XT + 2):
            if t < XT:
                project(3, t)
            if 1 <= t <= NT:
                mix(t - 1)
            if 2 <= t:
                turn_oa(t - 2)
            if t < XT:
                project(4, t)

    def stage1_scalar(act):
        chain = Chain(act, act_chain)
        for t in range(2):
            square_x(act, t)
        for t in range(XT):
            take_hT(act, t)
            if t + 2 < XT:
                square_x(act, t + 2)
            take_z(act, 0, t)
        for c in (1, 2):
            for t in range(XT):
                take_z(act, c, t)
        act.wait_ge(gate_raw, XT + 1)
        act.activation(gate[:, :, :], gate[:, :, :], ACT.Tanh, scale=0.5).then_inc(gate_tanh, 1)
        for t in range(XT + 2):
            if t < XT:
                take_z(act, 3, t)
            if t >= 1 and t - 1 < XT:
                n = rows(t - 1)
                act.wait_ge(oa_ready, t)
                if t >= 2:
                    act.wait_ge(oa_squared, t - 1)
                act.activation(sq[0:n, :], oa[0:n, (t - 1) % 2, :], ACT.Square, accum_out=ssa[0:n, t - 1:t])\
                   .then_inc(oa_squared, 1)
            if t >= 2:
                n = rows(t - 2)
                act.wait_ge(oa_turned, t - 1)
                act.activation(oaT[:, :, P * (t - 2):P * (t - 2) + n],
                               pb(4 + t % 2).rearrange("p (k n) -> p k n", k=4)[:, :, 0:n], ACT.Copy)\
                   .then_inc(oaT_ready, 1)
            if t < XT:
                take_z(act, 4, t)
                n = rows(t)
                act.wait_ge(v_centered, t + 1)
                if t >= 1:
                    act.wait_ge(v_var, t)
                    act.wait_ge(oa_squared, t)
                act.activation(sq[0:n, :], vg[0:n, t % 2, :], ACT.Square).then_inc(v_squared, 1)

    def square_x(act, t):
        n = rows(t)
        act.wait_ge(x_in[t], 16)
        if t >= 1:
            act.wait_ge(x_squared, t)
        act.activation(sq_big[0:n, :], x_all[0:n, t, :], ACT.Square, accum_out=ssx[0:n, t:t + 1]).then_inc(x_squared, 1)

    def take_hT(act, t):
        n = rows(t)
        act.wait_ge(h_turned, t + 1)
        act.activation(hT[:, 0:4, P * t:P * t + n], pb(4).rearrange("p (k n) -> p k n", k=4)[:, :, 0:n], ACT.Copy)\
           .then_inc(hT_low, 1)

    def take_z(act, c, t):
        n, w, at_n = rows(t), CH[c][1], zn(c, t)
        z = pb(at_n % 4)[0:n, 0:w]
        act.wait_ge(z_ready, at_n + 1)
        if c < 2 and t < NT:
            m = c * NT + t
            if m >= 2:
                act.wait_ge(k_turned, m - 1)
                act.wait_ge(v_kept, m - 1)
                act.wait_ge(kv_stored[m % 2], stores_before(m))
                if c == 1 and t >= 2:
                    act.wait_ge(gate_raw, t)
            act.activation(kvst[0:n, m % 2, 0:w], z, ACT.Copy).then_inc(z_taken, 1)
        elif c < 2:
            act.activation(kv_new[:, 512 * c:512 * c + w], z, ACT.Copy).then_inc(z_taken, 1)
        elif c == 2:
            dst = q_all[:, :, P * t:P * t + P] if t < NT else q_s
            src = z.rearrange("p (k n) -> p k n", k=4) if t < NT else z
            act.activation(dst, src, ACT.Copy, scale=DH ** -0.5).then_inc(z_taken, 1)
        elif c == 3:
            if t >= 2:
                act.wait_ge(oa_ready, t - 1)
            else:
                act.wait_ge(h_turned, XT)
            act.activation(u_sb[0:n, t % 2, :], z, ACT.Gelu_apprx_tanh).then_inc(z_taken, 1)
        else:
            if t >= 2:
                act.wait_ge(mixed, t - 1)
            if t >= 2:
                act.wait_ge(vn_ready, t - 1)
            act.activation(vg[0:n, t % 2, :], z, ACT.Gelu_apprx_tanh).then_inc(z_taken, 1)

    def stores_before(m):
        def stored(j):
            return 2 if j < NT else (1 if j - NT >= 4 else 0)
        return 16 * sum(stored(j) for j in range(m % 2, m - 1, 2))

    def stage1_pool(pool):
        chain = Chain(pool, pool_chain)
        pool.memset(minus_half[:, :], -0.5).then_inc(zeroed, 1)
        pool.memset(gate[:, :, :], 0.0).then_inc(gate_raw, 1)
        pool.wait_ge(zeroed, 1)

        def inv_x(t):
            pool.wait_ge(x_squared, t + 1)
            inv_rms(pool, chain.link, ssx[0:rows(t), t:t + 1], rx[0:rows(t), t:t + 1], D).then_inc(x_scaled_by, 1)

        def store_kv(c, t):
            m = c * NT + t
            pool.wait_ge(z_taken, zn(c, t) + 1)
            if t < NT:
                col = 384 if c == 0 else 128
                pool.tensor_copy(v_all[:, t, c, :], kvst[:, m % 2, col:col + P]).then_inc(v_kept, 1)
                r = slice(P * t, P * t + P)
                flat = "s k g d -> s (k g d)"
                if c == 0:
                    pool.dma_start(O["p_kv_cmp"][0, 0, r].rearrange(flat), kvst[:, m % 2, 0:256])\
                        .then_inc(kv_stored[m % 2], 16)
                    pool.dma_start(O["p_kv_slc"][0, 0, r].rearrange(flat), kvst[:, m % 2, 256:512])\
                        .then_inc(kv_stored[m % 2], 16)
                elif t >= 4:
                    pool.dma_start(O["p_win_kv"][0, 0, P * (t - 4):P * (t - 4) + P].rearrange(flat),
                                   kvst[:, m % 2, 0:256]).then_inc(kv_stored[m % 2], 16)
            elif c == 0:
                flat = "b s k g d -> b (s k g d)"
                pool.dma_start(O["s_kv_cmp"][0].rearrange(flat), kv_new[:, 0:256]).then_inc(new_stored, 16)
                pool.dma_start(O["s_kv_slc"][0].rearrange(flat), kv_new[:, 256:512]).then_inc(new_stored, 16)
            else:
                pool.dma_start(O["s_win_kv"][0, :, 511].rearrange("b k g d -> b (k g d)"), kv_new[:, 512:768])\
                    .then_inc(new_stored, 16)

        inv_x(0)
        inv_x(1)
        for t in range(XT):
            if t + 2 < XT:
                inv_x(t + 2)
            store_kv(0, t)
        for t in range(XT):
            store_kv(1, t)
        for t in range(XT + 1):
            if t >= 1:
                pool.wait_ge(oa_squared, t)
                n = rows(t - 1)
                inv_rms(pool, chain.link, ssa[0:n, t - 1:t], ra[0:n, t - 1:t], 512).then_inc(oa_inv, 1)
            if t < XT:
                n = rows(t)
                pool.wait_ge(v_var, t + 1)
                inv_rms(pool, chain.link, lnr[0:n, 1, :], lnr[0:n, 2, :], DH).then_inc(v_inv, 1)
                if t >= NT - 1:
                    pool.wait_ge(vn_ready, t + 1)
                    if t == NT - 1:
                        dst = O["p_gmlp_v"][0, 0].rearrange("s h d -> s (h d)")
                    else:
                        dst = O["s_gmlp_v"][0].rearrange("b s h d -> b (s h d)")
                    pool.dma_start(dst, vg[0:n, t % 2, :]).then_inc(gv_stored, 16)
        return chain

    def stage1_vector(dve):
        chain = Chain(dve, vec_chain)
        link = chain.link
        dve.wait_ge(ident_in, 32)

        def scale_h(t):
            n = rows(t)
            dve.wait_ge(x_scaled_by, t + 1)
            if t >= 2:
                dve.wait_ge(h_turned, t - 1)
            dve.scalar_tensor_tensor(out=h_ring[0:n, t % 2, :], in0=x_all[0:n, t, :], scalar=rx[0:n, t:t + 1],
                                     in1=norm_g[0:n, :], op0=ALU.mult, op1=ALU.mult).then_inc(h_ready, 1)

        def take_hT_high(t):
            n = rows(t)
            dve.wait_ge(h_turned, t + 1)
            dve.tensor_copy(hT[:, 4:8, P * t:P * t + n], pb(5).rearrange("p (k n) -> p k n", k=4)[:, :, 0:n])\
               .then_inc(hT_high, 1)

        def take_kT(m):
            c, t = m // NT, m % NT
            dve.wait_ge(k_turned, m + 1)
            dve.tensor_copy(kT[0:DH, 2 * c:2 * c + 2, P * t:P * t + P],
                            pb(6 + m % 2)[0:DH, 0:256].rearrange("p (g n) -> p g n", g=2)).then_inc(kT_ready, 1)

        scale_h(0)
        scale_h(1)

        def mask_ws():
            dve.wait_ge(const_in, ALL_CONST)
            dve.wait_ge(ws_turned, 2)
            for b in range(2):
                dve.tensor_tensor(wsT[:, 4 * b:4 * b + 4, :], pb(6 + b).rearrange("p (h n) -> p h n", h=4),
                                  upper[:, None, :].to_broadcast([P, 4, P]), ALU.mult).then_inc(ws_masked, 1)
            dve.tensor_copy(bsT, pb(3)[:, 0:GH]).then_inc(ws_masked, 1)

        for t in range(XT):
            take_hT_high(t)
            if t + 2 < XT:
                scale_h(t + 2)
            if t == 1:
                mask_ws()
            if t >= 1:
                take_kT(t - 1)

        def add_gate_b(t):
            n = rows(t)
            dve.wait_ge(z_taken, zn(1, t) + 1)
            if t == 0:
                dve.wait_ge(gate_raw, 1)
            src = kvst[0:n, t % 2, 256:280] if t < NT else kv_new[:, 768:792]
            dve.tensor_tensor(gate[0:n, t, :], src, gate_b[0:n, :], ALU.add).then_inc(gate_raw, 1)

        for t in range(XT):
            add_gate_b(t)
            if t >= 1:
                take_kT(NT + t - 1)
        dve.wait_ge(gate_tanh, 1)
        dve.tensor_scalar(gate[:, :, :], gate[:, :, :], 0.5, 0.5, ALU.mult, ALU.add).then_inc(gate_ready, 1)

        def per_head(a, n):
            return a[0:n, :, None].to_broadcast([n, GH, DH])

        def heads(a, n, slot):
            return a[0:n, slot, :].rearrange("p (h d) -> p h d", h=GH)

        def layer_norm(t):
            n = rows(t)
            v = heads(vg, n, t % 2)
            dve.wait_ge(z_taken, zn(4, t) + 1)
            link(dve.tensor_reduce(lnr[0:n, 0, :], v, AX, ALU.add))
            link(dve.tensor_scalar(lnr[0:n, 0, :], lnr[0:n, 0, :], -1.0 / DH, None, ALU.mult))
            dve.tensor_tensor(v, v, per_head(lnr[:, 0, :], n), ALU.add).then_inc(v_centered, 1)
            dve.wait_ge(v_squared, t + 1)
            dve.tensor_reduce(lnr[0:n, 1, :], sq[0:n, :].rearrange("p (h d) -> p h d", h=GH), AX, ALU.add)\
               .then_inc(v_var, 1)
            dve.wait_ge(v_inv, t + 1)
            link(dve.tensor_tensor(v, v, per_head(lnr[:, 2, :], n), ALU.mult))
            link(dve.tensor_tensor(vg[0:n, t % 2, :], vg[0:n, t % 2, :], ln_g[0:n, :], ALU.mult))
            dve.tensor_tensor(vg[0:n, t % 2, :], vg[0:n, t % 2, :], ln_b[0:n, :], ALU.add).then_inc(vn_ready, 1)

        def gate_mixed(t):
            n = rows(t)
            o = heads(oa, n, t % 2)
            if t >= 2:
                dve.wait_ge(oa_turned, t - 1)
            if t < NT:
                dve.wait_ge(mixed, t + 1)
                link(dve.tensor_tensor(o, pb(6 + t % 2).rearrange("p (h d) -> p h d", h=GH), per_head(bsT, n), ALU.add))
            else:
                dve.wait_ge(vn_ready, XT)
                link(dve.tensor_tensor(o, heads(vg, n, t % 2), per_head(w00, n), ALU.mult))
                link(dve.tensor_tensor(o, o, per_head(b00, n), ALU.add))
            dve.tensor_tensor(oa[0:n, t % 2, :], oa[0:n, t % 2, :], u_sb[0:n, t % 2, :], ALU.mult).then_inc(oa_ready, 1)

        def norm_oa(t):
            n = rows(t)
            dve.wait_ge(oa_inv, t + 1)
            dve.scalar_tensor_tensor(out=oa[0:n, t % 2, :], in0=oa[0:n, t % 2, :], scalar=ra[0:n, t:t + 1],
                                     in1=norma_g[0:n, :], op0=ALU.mult, op1=ALU.mult).then_inc(oan_ready, 1)

        for t in range(XT + 1):
            if t >= 1:
                gate_mixed(t - 1)
            if t < XT:
                layer_norm(t)
            if t >= 1:
                norm_oa(t - 1)
        return chain

    w1 = [at(0, [16, P]), at(2048, [16, P])]
    raw = [at(4096, [4, 512]), at(6144, [4, 512])]
    sorted_rows = at(11264, [4, 4, P])
    hid = [at(8192, [4, 64]), at(8448, [4, 64])]
    w2 = [at(8704, [DH]), at(8768, [DH])]
    b1 = at(8832, [2])
    pe_raw = at(8834, [2, P])
    peT = at(9090, [2, 16])
    hid_bias = at(9122, [2])
    kcT_s = at(9216, [NB, NG, 64])
    vc_s = at(10240, [NB, P])
    pairsT = at(0, [2, 4, 8, 64], hT_flat), at(4096, [2, 4, 8, 64], hT_flat)
    NS = NB + 1

    w_cmp_ready = sem("w_cmp_ready")
    raw_ready = [sem("raw_ready0"), sem("raw_ready1")]
    raw_ready_pool = [sem("raw_ready_pool0"), sem("raw_ready_pool1")]
    pe_turned, pe_taken, bias_summed, bias_ready = sem("pe_turned"), sem("pe_taken"), sem("bias_summed"), sem("bias_ready")
    sorted_even, sorted_odd, pairs_turned = sem("sorted_even"), sem("sorted_odd"), sem("pairs_turned")
    pairs_even, pairs_odd = sem("pairs_even"), sem("pairs_odd")
    hid_summed, hid_ready = sem("hid_summed"), sem("hid_ready")
    cmp_summed, kc_ready, vc_ready = sem("cmp_summed"), sem("kc_ready"), sem("vc_ready")

    def stage2_sync(sp):
        sp.wait_ge(z_ready, 9 * 5)
        sp.wait_ge(z_taken, 9 * 5)
        names = [("cmp_wk1", "cmp_wk2", "cmp_bk1", "cmp_pe_k"), ("cmp_wv1", "cmp_wv2", "cmp_bv1", "cmp_pe_v")]
        sp.wait_ge(oaT_ready, XT)
        sp.wait_ge(gv_stored, 32)
        for slot in range(2):
            sp.wait_ge(kv_stored[slot], stores_before(2 * NT + slot))
        for kv in range(2):
            n1, n2, nb, npe = names[kv]
            for b in range(2):
                sp.dma_start(w1[kv][:, 8 * b:8 * b + 8, :], A[n1][0, D * b:D * b + D].rearrange("(r p) h -> p r h", p=P))\
                  .then_inc(w_cmp_ready, 16)
            sp.dma_start(w2[kv], A[n2][0]).then_inc(w_cmp_ready, 16)
            sp.dma_start(b1[:, kv:kv + 1], A[nb][0].rearrange("(h o) -> h o", o=1)).then_inc(w_cmp_ready, 16)
            sp.dma_start(pe_raw[0:16, kv, :], A[npe][0].rearrange("(r t) d -> r (t d)", t=2)).then_inc(w_cmp_ready, 16)
        for s in range(NS):
            if s < NB:
                load_raw(sp, s, 0, raw_ready)
            else:
                wait_raw_free(sp, s)
                src = O["p_kv_cmp"][0, 0].rearrange("(a r t) k g d -> r a (t k g d)", r=P, t=2)
                sp.dma_start(raw[s % 2][:, :, :], src).then_inc(raw_ready[s % 2], 16)

    def wait_raw_free(eng, s):
        if s >= 2:
            eng.wait_ge(sorted_even, 2 * (s - 1))
            eng.wait_ge(sorted_odd, 2 * (s - 1))

    def load_raw(eng, s, half, done):
        pool_rows = A["cache_kv_cmp"][0].rearrange("n (r t) k g d -> n r (t k g d)", t=2)
        wait_raw_free(eng, s)
        with eng.Fori(0, 4) as a:
            page = eng.value_load(pages[0:1, bass.ds(a * 2 + (s * PAGES + half), 1)], min_val=0,
                                  max_val=pool_rows.shape[0] - 1)
            eng.dma_start(raw[s % 2][64 * half:64 * half + 64, bass.ds(a, 1), :],
                          pool_rows[bass.ds(page, 1)].rearrange("o r c -> r o c")).then_inc(done[s % 2], 16)

    def sort_rows(eng, copy, s, a, done):
        if a < 2:
            eng.wait_ge(raw_ready[s % 2], 64 * (s // 2 + 1) if s < NB else 64 * (s // 2) + 16)
            if s < NB:
                eng.wait_ge(raw_ready_pool[s % 2], 64 * (s // 2 + 1))
        if s >= 1:
            eng.wait_ge(pairs_turned, 4 * (s - 1) + a + 1)
        copy(sorted_rows[:, a].rearrange("p c (t d) -> p t c d", t=2),
             raw[s % 2][:, a].rearrange("p (t c d) -> p t c d", t=2, c=4)).then_inc(done, 1)

    def group_seqs(w):
        return [s for s in (2 * w, 2 * w + 1) if s < NS]

    NW = (NS + 1) // 2

    def stage2_pool(pool):
        pool.wait_ge(const_in, ALL_CONST)
        pool.wait_ge(z_ready, 9 * 5)
        for s in range(NB):
            load_raw(pool, s, 1, raw_ready_pool)

    def stage2_tensor(pe):
        pe.wait_ge(w_cmp_ready, 160)
        pe.wait_ge(oaT_ready, XT)
        for kv in range(2):
            ins = pe.transpose(pb(4)[:, 16 * kv:16 * kv + 16], pe_raw[0:16, kv, :], ident[0:16, 0:16])
        ins.then_inc(pe_turned, 1)
        pe.wait_ge(pe_taken, 1)
        for kv in range(2):
            for r in range(16):
                ins = pe.matmul(pb(5)[:, kv:kv + 1], w1[kv][:, r, :], peT[:, kv, r:r + 1], start=(r == 0), stop=(r == 15))
        ins.then_inc(bias_summed, 1)

        def turn_pairs(s):
            for a in range(4):
                n = 4 * s + a
                pe.wait_ge(sorted_odd if a % 2 else sorted_even, 2 * s + a // 2 + 1)
                if n >= 4:
                    if n % 2 == 0:
                        pe.wait_ge(pairs_even, (n - 4) // 2 + 1)
                    else:
                        pe.wait_ge(pairs_odd, (n - 4) // 2 + 1)
                else:
                    pe.wait_ge(z_taken, 45)
                for kvg in range(4):
                    ins = pe.transpose(pb(n % 4)[:, P * kvg:P * kvg + P], sorted_rows[:, a, kvg, :], ident[:, :])
                ins.then_inc(pairs_turned, 1)

        def hidden(w):
            ns = len(group_seqs(w))
            pe.wait_ge(pairs_even, 2 * (2 * w + ns))
            pe.wait_ge(pairs_odd, 2 * (2 * w + ns))
            if w == 0:
                pe.wait_ge(bias_ready, 1)
            else:
                pe.wait_ge(hid_ready, 2 * w)
            for kv in range(2):
                for r in range(16):
                    b = r // 8
                    mov = pairsT[w % 2][:, 0:ns, 2 * kv:2 * kv + 2, r % 8, b:b + CMP_N]
                    out = pb(4 + kv)[:, 0:2 * ns * CMP_N].rearrange("p (s g n) -> p s g n", s=ns, g=NG)
                    ins = pe.matmul(out, w1[kv][:, r, :], mov, start=(r == 0), stop=(r == 15))
                ins.then_inc(hid_summed, 1)

        def compressed(w):
            ns = len(group_seqs(w))
            m = 2 * ns
            pe.wait_ge(hid_ready, 2 * w + 2)
            if w >= 1:
                pe.wait_ge(kc_ready, w)
                pe.wait_ge(vc_ready, w)
            pe.matmul(pb(6)[0:DH, 0:m * CMP_N].rearrange("p (m n) -> p m n", m=m), w2[0], hid[0][:, 0:m, 0:CMP_N],
                      start=True, stop=True)
            for j in range(m):
                ins = pe.matmul(pb(7)[0:CMP_N, DH * j:DH * j + DH], hid[1][:, j, 0:CMP_N], w2[1], start=True, stop=True)
            ins.then_inc(cmp_summed, 1)

        for w in range(NW):
            for s in group_seqs(w):
                turn_pairs(s)
            if w >= 1:
                compressed(w - 1)
            hidden(w)
        compressed(NW - 1)

    def take_pairs(eng_copy, n, done):
        s, a = n // 4, n % 4
        dst = pairsT[(s // 2) % 2][:, s % 2, :, :, 16 * a:16 * a + 16]
        src = pb(n % 4).rearrange("p (c h r) -> p c r h", c=4, r=8)
        for c in range(4):
            ins = eng_copy(dst[:, c], src[:, c])
        ins.then_inc(done, 1)

    def stage2_scalar(act):
        def hid_gelu(w):
            ns = len(group_seqs(w))
            m = 2 * ns
            for kv in range(2):
                act.wait_ge(hid_summed, 2 * w + kv + 1)
                if w == 0:
                    act.wait_ge(bias_ready, 1)
                else:
                    act.wait_ge(cmp_summed, w)
                act.activation(hid[kv][:, 0:m, 0:CMP_N], pb(4 + kv)[:, 0:m * CMP_N].rearrange("p (m n) -> p m n", m=m),
                               ACT.Gelu_apprx_tanh, bias=hid_bias[:, kv:kv + 1]).then_inc(hid_ready, 1)

        for w in range(NW):
            for s in group_seqs(w):
                for a in (1, 3):
                    sort_rows(act, lambda d, i: act.activation(d, i, ACT.Copy), s, a, sorted_odd)
                for a in (1, 3):
                    n = 4 * s + a
                    act.wait_ge(pairs_turned, n + 1)
                    if s % 2 == 0 and w >= 2:
                        act.wait_ge(hid_summed, 2 * (w - 1))
                    take_pairs(lambda d, i: act.activation(d, i, ACT.Copy), n, pairs_odd)
            hid_gelu(w)

    def stage2_vector(dve, chain):
        dve.wait_ge(pe_turned, 1)
        dve.tensor_copy(peT, pb(4)[:, 0:32].rearrange("p (a r) -> p a r", a=2)).then_inc(pe_taken, 1)
        dve.wait_ge(bias_summed, 1)
        dve.tensor_tensor(hid_bias, pb(5)[:, 0:2], b1, ALU.add).then_inc(bias_ready, 1)

        def keep(w):
            seqs = group_seqs(w)
            m = 2 * len(seqs)
            dve.wait_ge(cmp_summed, w + 1)
            k_src = pb(6)[0:DH, 0:m * CMP_N].rearrange("p (m n) -> p m n", m=m)
            v_src = pb(7)[0:CMP_N, 0:DH * m]
            if seqs[0] < NB:
                dve.tensor_copy(kcT_s[0:DH, 2 * w:2 * w + 2, :, 0:CMP_N].rearrange("p s g n -> p (s g) n"), k_src)\
                   .then_inc(kc_ready, 1)
                dve.tensor_copy(vc_s[0:CMP_N, 2 * w:2 * w + 2, :].rearrange("p s c -> p (s c)"), v_src).then_inc(vc_ready, 1)
            else:
                dve.tensor_copy(kcT_p[0:DH, :, 0:CMP_N], k_src).then_inc(kc_ready, 1)
                dve.tensor_copy(vc_p[0:CMP_N, :], v_src).then_inc(vc_ready, 1)

        for w in range(NW):
            for s in group_seqs(w):
                for a in (0, 2):
                    sort_rows(dve, dve.tensor_copy, s, a, sorted_even)
                for a in (0, 2):
                    n = 4 * s + a
                    dve.wait_ge(pairs_turned, n + 1)
                    if s % 2 == 0 and w >= 2:
                        dve.wait_ge(hid_summed, 2 * (w - 1))
                    take_pairs(dve.tensor_copy, n, pairs_even)
            if w >= 1:
                keep(w - 1)
        keep(NW - 1)

    NTILE = 12
    kv_st = [at(0, [NTILE, P], regC), at(0, [NTILE, P]), at(NTILE * P, [NTILE, P])]
    kTs = at(0, [2, NTILE * P], hT_flat)
    t_slc = at(3072, [PAST + 1])
    t_win = at(4097, [513])
    t_cmp = at(4610, [CMP_N])
    imp_add_s = at(4673, [17])
    s_slc = at(5120, [PAST + 1])
    s_win = at(6145, [513])
    s_cmp = at(6660, [CMP_N])
    imp_pad = at(6724, [65])
    imp_s = at(6790, [17])
    imp_hit = at(6807, [17])
    top_s = at(6824, [8])
    sel_s = at(6832, [17])
    st_s = at(6850, [16])
    pT_slc = at(7168, [8, 64])
    pT_win = at(7680, [4, 64])
    sT_sb = at(7936, [NTILE, 64])
    same_group = at(8704, [64])
    seq_rows = at(8768, [64])
    rows_seq = at(8832, [8])
    head_pick = at(8840, [24])
    gate_rows = at(8864, [24])
    p_new = at(8888, [2, 8])
    gates_s = at(8904, [3])
    scT = at(8960, [64])
    pcT_s = at(9024, [64])
    pnT = at(9088, [2, 64])
    q_bd = at(11264, [NB, NH])
    qTs = at(11328, [NB, NH])
    knT = at(11392, [2, NB])
    q_s2 = at(11408, [NR, NG, DH])
    oT_s = at(11920, [64])

    table_ready = sem("table_ready")
    kv_in = [sem(f"kv_in{i}") for i in range(3)]
    kv_in_pool = [sem(f"kv_in_pool{i}") for i in range(3)]
    q_sorted, prep_turned, prep_taken = sem("q_sorted"), sem("prep_turned"), sem("prep_taken")
    cmp_scored, cmp_cols, cmp_turned, pc_ready = sem("cmp_scored"), sem("cmp_cols"), sem("cmp_turned"), sem("pc_ready")
    imp_summed = sem("imp_summed")
    k_tiles_turned, k_even, k_odd = sem("k_tiles_turned"), sem("k_even"), sem("k_odd")
    seq_scored, cols_taken, rows_turned = sem("seq_scored"), sem("cols_taken"), sem("rows_turned")
    max_s, exp_s, ps_ready = sem("max_s"), sem("exp_s"), sem("ps_ready")
    p_turned, pT_taken, seq_valued = sem("p_turned"), sem("pT_taken"), sem("seq_valued")
    oT_taken, o_turned, ob_s_ready = sem("oT_taken"), sem("o_turned"), sem("ob_s_ready")

    def stream_kv(eng, half, done, window):
        rows_of = A["cache_kv_slc"][0].rearrange("n t k g d -> n t k (g d)")
        win_of = A["state_win_kv"][0].rearrange("b (p c) k g d -> b p c k (g d)", c=4)
        for v in range(2 * NB):
            kv, s = v // NB, v % NB
            if v == 1:
                eng.wait_ge(hid_summed, 2 * NW)
                eng.wait_ge(cmp_summed, NW)
            if 3 <= v < NB + 3:
                eng.wait_ge(k_tiles_turned, 3 * (v - 2))
            elif v >= 3:
                eng.wait_ge(seq_valued, v - 2 - NB)
            with eng.Fori(0, PAGES // 2) as j:
                page = eng.value_load(pages[0:1, bass.ds(j * 2 + (s * PAGES + half), 1)], min_val=0,
                                      max_val=rows_of.shape[0] - 1)
                eng.dma_start(kv_st[v % 3][:, bass.ds(j * 2 + half, 1), :],
                              rows_of[bass.ds(page, 1), :, kv, :].rearrange("o t c -> t o c")).then_inc(done[v % 3], 16)
            if window:
                eng.dma_start(kv_st[v % 3][:, 8:12, :], win_of[s, :, :, kv, :]).then_inc(done[v % 3], 16)
                if v == 0:
                    load_tables(eng)

    def wait_stream(eng, v):
        eng.wait_ge(kv_in[v % 3], 80 * (v // 3 + 1))
        eng.wait_ge(kv_in_pool[v % 3], 64 * (v // 3 + 1))

    def load_tables(sp):
        sp.wait_ge(hid_summed, 2 * NW)
        sp.wait_ge(cmp_summed, NW)
        for dst, name, n in ((t_slc, "t_slc", 64), (t_win, "t_win", 64), (t_cmp, "t_cmp", 64),
                             (imp_add_s, "imp_add_s", 64), (same_group, "same_group", 64), (seq_rows, "seq_rows", 8),
                             (rows_seq, "rows_seq", 64), (head_pick, "head_pick", 64)):
            sp.dma_start(dst[0:n], C[name]).then_inc(table_ready, 16)

    def stage3_sync(sp):
        stream_kv(sp, 0, kv_in, True)

    def stage3_pool(pool):
        stream_kv(pool, 1, kv_in_pool, False)

    def stage3_tensor(pe):
        pe.wait_ge(table_ready, 128)
        pe.wait_ge(q_sorted, 1)
        pe.wait_ge(kc_ready, NW)
        pe.wait_ge(vc_ready, NW)
        pe.wait_ge(gate_ready, 1)
        for r in range(NR):
            pe.transpose(pb(0)[:, NB * r:NB * r + NB], q_s2[0:NB, r].rearrange("p g d -> p (g d)"), ident[0:NB, 0:NB])
        for h in range(NH):
            pe.transpose(pb(0)[0:DH, 32 + NB * h:40 + NB * h], q_s[:, DH * h:DH * h + DH], ident[0:NB, 0:NB])
        for br, col in ((0, 256), (1, 512)):
            pe.transpose(pb(0)[:, 96 + NB * br:104 + NB * br], kv_new[:, col:col + P], ident[0:NB, 0:NB])
        pe.matmul(pb(1)[0:64, 0:24], seq_rows[0:NB, :], gate[0:NB, NT, :], start=True, stop=True).then_inc(prep_turned, 1)
        pe.wait_ge(prep_taken, 1)
        for s in range(NB):
            for g in range(NG):
                ins = pe.matmul(pb(1)[0:CMP_N, 64 + NH * s + NR * g:64 + NH * s + NR * g + NR], kcT_s[0:DH, s, g, 0:CMP_N],
                                qTs[0:DH, s, NR * g:NR * g + NR], start=True, stop=True)
        ins.then_inc(cmp_scored, 1)

        def turn_keys(s):
            wait_stream(pe, s)
            for j in range(3):
                n = 3 * s + j
                if n >= 4:
                    if n % 2 == 0:
                        pe.wait_ge(k_even, (n - 4) // 2 + 1)
                    else:
                        pe.wait_ge(k_odd, (n - 4) // 2 + 1)
                for c in range(4):
                    ins = pe.transpose(pb(4 + n % 4)[:, P * c:P * c + P], kv_st[s % 3][:, 4 * j + c, :], ident[:, :])
                ins.then_inc(k_tiles_turned, 1)

        def score(s):
            n = 3 * s + 3
            pe.wait_ge(k_even, (n + 1) // 2)
            pe.wait_ge(k_odd, n // 2)
            for c in range(NTILE):
                out = pb(2)[:, 64 * c + NH * s:64 * c + NH * s + NH] if c < 8 else \
                    pb(3)[:, 64 * (c - 8) + NH * s:64 * (c - 8) + NH * s + NH]
                ins = pe.matmul(out, kTs[:, s % 2, P * c:P * c + P], q_bd[:, s, :], start=True, stop=True)
            ins.then_inc(seq_scored, 1)

        def turn_cmp():
            pe.wait_ge(cmp_cols, 1)
            pe.transpose(pb(1)[0:64, 128:128 + CMP_N], scT[0:CMP_N, :], ident[0:CMP_N, 0:CMP_N]).then_inc(cmp_turned, 1)

        def sum_importance():
            pe.wait_ge(pc_ready, 1)
            pe.matmul(pb(1)[0:64, 192:192 + CMP_N], same_group[0:64, :], s_cmp[0:64, :], start=True, stop=True)\
              .then_inc(imp_summed, 1)

        turn_keys(0)
        turn_cmp()
        for s in range(1, NB):
            turn_keys(s)
            score(s - 1)
            if s == 2:
                sum_importance()
        score(NB - 1)
        q_all_rows = q_bd.rearrange("p s h -> p (s h)")
        for br in range(2):
            ins = pe.matmul(pb(1)[0:64, 256 + 8 * br:264 + 8 * br], q_all_rows, knT[:, br, :], start=True, stop=True)
        ins.then_inc(seq_scored, 1)
        pe.wait_ge(cols_taken, 2)
        pe.wait_ge(k_even, 12)
        pe.wait_ge(k_odd, 12)
        for c in range(NTILE):
            ins = pe.transpose(pb(4 + c // 4)[0:64, P * (c % 4):P * (c % 4) + P], sT_sb[:, c, :], ident[:, :])
        ins.then_inc(rows_turned, 1)
        pe.wait_ge(ps_ready, 3)
        for c in range(4):
            pe.transpose(pb(6)[:, 64 * c:64 * c + 64], s_win[0:64, P * c:P * c + P], ident[0:64, 0:64])
        for c in range(8):
            pe.transpose(pb(7)[:, 64 * c:64 * c + 64], s_slc[0:64, P * c:P * c + P], ident[0:64, 0:64])
        for br in range(2):
            pe.transpose(pb(1)[0:NB, 300 + 64 * br:364 + 64 * br], p_new[0:64, br, :], ident[0:64, 0:64])
        pe.transpose(pb(1)[0:CMP_N, 432:496], s_cmp[0:64, :], ident[0:64, 0:64]).then_inc(p_turned, 1)
        pe.wait_ge(pT_taken, 4)
        o = pb(0)[:, 0:64]
        for br, col in ((0, 384), (1, 640)):
            pe.matmul(o, kv_new[:, col:col + P], pnT[0:NB, br, :], start=(br == 0), stop=False, skip_group_check=True)
        for s in range(NB):
            v = NB + s
            wait_stream(pe, v)
            cols = slice(NH * s, NH * s + NH)
            pe.matmul(o[:, cols], vc_s[0:CMP_N, s, :], pcT_s[0:CMP_N, cols], start=False, stop=False, skip_group_check=True)
            for c in range(NTILE):
                pr = pT_slc[:, c, cols] if c < 8 else pT_win[:, c - 8, cols]
                ins = pe.matmul(o[:, cols], kv_st[v % 3][:, c, :], pr, start=False, stop=(c == NTILE - 1),
                                skip_group_check=True)
            ins.then_inc(seq_valued, 1)
        pe.wait_ge(oT_taken, 1)
        for h in range(NH):
            g = h // NR
            ins = pe.transpose(pb(7 - g)[0:NB, DH * h:DH * h + DH], oT_s[DH * g:DH * g + DH, h:64:NH],
                               ident[DH * g:DH * g + DH, DH * g:DH * g + DH])
        ins.then_inc(o_turned, 1)

    def stage3_scalar(act):
        for n in range(1, 3 * NB, 2):
            s, j = n // 3, n % 3
            act.wait_ge(k_tiles_turned, n + 1)
            if s >= 2:
                act.wait_ge(seq_scored, s - 1)
            act.activation(kTs[:, s % 2, 512 * j:512 * j + 512], pb(4 + n % 4), ACT.Copy).then_inc(k_odd, 1)
            if n == 3:
                act.wait_ge(max_s, 1)
                act.activation(s_cmp[0:64, :], s_cmp[0:64, :], ACT.Exp, bias=st_s[0:64, 0:1],
                               accum_out=st_s[0:64, 3:4]).then_inc(exp_s, 1)
        act.wait_ge(seq_scored, NB)
        act.activation(sT_sb[:, 0:8, :], pb(2).rearrange("p (c n) -> p c n", c=8), ACT.Copy).then_inc(cols_taken, 1)
        act.wait_ge(max_s, 2)
        act.activation(s_win[0:64, :], s_win[0:64, :], ACT.Exp, bias=st_s[0:64, 1:2], accum_out=st_s[0:64, 4:5])\
           .then_inc(exp_s, 1)
        act.wait_ge(max_s, 3)
        act.activation(s_slc[0:64, :], s_slc[0:64, :], ACT.Exp, bias=st_s[0:64, 2:3], accum_out=st_s[0:64, 5:6])\
           .then_inc(exp_s, 1)
        act.wait_ge(p_turned, 1)
        act.activation(pT_slc, pb(7).rearrange("p (c n) -> p c n", c=8), ACT.Copy).then_inc(pT_taken, 1)

    def stage3_vector(dve, chain):
        link = chain.link
        dve.tensor_copy(q_s2[0:NB].rearrange("p r g d -> p g r d"), q_s.rearrange("p (g r d) -> p g r d", g=NG, r=NR))\
           .then_inc(q_sorted, 1)
        link(dve.memset(q_bd, 0.0))
        dve.wait_ge(prep_turned, 1)
        t4 = pb(0)[:, 0:32].rearrange("p (r s) -> p s r", r=NR)
        for g in range(NG):
            dve.tensor_copy(q_bd[DH * g:DH * g + DH, :, NR * g:NR * g + NR], t4[DH * g:DH * g + DH])
        dve.tensor_copy(qTs[0:DH], pb(0)[0:DH, 32:96].rearrange("p (h s) -> p s h", h=NH))
        dve.tensor_copy(knT, pb(0)[:, 96:112].rearrange("p (b s) -> p b s", b=2))
        dve.wait_ge(table_ready, 128)
        link(dve.tensor_tensor(gate_rows[0:64, :], pb(1)[0:64, 0:24], head_pick[0:64, :], ALU.mult))
        dve.tensor_reduce(gates_s[0:64, :], gate_rows[0:64, :].rearrange("p (h c) -> p c h", c=3), AX, ALU.add)\
           .then_inc(prep_taken, 1)
        dve.wait_ge(cmp_scored, 1)
        dve.tensor_copy(scT[0:CMP_N, :], pb(1)[0:CMP_N, 64:128]).then_inc(cmp_cols, 1)

        def take_keys(n):
            s, j = n // 3, n % 3
            dve.wait_ge(k_tiles_turned, n + 1)
            if s >= 2:
                dve.wait_ge(seq_scored, s - 1)
            dve.tensor_copy(kTs[:, s % 2, 512 * j:512 * j + 512], pb(4 + n % 4)).then_inc(k_even, 1)

        def cmp_probs():
            dve.wait_ge(cmp_turned, 1)
            link(dve.tensor_tensor(s_cmp[0:64, :], pb(1)[0:64, 128:128 + CMP_N], t_cmp[0:64, :], ALU.add))
            dve.tensor_reduce(st_s[0:64, 0:1], s_cmp[0:64, :], AX, ALU.max, negate=True).then_inc(max_s, 1)
            dve.wait_ge(exp_s, 1)
            link(dve.reciprocal(st_s[0:64, 6:7], st_s[0:64, 3:4]))
            dve.tensor_scalar(s_cmp[0:64, :], s_cmp[0:64, :], st_s[0:64, 6:7], None, ALU.mult).then_inc(pc_ready, 1)

        def select():
            link(dve.memset(imp_pad[0:64, :], 0.0))
            link(dve.memset(imp_s[0:64, :], 0.0))
            dve.wait_ge(imp_summed, 1)
            link(dve.tensor_copy(imp_pad[0:64, 1:1 + CMP_N], pb(1)[0:64, 192:192 + CMP_N]))
            link(dve.tensor_reduce(imp_s[0:64, 0:NBLK], block_windows(imp_pad[0:64, :]), AX, ALU.add))
            link(dve.tensor_tensor(imp_s[0:64, :], imp_s[0:64, :], imp_add_s[0:64, :], ALU.add))
            link(dve.max(top_s[0:64, :], imp_s[0:64, :]))
            link(dve.match_replace(out=imp_hit[0:64, :], in_to_replace=top_s[0:64, :], in_values=imp_s[0:64, :],
                                   imm_value=PICKED))
            link(dve.tensor_scalar(sel_s[0:64, :], imp_hit[0:64, :], 2e38, NEG, ALU.is_lt, ALU.mult))
            dve.tensor_scalar(s_cmp[0:64, :], s_cmp[0:64, :], gates_s[0:64, 0:1], None, ALU.mult).then_inc(ps_ready, 1)

        for n in range(0, 3 * NB, 2):
            take_keys(n)
            if n == 2:
                cmp_probs()
            if n == 8:
                select()
        dve.wait_ge(seq_scored, NB)
        dve.tensor_copy(sT_sb[:, 8:12, :], pb(3)[:, 0:256].rearrange("p (c n) -> p c n", c=4)).then_inc(cols_taken, 1)
        dve.wait_ge(seq_scored, NB + 1)
        for br in range(2):
            link(dve.tensor_tensor(p_new[0:64, br, :], pb(1)[0:64, 256 + 8 * br:264 + 8 * br], rows_seq[0:64, :], ALU.mult))
        link(dve.tensor_reduce(s_slc[0:64, PAST:PAST + 1], p_new[0:64, 0, :], AX, ALU.add))
        link(dve.tensor_reduce(s_win[0:64, 512:513], p_new[0:64, 1, :], AX, ALU.add))
        dve.wait_ge(rows_turned, 1)
        link(dve.tensor_tensor(s_win[0:64, 0:512], pb(6)[0:64, :], t_win[0:64, 0:512], ALU.add))
        dve.tensor_reduce(st_s[0:64, 1:2], s_win[0:64, :], AX, ALU.max, negate=True).then_inc(max_s, 1)
        link(dve.tensor_tensor(s_slc[0:64, 0:PAST], bank[2][0:64, :], t_slc[0:64, 0:PAST], ALU.add))
        blocks = s_slc[0:64, 0:PAST].rearrange("p (j n) -> p j n", j=NBLK)
        link(dve.tensor_tensor(blocks, blocks, sel_s[0:64, 0:NBLK, None].to_broadcast([64, NBLK, SEL]), ALU.add))
        dve.tensor_reduce(st_s[0:64, 2:3], s_slc[0:64, :], AX, ALU.max, negate=True).then_inc(max_s, 1)
        for br, s in ((1, s_win), (0, s_slc)):
            dve.wait_ge(exp_s, 3 - br)
            w = st_s[0:64, 8 + br:9 + br]
            link(dve.reciprocal(w, st_s[0:64, 5 - br:6 - br]))
            link(dve.tensor_tensor(w, w, gates_s[0:64, 1 + br:2 + br], ALU.mult))
            last = s.shape[1] - 1
            link(dve.tensor_scalar(s[0:64, :], s[0:64, :], w, None, ALU.mult))
            dve.tensor_scalar(p_new[0:64, br, :], rows_seq[0:64, :], s[0:64, last:last + 1], None, ALU.mult)\
               .then_inc(ps_ready, 1)
        dve.wait_ge(p_turned, 1)
        dve.tensor_copy(pT_win, pb(6)[:, 0:256].rearrange("p (c n) -> p c n", c=4)).then_inc(pT_taken, 1)
        dve.tensor_copy(pnT[0:NB], pb(1)[0:NB, 300:428].rearrange("p (b n) -> p b n", b=2)).then_inc(pT_taken, 1)
        dve.tensor_copy(pcT_s[0:CMP_N, :], pb(1)[0:CMP_N, 432:496]).then_inc(pT_taken, 1)
        dve.wait_ge(seq_valued, NB)
        dve.tensor_copy(oT_s, pb(0)[:, 0:64]).then_inc(oT_taken, 1)
        dve.wait_ge(o_turned, 1)
        dve.tensor_copy(ob_s[:, 0:256], pb(7)[0:NB, 0:256]).then_inc(ob_s_ready, 1)
        dve.tensor_copy(ob_s[:, 256:512], pb(6)[0:NB, 256:512]).then_inc(ob_s_ready, 1)

    def block_windows(padded):
        a = padded[:, 0:80] if padded.shape[1] >= 80 else padded
        return bass.AP(tensor=a.tensor, offset=a.offset, ap=[a.ap[0], [4, NBLK], [1, 5]])

    wo = at(0, [KD, D])
    p_buf = [at(8192, [D]), at(9216, [D])]
    pT_buf = [at(10240, [512]), at(10752, [512]), samp[:, 0:512], samp[:, 512:1024]]
    qT = at(11264, [2, NG, 512])
    tmp = at(13312, [512])
    ob = at(0, [512], regC)
    obT = at(512, [4, P], regC)
    pc = at(1024, [NH, 64], regC)
    h2 = at(1536, [D], regC)
    imp_pad2 = at(2560, [NG, 65], regC)
    imp2 = at(2690, [NG, NBLK], regC)
    imp_hit2 = at(2722, [NG, NBLK], regC)
    top2 = at(2754, [NG, 8], regC)
    sel2 = samp[:, 1024:1216].rearrange("p (g n) -> p g n", g=NG)
    ssb, rb = small[:, 36:45], small[:, 45:54]
    ssh, rh = small[:, 54:63], small[:, 63:72]
    ssf, rf = small[:, 72:81], small[:, 81:90]
    neg_max = small[:, 90:94]
    nm_c, sum_c = small[:, 96:104], small[:, 104:112]
    row_sum = {"w": small[:, 112:120], "s": small[:, 120:128]}
    weight = small[:, 128:136]

    def key_tiles(i, kind):
        return list(range(max(0, i - 4), i + 1)) if kind == "w" else list(range(i + 1))

    units = [(i, kind, h) for i in range(NT) for kind, h in
             [("w", h) for h in range(NH)] + [("c", 0)] + [("s", h) for h in range(NH)]]
    NU = 2 * NH + 1
    events = [("QT", 0), ("CS", 0)]
    before = {}
    for i in range(NT):
        tail = NT if i == 0 else i - 1
        for place, name in ((3, "OBQ"), (4, "OBN"), (5, "OBT"), (6, "WO"), (8, "H2N"), (10, "H2T")):
            before.setdefault(NU * i + place, []).append((name, tail))
        if i >= 4:
            before.setdefault(NU * i + 9, []).append(("SELT", i))
        if i + 1 < NT:
            before.setdefault(NU * i + 11, []).append(("QT", i + 1))
            before.setdefault(NU * i + 14, []).append(("CS", i + 1))
    for u in range(len(units) + 3):
        events += before.get(u, [])
        if u < len(units) and units[u][1] != "c":
            events.append(("QK", u))
        if 0 <= u - 2 < len(units):
            events.append(("T", u - 2))
        if 0 <= u - 3 < len(units):
            events.append(("PV", u - 3))
    events += [(name, NT - 1) for name in ("OBQ", "OBN", "OBT", "WO", "H2N", "H2T")]

    s_at, p_at, pt_at, o_at = {}, {}, {}, {}
    n_pt = 0
    for e in events:
        if e[0] in ("QT", "CS", "QK", "SELT", "OBT", "WO", "H2T"):
            s_at[e] = len(s_at)
        if e[0] == "QK":
            p_at[e[1]] = len(p_at)
        if e[0] == "T":
            i, kind, h = units[e[1]]
            n = 2 if kind == "c" else -(-len(key_tiles(i, kind)) // 4)
            pt_at[e[1]] = (n_pt, n)
            n_pt += n
    for u, (i, kind, h) in enumerate(units):
        o_at[u] = 3 * i + "wcs".index(kind)
    h2T_high = rounded("h2T_high", [P, KD, TOK], "hT")
    h2T_low = [rounded("h2T_low0", [P, 4, TOK], "q_all"), rounded("h2T_low1", [P, 4, TOK], "oaT")]

    qk_by_p = {n: u for u, n in p_at.items()}

    wo_ready, qaug_ready = sem("wo_ready"), [sem("qaug_ready0"), sem("qaug_ready1")]
    s_ready = sem("s_ready")
    s_taken = [sem("s_taken0"), sem("s_taken1")]
    max_ready = sem("max_ready")
    pt_ready, pt_taken = sem("pt_ready"), [sem("pt_taken0"), sem("pt_taken1")]
    pv_done, o_free = sem("pv_done"), sem("o_free")
    cmp_exp, pc_normed = sem("cmp_exp"), sem("pc_normed")
    sel_ready = sem("sel_ready")
    ob_ready, ob_squared, ob_inv, obn_ready = sem("ob_ready"), sem("ob_squared"), sem("ob_inv"), sem("obn_ready")
    x1_squared, x1_inv, h2_ready, h2_high = sem("x1_squared"), sem("x1_inv"), sem("h2_ready"), sem("h2_high")

    def s_pair(e):
        return bank[s_at[e] % 2]

    def wait_s(eng, e):
        eng.wait_ge(s_ready, s_at[e] + 1)

    def taken(ins, e):
        ins.then_inc(s_taken[s_at[e] % 2], 1)

    def wait_taken(eng, e):
        eng.wait_ge(s_taken[s_at[e] % 2], s_at[e] // 2 + 1)

    def tail_order(t):
        return 0 if t == NT else t + 1

    def load_qaug(sp, i):
        if i >= 2:
            last = s_at[("QK", NU * (i - 2) + NU - 1)]
            sp.wait_ge(s_ready, last + 1)
        sp.dma_start(qT[64:KAUG, i % 2].rearrange("p g n -> p (g n)"), C["qaug"][i]).then_inc(qaug_ready[i % 2], 16)

    def stage4_sync(sp):
        sp.wait_ge(ob_s_ready, 2)
        load_qaug(sp, 0)
        load_qaug(sp, 1)
        sp.dma_start(norm_g[:, :], norm_rows(A["norm2_g"][0]).to_broadcast([P, D])).then_inc(wo_ready, 16)
        for k in range(2):
            sp.dma_start(wo[:, 4 * k:4 * k + 4, :], A["w_out"][0, 512 * k:512 * k + 512].rearrange("(k p) n -> p k n", p=P))\
              .then_inc(wo_ready, 16)
        for i in range(2, NT):
            load_qaug(sp, i)

    def stage4_tensor(pe):
        pe.wait_ge(ob_s_ready, 2)
        for e in events:
            name, a = e
            if e in s_at and s_at[e] >= 2:
                pe.wait_ge(s_taken[s_at[e] % 2], s_at[e] // 2)
            if name == "QT":
                for h in range(NH):
                    ins = pe.transpose(s_pair(e)[0:DH, P * h:P * h + P], q_all[:, h // 2, P * a + DH * (h % 2):P * a + DH * (h % 2) + DH], ident[:, :])
                ins.then_inc(s_ready, 1)
            elif name == "CS":
                wait_taken(pe, ("QT", a))
                pe.wait_ge(qaug_ready[a % 2], 16 * (a // 2 + 1))
                out = s_pair(e)[:, 0:512].rearrange("p (h n) -> p h n", h=NH)
                pe.matmul(out, ident_bf[:, :], mask_cmp[:, a, None, :].to_broadcast([P, NH, 64]), start=True, stop=False,
                          skip_group_check=True)
                for h in range(NH):
                    g, r = h // NR, h % NR
                    ins = pe.matmul(out[:, h, 0:CMP_N], qT[0:KAUG, a % 2, g, P * r:P * r + P], kcT_p[0:KAUG, g, 0:CMP_N],
                                    start=False, stop=(h == NH - 1), skip_group_check=True)
                ins.then_inc(s_ready, 1)
            elif name == "QK":
                i, kind, h = units[a]
                g, r = h // NR, h % NR
                tiles = key_tiles(i, kind)
                if kind == "s" and i >= 4:
                    wait_taken(pe, ("SELT", i))
                q = qT[0:KAUG, i % 2, g, P * r:P * r + P]
                for c in range(0, len(tiles), 4):
                    part = tiles[c:c + 4]
                    masks = [(x, m) for x, m in ((i, mask_diag), (i - 4 if kind == "w" else -1, mask_low)) if x in part]
                    ins = pe.matmul(s_pair(e)[:, P * c:P * (c + len(part))], q,
                                    kT[0:KAUG, 2 * (kind == "w") + g, P * part[0]:P * part[-1] + P],
                                    start=True, stop=not masks, skip_group_check=True)
                    for n, (x, m) in enumerate(masks):
                        col = P * (x - tiles[0])
                        ins = pe.matmul(s_pair(e)[:, col:col + P], ident_bf[:, :], m[:, :], start=False,
                                        stop=(n == len(masks) - 1), skip_group_check=True)
                ins.then_inc(s_ready, 1)
            elif name == "SELT":
                pe.wait_ge(sel_ready, a - 3)
                for g in range(NG):
                    ins = pe.transpose(s_pair(e)[0:96, P * g:P * g + P], sel2[:, g, :], ident[:, :])
                ins.then_inc(s_ready, 1)
            elif name == "T":
                turn_probs(pe, a)
            elif name == "PV":
                values(pe, a)
            elif name == "OBT":
                n = rows(a)
                pe.wait_ge(obn_ready, tail_order(a) + 1)
                src = ob if a < NT else ob_s[:, :]
                for k in range(4):
                    ins = pe.transpose(s_pair(e)[:, P * k:P * k + n], src[0:n, P * k:P * k + P], ident[0:n, 0:n])
                ins.then_inc(s_ready, 1)
            elif name == "WO":
                n = rows(a)
                pe.wait_ge(wo_ready, 48)
                wait_taken(pe, ("OBT", a))
                for half in range(2):
                    for k in range(KD):
                        lhs = oaT[:, k, P * a:P * a + n] if k < 4 else obT[:, k - 4, 0:n]
                        ins = pe.matmul(s_pair(e)[0:n, 512 * half:512 * half + 512], lhs, wo[:, k, 512 * half:512 * half + 512],
                                        start=(k == 0), stop=(k == KD - 1))
                ins.then_inc(s_ready, 1)
            elif name == "H2T":
                n = rows(a)
                pe.wait_ge(h2_ready, tail_order(a) + 1)
                for k in range(KD):
                    ins = pe.transpose(s_pair(e)[:, P * k:P * k + n], h2[0:n, P * k:P * k + P], ident[0:n, 0:n])
                ins.then_inc(s_ready, 1)

    def turn_probs(pe, u):
        i, kind, h = units[u]
        first, n_chunks = pt_at[u]
        if kind == "c":
            pe.wait_ge(pc_normed, i + 1)
        else:
            wait_taken(pe, ("QK", u))
        nk = len(key_tiles(i, kind)) if kind != "c" else NH
        for c in range(n_chunks):
            n = first + c
            if n >= 2:
                pe.wait_ge(pt_taken[n % 2], n // 2)
            for b in range(4 * c, min(4 * c + 4, nk)):
                col = P * (b - 4 * c)
                if kind == "c":
                    ins = pe.transpose(pb(4 + n % 2)[0:64, col:col + P], pc[:, b, :], ident[:, :])
                else:
                    ins = pe.transpose(pb(4 + n % 2)[:, col:col + P], p_buf[p_at[u] % 2][:, P * b:P * b + P], ident[:, :])
            ins.then_inc(pt_ready, 1)

    def values(pe, u):
        i, kind, h = units[u]
        first, n_chunks = pt_at[u]
        bank_o = pb(6 + o_at[u] % 2)
        if h == 0 and o_at[u] >= 2:
            pe.wait_ge(o_free, o_at[u] - 1)
        tiles = key_tiles(i, kind) if kind != "c" else list(range(NH))
        for c in range(n_chunks):
            n = first + c
            pe.wait_ge(pt_taken[n % 2], n // 2 + 1)
            for b in range(4 * c, min(4 * c + 4, len(tiles))):
                col = P * (b - 4 * c)
                if kind == "c":
                    g = b // NR
                    ins = pe.matmul(bank_o[:, DH * b:DH * b + DH], pT_buf[n % 4][0:CMP_N, col:col + P],
                                    vc_p[0:CMP_N, DH * g:DH * g + DH], start=True, stop=True, skip_group_check=True)
                else:
                    g = h // NR
                    ins = pe.matmul(bank_o[:, DH * h:DH * h + DH], pT_buf[n % 4][:, col:col + P],
                                    v_all[:, tiles[b], int(kind == "w"), DH * g:DH * g + DH],
                                    start=(b == 0), stop=(b == len(tiles) - 1), skip_group_check=True)
            ins.then_inc(pv_done, 1)

    def branch_ends(u):
        return units[u][1] == "c" or units[u][2] == NH - 1

    def take_chunks(eng, copy, u, parity):
        i, kind, h = units[u]
        first, n_chunks = pt_at[u]
        nk = len(key_tiles(i, kind)) if kind != "c" else NH
        for c in range(n_chunks):
            n = first + c
            if n % 2 != parity:
                continue
            w = P * min(4, nk - 4 * c)
            r = CMP_N if kind == "c" else P
            eng.wait_ge(pt_ready, n + 1)
            if n >= 4:
                eng.wait_ge(pv_done, n - 3)
            copy(pT_buf[n % 4][0:r, 0:w], pb(4 + n % 2)[0:r, 0:w]).then_inc(pt_taken[n % 2], 1)

    def stage4_scalar(act):
        def copy(dst, src):
            return act.activation(dst, src, ACT.Copy)

        for e in events:
            name, a = e
            if name == "CS":
                wait_taken(act, e)
                act.activation(pc, pc, ACT.Exp).then_inc(cmp_exp, 1)
            elif name == "QK":
                i, kind, h = units[a]
                w = P * len(key_tiles(i, kind))
                n = p_at[a]
                act.wait_ge(max_ready, n + 1)
                if n >= 2:
                    first, n_chunks = pt_at[qk_by_p[n - 2]]
                    act.wait_ge(pt_ready, first + n_chunks)
                taken(act.activation(p_buf[n % 2][:, 0:w], s_pair(e)[:, 0:w], ACT.Exp, bias=neg_max[:, n % 4:n % 4 + 1],
                                     accum_out=row_sum[kind][:, h:h + 1]), e)
            elif name == "T":
                take_chunks(act, copy, a, 1)
            elif name == "OBQ":
                n, k = rows(a), tail_order(a)
                act.wait_ge(ob_ready, k) if k else act.wait_ge(ob_s_ready, 2)
                if k:
                    wait_s(act, ("H2T", NT if k == 1 else a - 1))
                src = ob if a < NT else ob_s[:, :]
                act.activation(h2[0:n, 0:512], src[0:n, :], ACT.Square, accum_out=ssb[0:n, a:a + 1]).then_inc(ob_squared, 1)
            elif name == "WO":
                n, k = rows(a), tail_order(a)
                wait_taken(act, e)
                act.wait_ge(ob_squared, k + 1)
                act.activation(h2[0:n, :], x_all[0:n, a, :], ACT.Square, accum_out=ssh[0:n, a:a + 1]).then_inc(x1_squared, 1)
            elif name == "H2T":
                n = rows(a)
                wait_s(act, e)
                act.activation(h2T_high[:, :, P * a:P * a + n],
                               s_pair(e)[:, :].rearrange("p (k n) -> p k n", k=KD)[:, :, 0:n], ACT.Copy).then_inc(h2_high, 1)

    def stage4_pool(pool, chain):
        for e in events:
            name, a = e
            n = rows(a) if name in ("OBQ", "WO") else 0
            if name == "OBQ":
                pool.wait_ge(ob_squared, tail_order(a) + 1)
                inv_rms(pool, chain.link, ssb[0:n, a:a + 1], rb[0:n, a:a + 1], 512).then_inc(ob_inv, 1)
            elif name == "WO":
                pool.wait_ge(x1_squared, tail_order(a) + 1)
                inv_rms(pool, chain.link, ssh[0:n, a:a + 1], rh[0:n, a:a + 1], D).then_inc(x1_inv, 1)

    def stage4_vector(dve, chain):
        link = chain.link

        def cmp_softmax(e, i):
            wait_s(dve, e)
            s = s_pair(e)[:, 0:512].rearrange("p (h n) -> p h n", h=NH)
            link(dve.tensor_reduce(nm_c, s, AX, ALU.max, negate=True))
            link(dve.tensor_scalar(nm_c, nm_c, -NEG / 10, None, ALU.min))
            if i:
                first, n_chunks = pt_at[NU * (i - 1) + NH]
                dve.wait_ge(pt_ready, first + n_chunks)
            taken(dve.tensor_tensor(pc, s, nm_c[:, :, None].to_broadcast([P, NH, 64]), ALU.add), e)
            dve.wait_ge(cmp_exp, i + 1)
            link(dve.tensor_reduce(sum_c, pc, AX, ALU.add))
            link(dve.tensor_scalar(sum_c, sum_c, 1e-30, None, ALU.max))
            link(dve.reciprocal(sum_c, sum_c))
            dve.tensor_tensor(pc, pc, sum_c[:, :, None].to_broadcast([P, NH, 64]), ALU.mult).then_inc(pc_normed, 1)
            if i >= 4:
                dve.wait_ge(pc_normed, i + 1)
                pc_g = pc.rearrange("p (g r) n -> p g n r", g=NG)
                for g in range(NG):
                    link(dve.tensor_reduce(imp_pad2[:, g, 1:65], pc_g[:, g], AX, ALU.add))
                for g in range(NG):
                    link(dve.tensor_reduce(imp2[:, g, :], block_windows(imp_pad2[:, g, :]), AX, ALU.add))
                link(dve.tensor_tensor(imp2, imp2, imp_add[:, i, None, :].to_broadcast([P, NG, NBLK]), ALU.add))
                for g in range(NG):
                    link(dve.max(top2[:, g, :], imp2[:, g, :]))
                for g in range(NG):
                    link(dve.match_replace(out=imp_hit2[:, g, :], in_to_replace=top2[:, g, :], in_values=imp2[:, g, :],
                                           imm_value=PICKED))
                dve.tensor_scalar(sel2[:, :, 64:80], imp_hit2, 2e38, NEG, ALU.is_lt, ALU.mult).then_inc(sel_ready, 1)

        def add_branch(u):
            i, kind, h = units[u]
            n = o_at[u]
            gate_h = gate[:, i, :].rearrange("p (h c) -> p c h", c=3)
            if kind == "c":
                w = gate_h[:, 0, :]
            else:
                w = weight
                link(dve.reciprocal(weight, row_sum[kind]))
                link(dve.tensor_tensor(weight, weight, gate_h[:, 1 if kind == "s" else 2, :], ALU.mult))
            dve.wait_ge(pv_done, sum(pt_at[u]))
            first = kind == "w"
            dst = (ob if first else tmp).rearrange("p (h d) -> p h d", h=NH)
            if first and i:
                dve.wait_ge(s_ready, s_at[("OBT", i - 1)] + 1)
            dve.tensor_tensor(dst, pb(6 + n % 2).rearrange("p (h d) -> p h d", h=NH), w[:, :, None].to_broadcast([P, NH, DH]),
                              ALU.mult).then_inc(o_free, 1)
            dve.wait_ge(o_free, n + 1)
            if not first:
                ins = dve.tensor_tensor(ob, ob, tmp, ALU.add)
                if kind == "s":
                    ins.then_inc(ob_ready, 1)
                else:
                    link(ins)

        link(dve.memset(samp[:, 1024:1216], 0.0))
        link(dve.memset(regC[:, 2560:2690], 0.0))
        for e in events:
            name, a = e
            if name == "QT":
                wait_s(dve, e)
                taken(dve.tensor_copy(qT[0:DH, a % 2].rearrange("p g n -> p (g n)"), s_pair(e)[0:DH, :]), e)
            elif name == "CS":
                cmp_softmax(e, a)
            elif name == "QK":
                i, kind, h = units[a]
                w = P * len(key_tiles(i, kind))
                wait_s(dve, e)
                n = p_at[a]
                dve.tensor_reduce(neg_max[:, n % 4:n % 4 + 1], s_pair(e)[:, 0:w], AX, ALU.max, negate=True)\
                   .then_inc(max_ready, 1)
            elif name == "SELT":
                wait_s(dve, e)
                dve.wait_ge(qaug_ready[a % 2], 16 * (a // 2 + 1))
                for g in range(NG):
                    rows_q = qT[64:96, a % 2, g].rearrange("p (r n) -> p r n", r=NR)
                    ins = dve.tensor_tensor(rows_q, rows_q, s_pair(e)[64:96, None, P * g:P * g + P].to_broadcast([32, NR, P]),
                                            ALU.add)
                taken(ins, e)
            elif name == "T":
                take_chunks(dve, dve.tensor_copy, a, 0)
            elif name == "PV" and branch_ends(a):
                add_branch(a)
            elif name == "OBN":
                n, k = rows(a), tail_order(a)
                src = ob if a < NT else ob_s[:, :]
                dve.wait_ge(ob_inv, k + 1)
                dve.scalar_tensor_tensor(out=src[0:n, :], in0=src[0:n, :], scalar=rb[0:n, a:a + 1], in1=normb_g[0:n, :],
                                         op0=ALU.mult, op1=ALU.mult).then_inc(obn_ready, 1)
            elif name == "OBT":
                n, k = rows(a), tail_order(a)
                wait_s(dve, e)
                taken(dve.tensor_copy(obT[:, :, 0:n], s_pair(e)[:, 0:512].rearrange("p (k n) -> p k n", k=4)[:, :, 0:n]), e)
            elif name == "WO":
                n, k = rows(a), tail_order(a)
                wait_s(dve, e)
                taken(dve.tensor_tensor(x_all[0:n, a, :], x_all[0:n, a, :], s_pair(e)[0:n, :], ALU.add), e)
            elif name == "H2N":
                n, k = rows(a), tail_order(a)
                dve.wait_ge(x1_inv, k + 1)
                dve.wait_ge(wo_ready, 48)
                dve.scalar_tensor_tensor(out=h2[0:n, :], in0=x_all[0:n, a, :], scalar=rh[0:n, a:a + 1], in1=norm_g[0:n, :],
                                         op0=ALU.mult, op1=ALU.mult).then_inc(h2_ready, 1)
            elif name == "H2T":
                n = rows(a)
                dve.wait_ge(h2_high, tail_order(a) + 1)
                for half in range(2):
                    ins = dve.tensor_tensor(h2T_low[half][:, :, P * a:P * a + n],
                                            s_pair(e)[:, 512 * half:512 * half + 512].rearrange("p (k n) -> p k n", k=4)[:, :, 0:n],
                                            h2T_high[:, 4 * half:4 * half + 4, P * a:P * a + n].bitcast(F32), ALU.subtract)
                taken(ins, e)

    FG = P
    NJ = FF // FG
    TCH = TOK // 3
    w_low_at, w_high_at = [[8192, 9216, 10240], [1024, 2048, 3072]], [[11264, 12288, 0], [4096, 5120, 6144]]
    w_raw = [[at(w_low_at[i][x], [KD, FG]) for x in range(2)] + [at(w_low_at[i][2], [1, D])] for i in range(2)]
    w_low, w_high = ([[rounded(f"{part}{i}_{x}", [P, KD, FG] if x < 2 else [P, 1, D], "arena", word[i][x])[:, :, :]
                       for x in range(3)] for i in range(2)]
                     for part, word in (("w_low", w_low_at), ("w_high", w_high_at)))
    act_raw = [at(TOK * i, [TOK], kT_space) for i in (0, 1)]
    act_low = [rounded(f"act_low{i}", [P, TOK], "kT_space", TOK * i) for i in (0, 1)]
    act_high = [rounded("act_high0", [P, TOK], "kT_space", 2 * TOK), rounded("act_high1", [P, TOK], "v_all")]
    y_out = [at(D * i, [D], regC) for i in range(2)]
    sq_y = at(7168, [D])

    gu_loaded = [sem("gu_loaded0"), sem("gu_loaded1")]
    wd_loaded = [sem("wd_loaded0"), sem("wd_loaded1")]
    gu_high, gu_low, wd_high, wd_low = sem("gu_high"), sem("gu_low"), sem("wd_high"), sem("wd_low")
    gu_ready, silu_ready, act_ready = sem("gu_ready"), sem("silu_ready"), sem("act_ready")
    act_high_ready, act_low_ready = sem("act_high_ready"), sem("act_low_ready")
    y_ready, y_added = sem("y_ready"), sem("y_added")
    final_g_ready, y_squared, y_inv, y_normed = sem("final_g_ready"), sem("y_squared"), sem("y_inv"), sem("y_normed")
    y_stored = [sem("y_stored0"), sem("y_stored1")]

    def load_gate_up(sp, j, s, first):
        if not first:
            sp.wait_ge(gu_ready, j * 3 - 3)
        for x, name in enumerate(("w_gate", "w_up")):
            sp.dma_start(w_raw[s][x], A[name][0].rearrange("(k p) f -> p k f", p=P)[:, :, bass.ds(j * FG, FG)])\
              .then_inc(gu_loaded[s], 16)

    def load_down(sp, j, s, first):
        if not first:
            sp.wait_ge(y_ready, j * XT - XT)
        sp.dma_start(w_raw[s][2], A["w_down"][0].rearrange("(f p) n -> p f n", p=P)[:, bass.ds(j, 1), :])\
          .then_inc(wd_loaded[s], 16)

    def stage5_sync(sp):
        first, n_chunks = pt_at[len(units) - 1]
        sp.wait_ge(pt_ready, first + n_chunks)
        load_gate_up(sp, 0, 0, True)
        sp.wait_ge(pv_done, first + n_chunks)
        load_down(sp, 0, 0, True)
        sp.wait_ge(s_ready, s_at[("WO", NT - 1)] + 1)
        load_gate_up(sp, 1, 1, True)
        load_down(sp, 1, 1, True)
        sp.wait_ge(h2_ready, XT)
        sp.dma_start(norm_g[:, :], norm_rows(A["final_norm_g"]).to_broadcast([P, D])).then_inc(final_g_ready, 16)
        with sp.Fori(0, (NJ - 2) // 2) as i:
            for s in range(2):
                load_gate_up(sp, i * 2 + (2 + s), s, False)
                load_down(sp, i * 2 + (2 + s), s, False)
        for t in range(XT):
            sp.wait_ge(y_normed, t + 1)
            dst = O["y_prompt"][0, P * t:P * t + P] if t < NT else O["y_sample"][:, 0, :]
            sp.dma_start(dst, y_out[t % 2][0:rows(t), :]).then_inc(y_stored[t % 2], 16)

    def stage5_tensor(pe):
        def gate_up(j, s, first):
            pe.wait_ge(gu_high, j * 2 + 2)
            pe.wait_ge(gu_low, j * 2 + 2)
            for c in range(3):
                if not (first and j == 0 and c < 2):
                    pe.wait_ge(act_ready, j * 3 + (c - 1))
                cols = slice(TCH * c, TCH * c + TCH)
                for x in range(2):
                    out = pb(2 * x + (s + c) % 2)[:, 0:TCH]
                    for k in range(KD):
                        high, low = h2T_high[:, k, cols], h2T_low[k // 4][:, k % 4, cols]
                        wh, wl = w_high[s][x][:, k, :], w_low[s][x][:, k, :]
                        pe.matmul(out, wh, high, start=(k == 0), stop=False)
                        pe.matmul(out, wh, low, start=False, stop=False)
                        ins = pe.matmul(out, wl, high, start=False, stop=(k == KD - 1))
                ins.then_inc(gu_ready, 1)

        def down(j, s, first):
            pe.wait_ge(act_high_ready, j * 3 + 3)
            pe.wait_ge(act_low_ready, j * 3 + 3)
            pe.wait_ge(wd_high, j + 1)
            pe.wait_ge(wd_low, j + 1)
            for t in range(XT):
                n = rows(t)
                if not (first and j == 0 and t < 2):
                    pe.wait_ge(y_added, j * XT + (t - 1))
                ah, al = (a[s][:, P * t:P * t + n] for a in (act_high, act_low))
                for half in range(2):
                    cols = slice(512 * half, 512 * half + 512)
                    out = bank[2 + (s + t) % 2][0:n, cols]
                    wh, wl = w_high[s][2][:, 0, cols], w_low[s][2][:, 0, cols]
                    pe.matmul(out, ah, wh, start=True, stop=False)
                    pe.matmul(out, ah, wl, start=False, stop=False)
                    ins = pe.matmul(out, al, wh, start=False, stop=True)
                ins.then_inc(y_ready, 1)

        wait_taken(pe, ("H2T", NT - 1))
        wait_taken(pe, ("WO", NT - 1))
        gate_up(0, 0, True)
        gate_up(1, 1, True)
        down(0, 0, True)
        with pe.Fori(0, (NJ - 2) // 2) as i:
            gate_up(i * 2 + 2, 0, False)
            down(i * 2 + 1, 1, False)
            gate_up(i * 2 + 3, 1, False)
            down(i * 2 + 2, 0, False)
        down(NJ - 1, 1, False)

    def stage5_scalar(act):
        def round_gate_up(j, s):
            act.wait_ge(gu_loaded[s], (j - s) * 16 + 32)
            for x in range(2):
                act.activation(w_high[s][x], w_raw[s][x], ACT.Copy).then_inc(gu_high, 1)

        def round_down(j, s):
            act.wait_ge(wd_loaded[s], (j - s) * 8 + 16)
            act.activation(w_high[s][2], w_raw[s][2], ACT.Copy).then_inc(wd_high, 1)

        def silu(j, s, first):
            if not first:
                act.wait_ge(y_ready, j * XT - XT)
            for c in range(4):
                if c < 3:
                    act.wait_ge(gu_ready, j * 3 + (c + 1))
                    act.activation(act_raw[s][:, TCH * c:TCH * c + TCH], pb((s + c) % 2)[:, 0:TCH], ACT.Silu)\
                       .then_inc(silu_ready, 1)
                if c >= 1:
                    cols = slice(TCH * (c - 1), TCH * c)
                    act.wait_ge(act_ready, j * 3 + c)
                    act.activation(act_high[s][:, cols], act_raw[s][:, cols], ACT.Copy).then_inc(act_high_ready, 1)

        def step(j, s, first=False, last=False):
            silu(j, s, first)
            if not last:
                round_gate_up(j + 1, 1 - s)
            round_down(j, s)

        wait_s(act, ("H2T", NT - 1))
        round_gate_up(0, 0)
        step(0, 0, first=True)
        step(1, 1, first=True)
        with act.Fori(0, (NJ - 4) // 2) as i:
            step(i * 2 + 2, 0)
            step(i * 2 + 3, 1)
        step(NJ - 2, 0)
        step(NJ - 1, 1, last=True)
        for t in range(XT):
            n = rows(t)
            act.wait_ge(y_added, (NJ - 1) * XT + t + 1)
            if t:
                act.wait_ge(y_squared, t)
            act.activation(sq_y[0:n, :], x_all[0:n, t, :], ACT.Square, accum_out=ssf[0:n, t:t + 1]).then_inc(y_squared, 1)

    def stage5_pool(pool, chain):
        def low_gate_up(j, s):
            for x in range(2):
                pool.wait_ge(gu_high, j * 2 + (x + 1))
                pool.tensor_tensor(w_low[s][x], w_raw[s][x], w_high[s][x].bitcast(F32), ALU.subtract).then_inc(gu_low, 1)

        def low_down(j, s):
            pool.wait_ge(wd_high, j + 1)
            pool.tensor_tensor(w_low[s][2], w_raw[s][2], w_high[s][2].bitcast(F32), ALU.subtract).then_inc(wd_low, 1)

        low_gate_up(0, 0)
        with pool.Fori(0, (NJ - 2) // 2) as i:
            for s in range(2):
                low_gate_up(i * 2 + (1 + s), 1 - s)
                low_down(i * 2 + s, s)
        low_gate_up(NJ - 1, 1)
        low_down(NJ - 2, 0)
        low_down(NJ - 1, 1)
        for t in range(XT):
            n = rows(t)
            pool.wait_ge(y_squared, t + 1)
            inv_rms(pool, chain.link, ssf[0:n, t:t + 1], rf[0:n, t:t + 1], D).then_inc(y_inv, 1)

    def stage5_vector(dve, chain):
        def gate_mul(j, s):
            for c in range(4):
                if c < 3:
                    a = act_raw[s][:, TCH * c:TCH * c + TCH]
                    dve.wait_ge(silu_ready, j * 3 + (c + 1))
                    dve.tensor_tensor(a, a, pb(2 + (s + c) % 2)[:, 0:TCH], ALU.mult).then_inc(act_ready, 1)
                if c >= 1:
                    cols = slice(TCH * (c - 1), TCH * c)
                    dve.wait_ge(act_high_ready, j * 3 + c)
                    dve.tensor_tensor(act_low[s][:, cols], act_raw[s][:, cols], act_high[s][:, cols].bitcast(F32), ALU.subtract)\
                       .then_inc(act_low_ready, 1)

        def add_tile(j, s, t, first):
            n = rows(t)
            dve.wait_ge(y_ready, j * XT + (t + 1))
            if not first:
                dve.wait_ge(y_added, j * XT + (t + 1 - XT))
            dve.tensor_tensor(x_all[0:n, t, :], x_all[0:n, t, :], bank[2 + (s + t) % 2][0:n, :], ALU.add).then_inc(y_added, 1)

        def add(j, s, first=False):
            for t in range(XT):
                add_tile(j, s, t, first)

        def final_norm(t):
            n = rows(t)
            dve.wait_ge(y_inv, t + 1)
            if t >= 2:
                dve.wait_ge(y_stored[t % 2], 16 * (t // 2))
            dve.scalar_tensor_tensor(out=y_out[t % 2][0:n, :], in0=x_all[0:n, t, :], scalar=rf[0:n, t:t + 1],
                                     in1=norm_g[0:n, :], op0=ALU.mult, op1=ALU.mult).then_inc(y_normed, 1)

        gate_mul(0, 0)
        gate_mul(1, 1)
        add(0, 0, True)
        with dve.Fori(0, (NJ - 2) // 2) as i:
            gate_mul(i * 2 + 2, 0)
            add(i * 2 + 1, 1)
            gate_mul(i * 2 + 3, 1)
            add(i * 2 + 2, 0)
        dve.wait_ge(final_g_ready, 16)
        for t in range(XT + 1):
            if t < XT:
                add_tile(NJ - 1, 1, t, False)
            if t >= 1:
                final_norm(t - 1)

    block = ctx.enter_context(nc.Block())

    @block.sync
    def _(sp):
        stage1_sync(sp)
        stage2_sync(sp)
        stage3_sync(sp)
        stage4_sync(sp)
        stage5_sync(sp)
        for slot in range(2):
            sp.wait_ge(kv_stored[slot], stores_before(2 * NT + slot))
        sp.wait_ge(new_stored, 48)
        sp.wait_ge(gv_stored, 32)
        sp.wait_ge(win_copied, 16)
        sp.wait_ge(y_stored[0], 16 * 5)
        sp.wait_ge(y_stored[1], 16 * 4)

    @block.gpsimd
    def _(pool):
        chain = stage1_pool(pool)
        stage2_pool(pool)
        stage3_pool(pool)
        stage4_pool(pool, chain)
        stage5_pool(pool, chain)

    @block.tensor
    def _(pe):
        stage1_tensor(pe)
        stage2_tensor(pe)
        stage3_tensor(pe)
        stage4_tensor(pe)
        stage5_tensor(pe)

    @block.scalar
    def _(act):
        stage1_scalar(act)
        stage2_scalar(act)
        stage3_scalar(act)
        stage4_scalar(act)
        stage5_scalar(act)

    @block.vector
    def _(dve):
        chain = stage1_vector(dve)
        stage2_vector(dve, chain)
        stage3_vector(dve, chain)
        stage4_vector(dve, chain)
        stage5_vector(dve, chain)

    ctx.close()


def kernel(**inputs):
    import concourse.bacc as bacc
    from concourse.bass_utils import run_bass_kernel_spmd

    nc = bacc.Bacc("TRN2", target_bir_lowering=False, num_devices=1)
    arrays, A, C, O = {}, {}, {}, {}
    for name in RAW_INPUTS:
        a = np.ascontiguousarray(inputs[name])
        arrays["in_" + name] = a
        A[name] = nc.dram_tensor("in_" + name, a.shape, mybir.dt.from_np(a.dtype), kind="ExternalInput").ap()
    for name, a in constants().items():
        arrays["const_" + name] = a
        C[name] = nc.dram_tensor("const_" + name, a.shape, mybir.dt.from_np(a.dtype), kind="ExternalInput").ap()
    for name, shape in OUTPUTS:
        O[name] = nc.dram_tensor("out_" + name, shape, F32, kind="ExternalOutput").ap()
    build_program(nc, A, C, O)
    r = run_bass_kernel_spmd(nc, [arrays], core_ids=[0])
    return tuple(r.results[0]["out_" + name] for name, _ in OUTPUTS)
```

```python
from contextlib import ExitStack

import numpy as np
import concourse.bass as bass
from concourse import mybir

F32 = mybir.dt.float32
F32R = mybir.dt.float32r
BF16 = mybir.dt.bfloat16
I32 = mybir.dt.int32
ACT = mybir.ActivationFunctionType
ALU = mybir.AluOpType
AX = mybir.AxisListType.X

P = 128
D = 1024
KD = D // P
SEQ = 1024
NT = SEQ // P
NB = 8
PAST = 1024
PAGES = 8
DH = 64
GH = 8
NH = 8
NG = 2
NR = 4
FF = 2816
CMP_N = 63
NBLK = 16
SEL = 64
EPS = 1e-6
NEG = -1e30
FORCED = 1e30
PICKED = 3e38
XT = NT + 1
TOK = SEQ + NB
KAUG = 97


def rows(t):
    return P if t < NT else NB


def constants():
    bf = mybir.dt.np(BF16)
    f = np.float32
    slope = 2.0 ** -np.arange(1, NH + 1)
    t = np.arange(SEQ)
    q, k = np.arange(P)[:, None], np.arange(P)[None, :]
    c = {}
    c["ident"] = np.eye(P, dtype=f)
    c["ident_bf"] = np.eye(P).astype(bf)
    c["upper01"] = (q <= k).astype(f)
    c["mask_diag"] = np.where(k <= q, 0, NEG).astype(bf)
    c["mask_low"] = np.where(k > q, 0, NEG).astype(bf)
    end = 16 * np.arange(64) + 31
    cm = np.where((end[None, :] <= t[:, None]) & (np.arange(64) < CMP_N)[None, :], 0, NEG)
    c["mask_cmp"] = np.ascontiguousarray(cm.reshape(NT, P, 64).transpose(1, 0, 2)).astype(bf)

    def kaug(pos, second):
        a = np.zeros((33, len(pos)), f)
        a[16 * second + pos // SEL, np.arange(len(pos))] = 1
        a[32] = pos % SEL
        return a
    c["kaug"] = np.stack([kaug(t, 0), kaug(t, 0), kaug(t, 1), kaug(t, 1)], 1)
    c["kaug_cmp"] = np.stack([kaug(np.minimum(end, SEQ - 1), 1)] * 2, 1)
    qa = np.zeros((NT, 33, NG, NR, P), f)
    for i in range(NT):
        for g in range(NG):
            for r in range(NR):
                s = slope[g * NR + r]
                blk = s * (SEL * np.arange(NBLK) - P * i)
                qa[i, 0:16, g, r] = blk[:, None]
                qa[i, 16:32, g, r] = blk[:, None]
                qa[i, 32, g, r] = s
    c["qaug"] = qa.reshape(NT, 33, NH * P)
    j = np.arange(NBLK)[None, :]
    cur = (t // SEL)[:, None]
    forced = (j == 0) | ((j <= cur) & (j > cur - 2))
    add = np.where(j * SEL <= t[:, None], np.where(forced, FORCED, 0.0), NEG)
    c["imp_add"] = np.ascontiguousarray(add.reshape(NT, P, NBLK).transpose(1, 0, 2)).astype(f)
    row = np.arange(NB * NH)
    sl = slope[row % NH][:, None]
    c["same_group"] = ((row[:, None] // NR) == (row[None, :] // NR)).astype(f)
    c["seq_rows"] = (np.arange(NB)[:, None] == row[None, :] // NH).astype(f)
    c["rows_seq"] = np.ascontiguousarray(c["seq_rows"].T)
    c["head_pick"] = np.repeat((np.arange(NH)[None, :] == (row % NH)[:, None]), 3, 1).astype(f)
    c["t_slc"] = (-sl * (PAST - np.arange(PAST + 1))[None, :]).astype(f)
    w = np.arange(512).reshape(P, 4).T.reshape(-1)
    dist = 512 - w
    tw = np.where(dist[None, :] < 512, -sl * dist[None, :], NEG)
    c["t_win"] = np.concatenate([tw, np.zeros((64, 1))], 1).astype(f)
    c["t_cmp"] = (-sl * (PAST - end[None, :CMP_N])).astype(f)
    c["imp_add_s"] = np.broadcast_to(np.where(np.isin(np.arange(17), (0, 15, 16)), FORCED, 0.0), (64, 17)).astype(f)
    return {k_: np.ascontiguousarray(v) for k_, v in c.items()}


RAW_INPUTS = ["x_prompt", "x_sample", "cache_kv_cmp", "cache_kv_slc", "state_win_kv", "page_table", "norm1_g", "w_in",
              "gate_b", "gmlp_ln_g", "gmlp_ln_b", "gmlp_ws", "gmlp_bs", "cmp_pe_k", "cmp_wk1", "cmp_bk1", "cmp_wk2",
              "cmp_pe_v", "cmp_wv1", "cmp_bv1", "cmp_wv2", "out_norm_a", "out_norm_b", "w_out", "norm2_g", "w_gate",
              "w_up", "w_down", "final_norm_g"]
OUTPUTS = [("y_prompt", (1, SEQ, D)), ("y_sample", (NB, 1, D)), ("p_kv_cmp", (1, 1, SEQ, 2, NG, DH)),
           ("p_kv_slc", (1, 1, SEQ, 2, NG, DH)), ("p_win_kv", (1, 1, 512, 2, NG, DH)),
           ("p_gmlp_v", (1, 1, P, GH, DH)), ("s_kv_cmp", (1, NB, 1, 2, NG, DH)), ("s_kv_slc", (1, NB, 1, 2, NG, DH)),
           ("s_win_kv", (1, NB, 512, 2, NG, DH)), ("s_gmlp_v", (1, NB, 1, GH, DH))]


def build_program(nc, A, C, O):
    ctx = ExitStack()

    sb_at = {}

    def sb(name, shape, dt=F32):
        sb_at[name] = -(-nc.sbuf_base // 32) * 32
        return ctx.enter_context(nc.sbuf_tensor(name, shape, dt))

    def rounded(name, shape, base, word=0):
        return nc.alloc_sbuf_tensor_at(name, shape, F32R, offset=sb_at[base] + 4 * word)

    def sem(name):
        return ctx.enter_context(nc.semaphore(name))

    bank = [ctx.enter_context(nc.psum_tensor(f"bankpair{i}", [P, 1024], F32)) for i in range(4)]

    def pb(i):
        return bank[i // 2][:, 512 * (i % 2):512 * (i % 2) + 512]

    x_all = sb("x_all", [P, XT, D])
    REGC, ARENA = 2776, 13824
    work = sb("work", [P, REGC + ARENA + KD * TOK])
    regC = work[:, 0:REGC]
    arena = work[:, REGC:REGC + ARENA]
    hT_flat = work[:, REGC + ARENA:REGC + ARENA + KD * TOK]
    hT = hT_flat.rearrange("p (k n) -> p k n", k=KD)
    sb_at["arena"], sb_at["hT"] = sb_at["work"] + 4 * REGC, sb_at["work"] + 4 * (REGC + ARENA)
    q_all = sb("q_all", [P, 4, TOK])
    kT_space = sb("kT_space", [P, 4 * SEQ])
    kT = kT_space[0:KAUG, :].rearrange("p (c n) -> p c n", c=4)
    v_all = sb("v_all", [P, NT, 2, P])
    oaT = sb("oaT", [P, 4, TOK])
    kcT_p = sb("kcT_p", [KAUG, NG, 64])
    vc_p = sb("vc_p", [64, P])
    ident = sb("ident", [P, P])
    ident_bf = sb("ident_bf", [P, P], BF16)
    mask_diag = sb("mask_diag", [P, P], BF16)
    mask_low = sb("mask_low", [P, P], BF16)
    mask_cmp = sb("mask_cmp", [P, NT, 64], BF16)
    imp_add = sb("imp_add", [P, NT, NBLK])
    norm_g = sb("norm_g", [P, D])
    normb_g = sb("normb_g", [P, 512])
    gate = sb("gate", [P, XT, 24])
    samp = sb("samp", [P, 1304])
    kv_new = samp[0:NB, 0:792]
    q_s = samp[0:NB, 792:1304]
    ob_s = sb("ob_s", [NB, 512])
    minus_half = sb("minus_half", [P, 8])
    small = sb("small", [P, 144])
    lnr = sb("lnr", [P, 3, GH])
    pages = ob_s[0:1, 0:NB * PAGES].bitcast(I32)

    def at(off, shape, base=None):
        n = int(np.prod(shape))
        v = (arena if base is None else base)[:, off:off + n]
        if len(shape) == 2:
            v = v.rearrange("p (a b) -> p a b", a=shape[0])
        elif len(shape) == 3:
            v = v.rearrange("p (a b c) -> p a b c", a=shape[0], b=shape[1])
        elif len(shape) == 4:
            v = v.rearrange("p (a b c d) -> p a b c d", a=shape[0], b=shape[1], c=shape[2])
        return v

    class Chain:

        def __init__(self, eng, s):
            self.eng, self.s, self.n = eng, s, 0

        def link(self, ins):
            self.n += 1
            ins.then_inc(self.s, 1)
            self.eng.wait_ge(self.s, self.n)

    vec_chain, pool_chain = sem("vec_chain"), sem("pool_chain")

    def inv_rms(pool, link, total, out, width):
        link(pool.tensor_scalar(out, total, 1.0 / width, EPS, ALU.mult, ALU.add))
        n = out.shape[1]
        return pool.tensor_tensor(out, out, minus_half[0:out.shape[0], 0:n], ALU.pow)

    def norm_rows(v):
        return v.rearrange("(a n) -> a n", a=1)

    wslot = [at(0, [KD, 512]), at(4096, [KD, 512])]
    kvst = at(8192, [2, 512])
    h_ring = at(9216, [2, D])
    sq_big = at(11264, [D])
    ws_raw = at(12288, [GH, P])
    vg = at(9216, [2, 512])
    u_sb = at(10240, [2, 512])
    oa = at(11264, [2, 512])
    sq = at(12288, [512])
    wsT = at(0, [GH, P], regC)
    ln_g = at(1024, [512], regC)
    ln_b = at(1536, [512], regC)
    norma_g = at(2048, [512], regC)
    gate_b = at(2560, [24], regC)
    bs_raw = at(2584, [P], regC)
    bsT = at(2712, [GH], regC)
    w00 = at(2720, [GH], regC)
    b00 = at(2728, [GH], regC)
    upper = at(13312, [P])
    ssx, ssa = small[:, 0:9], small[:, 9:18]
    rx, ra = small[:, 18:27], small[:, 27:36]

    CH = [(1536, 512), (2048, 280), (1024, 512), (512, 512), (0, 512)]

    x_in = [sem(f"x_in{t}") for t in range(XT)]
    ident_in, const_in = sem("ident_in"), sem("const_in")
    w_in_ready = [sem(f"w_in_ready{c}") for c in range(5)]
    zeroed = sem("zeroed")
    x_squared, x_scaled_by, h_ready = sem("x_squared"), sem("x_scaled_by"), sem("h_ready")
    h_turned, hT_low, hT_high = sem("h_turned"), sem("hT_low"), sem("hT_high")
    ws_turned, ws_masked = sem("ws_turned"), sem("ws_masked")
    z_ready, z_taken = sem("z_ready"), sem("z_taken")
    k_turned, kT_ready, v_kept = sem("k_turned"), sem("kT_ready"), sem("v_kept")
    kv_stored = [sem("kv_stored0"), sem("kv_stored1")]
    new_stored, gv_stored = sem("new_stored"), sem("gv_stored")
    gate_raw, gate_tanh, gate_ready = sem("gate_raw"), sem("gate_tanh"), sem("gate_ready")
    v_centered, v_squared, v_var, v_inv, vn_ready = (sem("v_centered"), sem("v_squared"), sem("v_var"),
                                                     sem("v_inv"), sem("vn_ready"))
    mixed, oa_ready, oa_squared, oa_inv = sem("mixed"), sem("oa_ready"), sem("oa_squared"), sem("oa_inv")
    oan_ready, oa_turned, oaT_ready = sem("oan_ready"), sem("oa_turned"), sem("oaT_ready")
    win_copied = sem("win_copied")

    loads1 = [
        (ident[:, :], C["ident"]), (norm_g[:, :], norm_rows(A["norm1_g"][0]).to_broadcast([P, D])), (upper, C["upper01"]),
        (ws_raw, A["gmlp_ws"][0].rearrange("h t s -> t h s")), (bs_raw[0:GH, :], A["gmlp_bs"][0]),
        (ln_g, norm_rows(A["gmlp_ln_g"][0].rearrange("h d -> (h d)")).to_broadcast([P, 512])),
        (ln_b, norm_rows(A["gmlp_ln_b"][0].rearrange("h d -> (h d)")).to_broadcast([P, 512])),
        (norma_g, norm_rows(A["out_norm_a"][0]).to_broadcast([P, 512])),
        (normb_g[:, :], norm_rows(A["out_norm_b"][0]).to_broadcast([P, 512])),
        (gate_b, norm_rows(A["gate_b"][0]).to_broadcast([P, 24])),
        (w00[0:NB, :], A["gmlp_ws"][0, :, 0, 0:1].rearrange("h o -> o h").to_broadcast([NB, GH])),
        (b00[0:NB, :], A["gmlp_bs"][0, :, 0:1].rearrange("h o -> o h").to_broadcast([NB, GH])),
        (ident_bf[:, :], C["ident_bf"]), (mask_diag[:, :], C["mask_diag"]), (mask_low[:, :], C["mask_low"]),
        (mask_cmp[:, :, :], C["mask_cmp"]), (imp_add[:, :, :], C["imp_add"]),
        (kT[64:KAUG, :, :], C["kaug"]), (kcT_p[64:KAUG, :, :], C["kaug_cmp"]), (pages[:, :], norm_rows(A["page_table"].rearrange("b p -> (b p)"))),
    ]

    def x_dram(t):
        return A["x_prompt"][0, P * t:P * t + P, :] if t < NT else A["x_sample"][:, 0, :]

    def load_w_in(sp, c):
        c0, w = CH[c]
        if c >= 2:
            sp.wait_ge(z_ready, 9 * (c - 1))
        sp.dma_start(wslot[c % 2][:, :, 0:w], A["w_in"][0].rearrange("(k p) n -> p k n", p=P)[:, :, c0:c0 + w])\
          .then_inc(w_in_ready[c], 16)

    def stage1_sync(sp):
        with nc.allow_non_contiguous_dma(reason="one value per head of the sample mixer"):
            sp.dma_start(x_all[:, 0, :], x_dram(0)).then_inc(x_in[0], 16)
            for dst, src in loads1[:2]:
                sp.dma_start(dst, src).then_inc(ident_in, 16)
            sp.dma_start(x_all[:, 1, :], x_dram(1)).then_inc(x_in[1], 16)
            load_w_in(sp, 0)
            for t in range(2, XT):
                sp.dma_start(x_all[0:rows(t), t, :], x_dram(t)).then_inc(x_in[t], 16)
            for dst, src in loads1[2:]:
                sp.dma_start(dst, src).then_inc(const_in, 16)
            load_w_in(sp, 1)
            sp.dma_start(O["s_win_kv"][0, :, 0:511].rearrange("b w k g d -> b (w k g d)"),
                         A["state_win_kv"][0, :, 1:512].rearrange("b w k g d -> b (w k g d)")).then_inc(win_copied, 16)
            for c in (2, 3, 4):
                load_w_in(sp, c)

    ALL_CONST = 16 * (len(loads1) - 2)

    def zn(c, t):
        return 9 * c + t if c < 3 else 27 + 2 * t + (c - 3)

    def stage1_tensor(pe):
        pe.wait_ge(ident_in, 32)

        def turn_ws():
            pe.wait_ge(const_in, ALL_CONST)
            for h in range(GH):
                ins = pe.transpose(pb(6 + h // 4)[:, P * (h % 4):P * (h % 4) + P], ws_raw[:, h, :], ident[:, :])
            ins.then_inc(ws_turned, 1)
            pe.transpose(pb(3)[:, 0:GH], bs_raw[0:GH, :], ident[0:GH, 0:GH]).then_inc(ws_turned, 1)

        def turn_h(t):
            n = rows(t)
            pe.wait_ge(h_ready, t + 1)
            if t >= 1:
                pe.wait_ge(hT_low, t)
                pe.wait_ge(hT_high, t)
            for k in range(KD):
                ins = pe.transpose(pb(4 + k // 4)[:, P * (k % 4):P * (k % 4) + n],
                                   h_ring[0:n, t % 2, P * k:P * k + P], ident[0:n, 0:n])
            ins.then_inc(h_turned, 1)

        def project(c, t):
            n, w, at_n = rows(t), CH[c][1], zn(c, t)
            pe.wait_ge(w_in_ready[c], 16)
            if c == 0:
                pe.wait_ge(hT_low, t + 1)
                pe.wait_ge(hT_high, t + 1)
            if at_n >= 4:
                pe.wait_ge(z_taken, at_n - 3)
            if at_n == 3:
                pe.wait_ge(ws_masked, 3)
            for k in range(KD):
                ins = pe.matmul(pb(at_n % 4)[0:n, 0:w], hT[:, k, P * t:P * t + n], wslot[c % 2][:, k, 0:w],
                                start=(k == 0), stop=(k == KD - 1))
            ins.then_inc(z_ready, 1)

        def turn_k(m):
            c, t = m // NT, m % NT
            pe.wait_ge(z_taken, zn(c, t) + 1)
            if m == 0:
                pe.wait_ge(ws_masked, 2)
            if m >= 2:
                pe.wait_ge(kT_ready, m - 1)
            col = 256 if c == 0 else 0
            for g in range(NG):
                ins = pe.transpose(pb(6 + m % 2)[0:DH, P * g:P * g + P], kvst[:, m % 2, col + DH * g:col + DH * g + DH],
                                   ident[:, :])
            ins.then_inc(k_turned, 1)

        turn_h(0)
        turn_h(1)
        for t in range(XT):
            project(0, t)
            if t == 1:
                turn_ws()
            if t == 2:
                turn_k(0)
            if t >= 2:
                turn_k(t - 1)
            if t + 2 < XT:
                turn_h(t + 2)
        for t in range(XT):
            project(1, t)
            if t >= 1:
                turn_k(NT + t - 1)
        for t in range(XT):
            project(2, t)

        def mix(t):
            pe.wait_ge(vn_ready, t + 1)
            if t >= 2:
                pe.wait_ge(oa_ready, t - 1)
            else:
                pe.wait_ge(kT_ready, 2 * NT)
            for h in range(GH):
                ins = pe.matmul(pb(6 + t % 2)[:, DH * h:DH * h + DH], wsT[:, h, :], vg[:, t % 2, DH * h:DH * h + DH],
                                start=True, stop=True)
            ins.then_inc(mixed, 1)

        def turn_oa(t):
            n = rows(t)
            pe.wait_ge(oan_ready, t + 1)
            if t >= 2:
                pe.wait_ge(oaT_ready, t - 1)
            for k in range(4):
                ins = pe.transpose(pb(4 + t % 2)[:, P * k:P * k + n], oa[0:n, t % 2, P * k:P * k + P], ident[0:n, 0:n])
            ins.then_inc(oa_turned, 1)

        for t in range(XT + 2):
            if t < XT:
                project(3, t)
            if 2 <= t:
                turn_oa(t - 2)
            if 1 <= t <= NT:
                mix(t - 1)
            if t < XT:
                project(4, t)

    def stage1_scalar(act):
        for t in range(2):
            square_x(act, t)
        take_hT(act, 0)
        square_x(act, 2)
        for t in range(XT):
            if t + 1 < XT:
                take_hT(act, t + 1)
            if t + 3 < XT:
                square_x(act, t + 3)
            take_z(act, 0, t)
        for c in (1, 2):
            for t in range(XT):
                take_z(act, c, t)
        act.wait_ge(gate_raw, XT + 1)
        act.activation(gate[:, :, :], gate[:, :, :], ACT.Tanh, scale=0.5).then_inc(gate_tanh, 1)
        for t in range(XT + 2):
            if t < XT:
                take_z(act, 3, t)
            if t >= 2:
                n = rows(t - 2)
                act.wait_ge(oa_turned, t - 1)
                act.activation(oaT[:, :, P * (t - 2):P * (t - 2) + n],
                               pb(4 + t % 2).rearrange("p (k n) -> p k n", k=4)[:, :, 0:n], ACT.Copy)\
                   .then_inc(oaT_ready, 1)
            if t < XT:
                n = rows(t)
                act.wait_ge(v_centered, t + 1)
                if t >= 1:
                    act.wait_ge(v_var, t)
                if t >= 2:
                    act.wait_ge(oa_squared, t - 1)
                act.activation(sq[0:n, :], vg[0:n, t % 2, :], ACT.Square).then_inc(v_squared, 1)
            if 1 <= t <= XT:
                n = rows(t - 1)
                act.wait_ge(oa_ready, t)
                act.wait_ge(v_var, min(t + 1, XT))
                if t >= 2:
                    act.wait_ge(oa_squared, t - 1)
                act.activation(sq[0:n, :], oa[0:n, (t - 1) % 2, :], ACT.Square, accum_out=ssa[0:n, t - 1:t])\
                   .then_inc(oa_squared, 1)
            if t < XT:
                take_z(act, 4, t)
            if t == XT - 1:
                load_w_cmp(act)

    def square_x(act, t):
        n = rows(t)
        act.wait_ge(x_in[t], 16)
        if t >= 1:
            act.wait_ge(x_squared, t)
        act.activation(sq_big[0:n, :], x_all[0:n, t, :], ACT.Square, accum_out=ssx[0:n, t:t + 1]).then_inc(x_squared, 1)

    def take_hT(act, t):
        n = rows(t)
        act.wait_ge(h_turned, t + 1)
        act.activation(hT[:, 0:4, P * t:P * t + n], pb(4).rearrange("p (k n) -> p k n", k=4)[:, :, 0:n], ACT.Copy)\
           .then_inc(hT_low, 1)

    def take_z(act, c, t):
        n, w, at_n = rows(t), CH[c][1], zn(c, t)
        z = pb(at_n % 4)[0:n, 0:w]
        act.wait_ge(z_ready, at_n + 1)
        if c < 2 and t < NT:
            m = c * NT + t
            if m >= 2:
                act.wait_ge(k_turned, m - 1)
                act.wait_ge(v_kept, m - 1)
                act.wait_ge(kv_stored[m % 2], stores_before(m))
                if c == 1 and t >= 2:
                    act.wait_ge(gate_raw, t)
            act.activation(kvst[0:n, m % 2, 0:w], z, ACT.Copy).then_inc(z_taken, 1)
        elif c < 2:
            act.activation(kv_new[:, 512 * c:512 * c + w], z, ACT.Copy).then_inc(z_taken, 1)
        elif c == 2:
            dst = q_all[:, :, P * t:P * t + P] if t < NT else q_s
            src = z.rearrange("p (k n) -> p k n", k=4) if t < NT else z
            act.activation(dst, src, ACT.Copy, scale=DH ** -0.5).then_inc(z_taken, 1)
        elif c == 4:
            if t >= 2:
                act.wait_ge(oa_ready, t - 1)
            else:
                act.wait_ge(h_turned, XT)
            act.activation(u_sb[0:n, t % 2, :], z, ACT.Gelu_apprx_tanh).then_inc(z_taken, 1)
        else:
            if t >= 2:
                act.wait_ge(mixed, t - 1)
            if t >= 2:
                act.wait_ge(vn_ready, t - 1)
            act.activation(vg[0:n, t % 2, :], z, ACT.Gelu_apprx_tanh).then_inc(z_taken, 1)

    def stores_before(m):
        def stored(j):
            return 2 if j < NT else (1 if j - NT >= 4 else 0)
        return 16 * sum(stored(j) for j in range(m % 2, m - 1, 2))

    def stage1_pool(pool):
        chain = Chain(pool, pool_chain)
        pool.memset(minus_half[:, :], -0.5).then_inc(zeroed, 1)
        pool.memset(gate[:, :, :], 0.0).then_inc(gate_raw, 1)
        pool.wait_ge(zeroed, 1)

        def inv_x(t):
            pool.wait_ge(x_squared, t + 1)
            inv_rms(pool, chain.link, ssx[0:rows(t), t:t + 1], rx[0:rows(t), t:t + 1], D).then_inc(x_scaled_by, 1)

        def store_kv(c, t):
            m = c * NT + t
            pool.wait_ge(z_taken, zn(c, t) + 1)
            if t < NT:
                col = 384 if c == 0 else 128
                pool.tensor_copy(v_all[:, t, c, :], kvst[:, m % 2, col:col + P]).then_inc(v_kept, 1)
                r = slice(P * t, P * t + P)
                flat = "s k g d -> s (k g d)"
                if c == 0:
                    pool.dma_start(O["p_kv_cmp"][0, 0, r].rearrange(flat), kvst[:, m % 2, 0:256])\
                        .then_inc(kv_stored[m % 2], 16)
                    pool.dma_start(O["p_kv_slc"][0, 0, r].rearrange(flat), kvst[:, m % 2, 256:512])\
                        .then_inc(kv_stored[m % 2], 16)
                elif t >= 4:
                    pool.dma_start(O["p_win_kv"][0, 0, P * (t - 4):P * (t - 4) + P].rearrange(flat),
                                   kvst[:, m % 2, 0:256]).then_inc(kv_stored[m % 2], 16)
            elif c == 0:
                flat = "b s k g d -> b (s k g d)"
                pool.dma_start(O["s_kv_cmp"][0].rearrange(flat), kv_new[:, 0:256]).then_inc(new_stored, 16)
                pool.dma_start(O["s_kv_slc"][0].rearrange(flat), kv_new[:, 256:512]).then_inc(new_stored, 16)
            else:
                pool.dma_start(O["s_win_kv"][0, :, 511].rearrange("b k g d -> b (k g d)"), kv_new[:, 512:768])\
                    .then_inc(new_stored, 16)

        for t in range(3):
            inv_x(t)
        for t in range(XT):
            if t + 3 < XT:
                inv_x(t + 3)
            store_kv(0, t)
        for t in range(XT):
            store_kv(1, t)
        for t in range(XT + 1):
            if t < XT:
                n = rows(t)
                pool.wait_ge(v_var, t + 1)
                inv_rms(pool, chain.link, lnr[0:n, 1, :], lnr[0:n, 2, :], DH).then_inc(v_inv, 1)
                if t >= NT - 1:
                    pool.wait_ge(vn_ready, t + 1)
                    if t == NT - 1:
                        dst = O["p_gmlp_v"][0, 0].rearrange("s h d -> s (h d)")
                    else:
                        dst = O["s_gmlp_v"][0].rearrange("b s h d -> b (s h d)")
                    pool.dma_start(dst, vg[0:n, t % 2, :]).then_inc(gv_stored, 16)
            if t >= 1:
                pool.wait_ge(oa_squared, t)
                n = rows(t - 1)
                inv_rms(pool, chain.link, ssa[0:n, t - 1:t], ra[0:n, t - 1:t], 512).then_inc(oa_inv, 1)
            if t == NT:
                pool.wait_ge(const_in, ALL_CONST)
                pool.wait_ge(z_ready, 9 * 5)
                load_raw(pool, 0, 1, raw_ready_pool)
        return chain

    def stage1_vector(dve):
        chain = Chain(dve, vec_chain)
        link = chain.link
        dve.wait_ge(ident_in, 32)

        def scale_h(t):
            n = rows(t)
            dve.wait_ge(x_scaled_by, t + 1)
            if t >= 2:
                dve.wait_ge(h_turned, t - 1)
            dve.scalar_tensor_tensor(out=h_ring[0:n, t % 2, :], in0=x_all[0:n, t, :], scalar=rx[0:n, t:t + 1],
                                     in1=norm_g[0:n, :], op0=ALU.mult, op1=ALU.mult).then_inc(h_ready, 1)

        def take_hT_high(t):
            n = rows(t)
            dve.wait_ge(h_turned, t + 1)
            dve.tensor_copy(hT[:, 4:8, P * t:P * t + n], pb(5).rearrange("p (k n) -> p k n", k=4)[:, :, 0:n])\
               .then_inc(hT_high, 1)

        def take_kT(m):
            c, t = m // NT, m % NT
            dve.wait_ge(k_turned, m + 1)
            dve.tensor_copy(kT[0:DH, 2 * c:2 * c + 2, P * t:P * t + P],
                            pb(6 + m % 2)[0:DH, 0:256].rearrange("p (g n) -> p g n", g=2)).then_inc(kT_ready, 1)

        scale_h(0)
        scale_h(1)

        def mask_ws():
            dve.wait_ge(const_in, ALL_CONST)
            dve.wait_ge(ws_turned, 2)
            for b in range(2):
                dve.tensor_tensor(wsT[:, 4 * b:4 * b + 4, :], pb(6 + b).rearrange("p (h n) -> p h n", h=4),
                                  upper[:, None, :].to_broadcast([P, 4, P]), ALU.mult).then_inc(ws_masked, 1)
            dve.tensor_copy(bsT, pb(3)[:, 0:GH]).then_inc(ws_masked, 1)

        take_hT_high(0)
        scale_h(2)
        for t in range(XT):
            if t + 1 < XT:
                take_hT_high(t + 1)
            if t + 3 < XT:
                scale_h(t + 3)
            if t == 1:
                mask_ws()
            if t == 2:
                take_kT(0)
            if t >= 2:
                take_kT(t - 1)

        def add_gate_b(t):
            n = rows(t)
            dve.wait_ge(z_taken, zn(1, t) + 1)
            if t == 0:
                dve.wait_ge(gate_raw, 1)
            src = kvst[0:n, t % 2, 256:280] if t < NT else kv_new[:, 768:792]
            dve.tensor_tensor(gate[0:n, t, :], src, gate_b[0:n, :], ALU.add).then_inc(gate_raw, 1)

        for t in range(XT):
            add_gate_b(t)
            if t >= 1:
                take_kT(NT + t - 1)
        dve.wait_ge(gate_tanh, 1)
        dve.tensor_scalar(gate[:, :, :], gate[:, :, :], 0.5, 0.5, ALU.mult, ALU.add).then_inc(gate_ready, 1)

        def per_head(a, n):
            return a[0:n, :, None].to_broadcast([n, GH, DH])

        def heads(a, n, slot):
            return a[0:n, slot, :].rearrange("p (h d) -> p h d", h=GH)

        def layer_norm(t):
            n = rows(t)
            v = heads(vg, n, t % 2)
            dve.wait_ge(z_taken, zn(3, t) + 1)
            link(dve.tensor_reduce(lnr[0:n, 0, :], v, AX, ALU.add))
            link(dve.tensor_scalar(lnr[0:n, 0, :], lnr[0:n, 0, :], -1.0 / DH, None, ALU.mult))
            dve.tensor_tensor(v, v, per_head(lnr[:, 0, :], n), ALU.add).then_inc(v_centered, 1)
            dve.wait_ge(v_squared, t + 1)
            dve.tensor_reduce(lnr[0:n, 1, :], sq[0:n, :].rearrange("p (h d) -> p h d", h=GH), AX, ALU.add)\
               .then_inc(v_var, 1)
            dve.wait_ge(v_inv, t + 1)
            link(dve.tensor_tensor(v, v, per_head(lnr[:, 2, :], n), ALU.mult))
            link(dve.tensor_tensor(vg[0:n, t % 2, :], vg[0:n, t % 2, :], ln_g[0:n, :], ALU.mult))
            dve.tensor_tensor(vg[0:n, t % 2, :], vg[0:n, t % 2, :], ln_b[0:n, :], ALU.add).then_inc(vn_ready, 1)

        def gate_mixed(t):
            n = rows(t)
            dve.wait_ge(z_taken, zn(4, t) + 1)
            o = heads(oa, n, t % 2)
            if t >= 2:
                dve.wait_ge(oa_turned, t - 1)
            if t < NT:
                dve.wait_ge(mixed, t + 1)
                link(dve.tensor_tensor(o, pb(6 + t % 2).rearrange("p (h d) -> p h d", h=GH), per_head(bsT, n), ALU.add))
            else:
                dve.wait_ge(vn_ready, XT)
                link(dve.tensor_tensor(o, heads(vg, n, t % 2), per_head(w00, n), ALU.mult))
                link(dve.tensor_tensor(o, o, per_head(b00, n), ALU.add))
            dve.tensor_tensor(oa[0:n, t % 2, :], oa[0:n, t % 2, :], u_sb[0:n, t % 2, :], ALU.mult).then_inc(oa_ready, 1)

        def norm_oa(t):
            n = rows(t)
            dve.wait_ge(oa_inv, t + 1)
            dve.scalar_tensor_tensor(out=oa[0:n, t % 2, :], in0=oa[0:n, t % 2, :], scalar=ra[0:n, t:t + 1],
                                     in1=norma_g[0:n, :], op0=ALU.mult, op1=ALU.mult).then_inc(oan_ready, 1)

        for t in range(XT + 1):
            if t >= 1:
                gate_mixed(t - 1)
            if t < XT:
                layer_norm(t)
            if t >= 1:
                norm_oa(t - 1)
        return chain

    w1 = [at(0, [16, P]), at(2048, [16, P])]
    raw = [at(4096, [4, 512]), at(6144, [4, 512])]
    sorted_rows = at(11264, [4, 4, P])
    hid = [at(8192, [4, 64]), at(8448, [4, 64])]
    w2 = [at(8704, [DH]), at(8768, [DH])]
    b1 = at(8832, [2])
    pe_raw = at(8834, [2, P])
    peT = at(9090, [2, 16])
    hid_bias = at(9122, [2])
    kcT_s = at(9216, [NB, NG, 64])
    vc_s = at(10240, [NB, P])
    pairsT = at(0, [2, 4, 8, 64], hT_flat), at(4096, [2, 4, 8, 64], hT_flat)
    NS = NB + 1

    w_cmp_ready = sem("w_cmp_ready")
    raw_ready = [sem("raw_ready0"), sem("raw_ready1")]
    raw_ready_pool = [sem("raw_ready_pool0"), sem("raw_ready_pool1")]
    pe_turned, pe_taken, bias_summed, bias_ready = sem("pe_turned"), sem("pe_taken"), sem("bias_summed"), sem("bias_ready")
    sorted_even, sorted_odd, pairs_turned = sem("sorted_even"), sem("sorted_odd"), sem("pairs_turned")
    pairs_even, pairs_odd = sem("pairs_even"), sem("pairs_odd")
    hid_summed, hid_ready = sem("hid_summed"), sem("hid_ready")
    cmp_summed, kc_ready, vc_ready = sem("cmp_summed"), sem("kc_ready"), sem("vc_ready")

    def load_w_cmp(act):
        act.wait_ge(z_ready, 9 * 5)
        act.wait_ge(k_turned, 2 * NT)
        act.wait_ge(v_kept, 2 * NT)
        act.wait_ge(gate_raw, XT + 1)
        for slot in range(2):
            act.wait_ge(kv_stored[slot], stores_before(2 * NT + slot))
        names = [("cmp_wk1", "cmp_wk2", "cmp_bk1", "cmp_pe_k"), ("cmp_wv1", "cmp_wv2", "cmp_bv1", "cmp_pe_v")]
        for kv in range(2):
            n1, n2, nb, npe = names[kv]
            for b in range(2):
                act.dma_start(w1[kv][:, 8 * b:8 * b + 8, :], A[n1][0, D * b:D * b + D].rearrange("(r p) h -> p r h", p=P))\
                   .then_inc(w_cmp_ready, 16)
            act.dma_start(w2[kv], A[n2][0]).then_inc(w_cmp_ready, 16)
            act.dma_start(b1[:, kv:kv + 1], A[nb][0].rearrange("(h o) -> h o", o=1)).then_inc(w_cmp_ready, 16)
            act.dma_start(pe_raw[0:16, kv, :], A[npe][0].rearrange("(r t) d -> r (t d)", t=2)).then_inc(w_cmp_ready, 16)

    def stage2_sync(sp):
        sp.wait_ge(z_ready, 9 * 5)
        for s in range(NS):
            if s == 3:
                load_tables(sp)
            if s < NB:
                load_raw(sp, s, 0, raw_ready)
            else:
                wait_raw_free(sp, s)
                for slot in range(2):
                    sp.wait_ge(kv_stored[slot], stores_before(2 * NT + slot))
                src = O["p_kv_cmp"][0, 0].rearrange("(a r t) k g d -> r a (t k g d)", r=P, t=2)
                sp.dma_start(raw[s % 2][:, :, :], src).then_inc(raw_ready[s % 2], 16)

    def wait_raw_free(eng, s):
        if s >= 2:
            eng.wait_ge(sorted_even, 2 * (s - 1))
            eng.wait_ge(sorted_odd, 2 * (s - 1))

    def load_raw(eng, s, half, done):
        pool_rows = A["cache_kv_cmp"][0].rearrange("n (r t) k g d -> n r (t k g d)", t=2)
        wait_raw_free(eng, s)
        with eng.Fori(0, 4) as a:
            page = eng.value_load(pages[0:1, bass.ds(a * 2 + (s * PAGES + half), 1)], min_val=0,
                                  max_val=pool_rows.shape[0] - 1)
            eng.dma_start(raw[s % 2][64 * half:64 * half + 64, bass.ds(a, 1), :],
                          pool_rows[bass.ds(page, 1)].rearrange("o r c -> r o c")).then_inc(done[s % 2], 16)

    def sort_rows(eng, copy, s, a, done):
        if a < 2:
            eng.wait_ge(raw_ready[s % 2], 64 * (s // 2 + 1) if s < NB else 64 * (s // 2) + 16)
            if s < NB:
                eng.wait_ge(raw_ready_pool[s % 2], 64 * (s // 2 + 1))
        if s >= 1:
            eng.wait_ge(pairs_turned, 4 * (s - 1) + a + 1)
        elif a < 2:
            eng.wait_ge(oaT_ready, XT)
            eng.wait_ge(oa_squared, XT)
        copy(sorted_rows[:, a].rearrange("p c (t d) -> p t c d", t=2),
             raw[s % 2][:, a].rearrange("p (t c d) -> p t c d", t=2, c=4)).then_inc(done, 1)

    def group_seqs(w):
        return [s for s in (2 * w, 2 * w + 1) if s < NS]

    NW = (NS + 1) // 2

    def stage2_pool(pool):
        for s in range(1, NB):
            load_raw(pool, s, 1, raw_ready_pool)

    def stage2_tensor(pe):
        def sum_bias():
            pe.wait_ge(w_cmp_ready, 160)
            pe.wait_ge(oaT_ready, XT)
            for kv in range(2):
                ins = pe.transpose(pb(4)[:, 16 * kv:16 * kv + 16], pe_raw[0:16, kv, :], ident[0:16, 0:16])
            ins.then_inc(pe_turned, 1)
            pe.wait_ge(pe_taken, 1)
            for kv in range(2):
                for r in range(16):
                    ins = pe.matmul(pb(5)[:, kv:kv + 1], w1[kv][:, r, :], peT[:, kv, r:r + 1], start=(r == 0), stop=(r == 15))
            ins.then_inc(bias_summed, 1)

        def turn_pairs(s):
            for a in range(4):
                n = 4 * s + a
                pe.wait_ge(sorted_odd if a % 2 else sorted_even, 2 * s + a // 2 + 1)
                if n >= 4:
                    if n % 2 == 0:
                        pe.wait_ge(pairs_even, (n - 4) // 2 + 1)
                    else:
                        pe.wait_ge(pairs_odd, (n - 4) // 2 + 1)
                else:
                    pe.wait_ge(z_taken, 45)
                for kvg in range(4):
                    ins = pe.transpose(pb(n % 4)[:, P * kvg:P * kvg + P], sorted_rows[:, a, kvg, :], ident[:, :])
                ins.then_inc(pairs_turned, 1)

        def hidden(w):
            ns = len(group_seqs(w))
            pe.wait_ge(pairs_even, 2 * (2 * w + ns))
            pe.wait_ge(pairs_odd, 2 * (2 * w + ns))
            if w == 0:
                pe.wait_ge(bias_ready, 1)
            else:
                pe.wait_ge(hid_ready, 2 * w)
            for kv in range(2):
                for r in range(16):
                    b = r // 8
                    mov = pairsT[w % 2][:, 0:ns, 2 * kv:2 * kv + 2, r % 8, b:b + CMP_N]
                    out = pb(4 + kv)[:, 0:2 * ns * CMP_N].rearrange("p (s g n) -> p s g n", s=ns, g=NG)
                    ins = pe.matmul(out, w1[kv][:, r, :], mov, start=(r == 0), stop=(r == 15))
                ins.then_inc(hid_summed, 1)

        def compressed(w):
            ns = len(group_seqs(w))
            m = 2 * ns
            pe.wait_ge(hid_ready, 2 * w + 2)
            if w >= 1:
                pe.wait_ge(kc_ready, w)
                pe.wait_ge(vc_ready, w)
            pe.matmul(pb(6)[0:DH, 0:m * CMP_N].rearrange("p (m n) -> p m n", m=m), w2[0], hid[0][:, 0:m, 0:CMP_N],
                      start=True, stop=True)
            for j in range(m):
                ins = pe.matmul(pb(7)[0:CMP_N, DH * j:DH * j + DH], hid[1][:, j, 0:CMP_N], w2[1], start=True, stop=True)
            ins.then_inc(cmp_summed, 1)

        for w in range(NW):
            for s in group_seqs(w):
                turn_pairs(s)
            if w >= 1:
                compressed(w - 1)
            else:
                sum_bias()
            hidden(w)
        compressed(NW - 1)

    def take_pairs(eng_copy, n, done):
        s, a = n // 4, n % 4
        dst = pairsT[(s // 2) % 2][:, s % 2, :, :, 16 * a:16 * a + 16]
        src = pb(n % 4).rearrange("p (c h r) -> p c r h", c=4, r=8)
        for c in range(4):
            ins = eng_copy(dst[:, c], src[:, c])
        ins.then_inc(done, 1)

    def stage2_scalar(act):
        def hid_gelu(w):
            ns = len(group_seqs(w))
            m = 2 * ns
            for kv in range(2):
                act.wait_ge(hid_summed, 2 * w + kv + 1)
                if w == 0:
                    act.wait_ge(bias_ready, 1)
                else:
                    act.wait_ge(cmp_summed, w)
                act.activation(hid[kv][:, 0:m, 0:CMP_N], pb(4 + kv)[:, 0:m * CMP_N].rearrange("p (m n) -> p m n", m=m),
                               ACT.Gelu_apprx_tanh, bias=hid_bias[:, kv:kv + 1]).then_inc(hid_ready, 1)

        for w in range(NW):
            for s in group_seqs(w):
                for a in (1, 3):
                    sort_rows(act, lambda d, i: act.activation(d, i, ACT.Copy), s, a, sorted_odd)
                for a in (1, 3):
                    n = 4 * s + a
                    act.wait_ge(pairs_turned, n + 1)
                    if s % 2 == 0 and w >= 2:
                        act.wait_ge(hid_summed, 2 * (w - 1))
                    take_pairs(lambda d, i: act.activation(d, i, ACT.Copy), n, pairs_odd)
            hid_gelu(w)

    def stage2_vector(dve, chain):
        def take_bias():
            dve.wait_ge(pe_turned, 1)
            dve.tensor_copy(peT, pb(4)[:, 0:32].rearrange("p (a r) -> p a r", a=2)).then_inc(pe_taken, 1)
            dve.wait_ge(bias_summed, 1)
            dve.tensor_tensor(hid_bias, pb(5)[:, 0:2], b1, ALU.add).then_inc(bias_ready, 1)

        def keep(w):
            seqs = group_seqs(w)
            m = 2 * len(seqs)
            dve.wait_ge(cmp_summed, w + 1)
            k_src = pb(6)[0:DH, 0:m * CMP_N].rearrange("p (m n) -> p m n", m=m)
            v_src = pb(7)[0:CMP_N, 0:DH * m]
            if seqs[0] < NB:
                dve.tensor_copy(kcT_s[0:DH, 2 * w:2 * w + 2, :, 0:CMP_N].rearrange("p s g n -> p (s g) n"), k_src)\
                   .then_inc(kc_ready, 1)
                dve.tensor_copy(vc_s[0:CMP_N, 2 * w:2 * w + 2, :].rearrange("p s c -> p (s c)"), v_src).then_inc(vc_ready, 1)
            else:
                dve.tensor_copy(kcT_p[0:DH, :, 0:CMP_N], k_src).then_inc(kc_ready, 1)
                dve.tensor_copy(vc_p[0:CMP_N, :], v_src).then_inc(vc_ready, 1)

        for w in range(NW):
            for s in group_seqs(w):
                for a in (0, 2):
                    sort_rows(dve, dve.tensor_copy, s, a, sorted_even)
                for a in (0, 2):
                    n = 4 * s + a
                    dve.wait_ge(pairs_turned, n + 1)
                    if s % 2 == 0 and w >= 2:
                        dve.wait_ge(hid_summed, 2 * (w - 1))
                    take_pairs(dve.tensor_copy, n, pairs_even)
            if w == 0:
                take_bias()
                dve.wait_ge(gv_stored, 32)
            else:
                keep(w - 1)
        keep(NW - 1)

    NTILE = 12
    KVS = NTILE * P
    SP_PAGES, POOL_PAGES = 2, 4
    k_land = [0, REGC + 11264]
    in_hT = REGC + ARENA
    v_hold = [in_hT + KVS * 4, in_hT + KVS * 3, REGC + 4608, in_hT, REGC + 4608 + KVS, in_hT + KVS,
              REGC + 4608 + KVS * 2, in_hT + KVS * 2]

    def kv_part(word):
        return work[:, word:word + KVS].rearrange("p (c n) -> p c n", c=NTILE)

    k_rows = [kv_part(w) for w in k_land]
    v_rows = [kv_part(w) for w in v_hold]
    kTs = at(0, [2, NTILE * P])
    s_slc = at(0, [PAST + 1])
    s_win = at(1025, [513])
    q_pad = at(7680, [NB, 64], hT_flat)
    o_rows = at(0, [NB, P])
    pT_slc = at(2306, [8, 64])
    pT_win = at(2818, [4, 64])
    t_win = at(KVS, [513], regC)
    q_bd = at(2052, [NB, NH], regC)
    qTs = at(2116, [NB, NH], regC)
    knT = at(2180, [2, NB], regC)
    q_s2 = at(2196, [NR, NG, DH], regC)
    oT_s = at(2708, [64], regC)
    t_slc = at(3074, [PAST + 1])
    t_cmp = at(13312, [CMP_N])
    imp_add_s = at(13375, [17])
    s_cmp = at(12800, [CMP_N])
    imp_pad = at(12863, [65])
    imp_s = at(12928, [17])
    imp_hit = at(12945, [17])
    top_s = at(12962, [8])
    sel_s = at(12970, [17])
    st_s = at(12987, [16])
    same_group = at(13392, [64])
    seq_rows = at(13456, [64])
    rows_seq = at(13520, [8])
    head_pick = at(13528, [24])
    gate_rows = at(13003, [24])
    p_new = at(13027, [2, 8])
    gates_s = at(13043, [3])
    scT = at(13046, [64])
    pcT_s = at(13110, [64])
    pnT = at(13174, [2, 64])

    table_ready, t_slc_ready = sem("table_ready"), sem("t_slc_ready")
    kv_in = [sem("kv_in0"), sem("kv_in1")]
    kv_in_pool = [sem("kv_in_pool0"), sem("kv_in_pool1")]
    q_sorted, prep_turned, prep_taken = sem("q_sorted"), sem("prep_turned"), sem("prep_taken")
    cmp_scored, cmp_cols, cmp_turned, pc_ready = sem("cmp_scored"), sem("cmp_cols"), sem("cmp_turned"), sem("pc_ready")
    imp_summed = sem("imp_summed")
    k_tiles_turned, k_even, k_odd = sem("k_tiles_turned"), sem("k_even"), sem("k_odd")
    seq_scored, o_rows_taken, o_rows_turned = sem("seq_scored"), sem("o_rows_taken"), sem("o_rows_turned")
    max_s, exp_s, ps_ready = sem("max_s"), sem("exp_s"), sem("ps_ready")
    p_turned, pT_taken, seq_valued = sem("p_turned"), sem("pT_taken"), sem("seq_valued")
    oT_taken, o_turned, ob_s_ready = sem("oT_taken"), sem("o_turned"), sem("ob_s_ready")

    def stream_kv(eng, s, first, count, done):
        rows_of = A["cache_kv_slc"][0].rearrange("n t k g d -> n t k (g d)")
        if s == 0:
            eng.wait_ge(hid_summed, 2 * (NW - 1))
        if s == 1:
            eng.wait_ge(pairs_turned, 4 * NS)
        if s == 2:
            eng.wait_ge(hid_summed, 2 * NW)
            eng.wait_ge(cmp_summed, NW)
        if s >= 2:
            eng.wait_ge(k_tiles_turned, 3 * (s - 1))
        a = work[:, k_land[s % 2]:k_land[s % 2] + 1]
        dst = bass.AP(tensor=a.tensor, offset=a.offset,
                      ap=[a.ap[0], [v_hold[s] - k_land[s % 2], 2], [P, NTILE], [1, P]])
        with eng.Fori(0, count) as j:
            page = eng.value_load(pages[0:1, bass.ds(j + (s * PAGES + first), 1)], min_val=0,
                                  max_val=rows_of.shape[0] - 1)
            eng.dma_start(dst[:, :, bass.ds(j + first, 1), :],
                          rows_of[bass.ds(page, 1)].rearrange("o t k c -> t k o c")).then_inc(done[s % 2], 16)
        return dst

    def stream_last(act, s):
        win_of = A["state_win_kv"][0].rearrange("b (p c) k g d -> b p k c (g d)", c=4)
        dst = stream_kv(act, s, SP_PAGES + POOL_PAGES, PAGES - SP_PAGES - POOL_PAGES, kv_in)
        for kv in range(2):
            act.dma_start(dst[:, kv, 8:12, :], win_of[s, :, kv]).then_inc(kv_in[s % 2], 16)

    def wait_stream(eng, s):
        eng.wait_ge(kv_in[s % 2], 16 * (PAGES - POOL_PAGES + 2) * (s // 2 + 1))
        eng.wait_ge(kv_in_pool[s % 2], 16 * POOL_PAGES * (s // 2 + 1))

    def load_tables(sp):
        for dst, name, n in ((t_win, "t_win", 64), (t_cmp, "t_cmp", 64), (imp_add_s, "imp_add_s", 64),
                             (same_group, "same_group", 64), (seq_rows, "seq_rows", 8), (rows_seq, "rows_seq", 64),
                             (head_pick, "head_pick", 64)):
            sp.dma_start(dst[0:n], C[name]).then_inc(table_ready, 16)

    def stage3_sync(sp):
        for s in range(NB):
            stream_kv(sp, s, 0, SP_PAGES, kv_in)
            if s == 1:
                sp.wait_ge(hid_summed, 2 * NW)
                sp.dma_start(t_slc[0:64], C["t_slc"]).then_inc(t_slc_ready, 16)

    def stage3_pool(pool):
        for s in range(NB):
            stream_kv(pool, s, SP_PAGES, POOL_PAGES, kv_in_pool)

    def stage3_tensor(pe):
        pe.wait_ge(table_ready, 112)
        pe.wait_ge(q_sorted, 1)
        pe.wait_ge(kc_ready, NW)
        pe.wait_ge(vc_ready, NW)
        pe.wait_ge(gate_ready, 1)
        for r in range(NR):
            pe.transpose(pb(0)[:, NB * r:NB * r + NB], q_s2[0:NB, r].rearrange("p g d -> p (g d)"), ident[0:NB, 0:NB])
        for h in range(NH):
            pe.transpose(pb(0)[0:DH, 32 + NB * h:40 + NB * h], q_s[:, DH * h:DH * h + DH], ident[0:NB, 0:NB])
        for br, col in ((0, 256), (1, 512)):
            pe.transpose(pb(0)[:, 96 + NB * br:104 + NB * br], kv_new[:, col:col + P], ident[0:NB, 0:NB])
        pe.matmul(pb(1)[0:64, 0:24], seq_rows[0:NB, :], gate[0:NB, NT, :], start=True, stop=True).then_inc(prep_turned, 1)
        pe.wait_ge(prep_taken, 1)
        for s in range(NB):
            for g in range(NG):
                ins = pe.matmul(pb(1)[0:CMP_N, 64 + NH * s + NR * g:64 + NH * s + NR * g + NR], kcT_s[0:DH, s, g, 0:CMP_N],
                                qTs[0:DH, s, NR * g:NR * g + NR], start=True, stop=True)
        ins.then_inc(cmp_scored, 1)

        def turn_keys(s):
            wait_stream(pe, s)
            for j in range(3):
                n = 3 * s + j
                if n >= 4:
                    if n % 2 == 0:
                        pe.wait_ge(k_even, (n - 4) // 2 + 1)
                    else:
                        pe.wait_ge(k_odd, (n - 4) // 2 + 1)
                for c in range(4):
                    ins = pe.transpose(pb(4 + n % 4)[:, P * c:P * c + P], k_rows[s % 2][:, 4 * j + c, :], ident[:, :])
                ins.then_inc(k_tiles_turned, 1)

        def score(s):
            n = 3 * s + 3
            pe.wait_ge(k_even, (n + 1) // 2)
            pe.wait_ge(k_odd, n // 2)
            for c, b in enumerate((2, 3, 0)):
                ins = pe.matmul(pb(b)[0:64, :], q_pad[:, s, :], kTs[:, s % 2, 512 * c:512 * c + 512],
                                start=(s == 0), stop=(s == NB - 1), skip_group_check=True)
            ins.then_inc(seq_scored, 1)

        def turn_cmp():
            pe.wait_ge(cmp_cols, 1)
            pe.transpose(pb(1)[0:64, 128:128 + CMP_N], scT[0:CMP_N, :], ident[0:CMP_N, 0:CMP_N]).then_inc(cmp_turned, 1)

        def sum_importance():
            pe.wait_ge(pc_ready, 1)
            pe.matmul(pb(1)[0:64, 192:192 + CMP_N], same_group[0:64, :], s_cmp[0:64, :], start=True, stop=True)\
              .then_inc(imp_summed, 1)

        turn_keys(0)
        turn_cmp()
        for s in range(1, NB):
            turn_keys(s)
            score(s - 1)
            if s == 2:
                sum_importance()
        score(NB - 1)
        q_all_rows = q_bd.rearrange("p s h -> p (s h)")
        for br in range(2):
            ins = pe.matmul(pb(1)[0:64, 256 + 8 * br:264 + 8 * br], q_all_rows, knT[:, br, :], start=True, stop=True)
        ins.then_inc(seq_scored, 1)
        pe.wait_ge(k_even, 12)
        pe.wait_ge(k_odd, 12)
        pe.wait_ge(ps_ready, 3)
        for c in range(4):
            pe.transpose(pb(6)[:, 64 * c:64 * c + 64], s_win[0:64, P * c:P * c + P], ident[0:64, 0:64])
        for c in range(8):
            pe.transpose(pb(7)[:, 64 * c:64 * c + 64], s_slc[0:64, P * c:P * c + P], ident[0:64, 0:64])
        for br in range(2):
            pe.transpose(pb(1)[0:NB, 300 + 64 * br:364 + 64 * br], p_new[0:64, br, :], ident[0:64, 0:64])
        pe.transpose(pb(1)[0:CMP_N, 432:496], s_cmp[0:64, :], ident[0:64, 0:64]).then_inc(p_turned, 1)
        pe.wait_ge(pT_taken, 4)
        for s in range(NB):
            wait_stream(pe, s)
            cols = slice(NH * s, NH * s + NH)
            o = bank[1][0:NH, P * s:P * s + P]
            for br, col in ((0, 384), (1, 640)):
                pe.matmul(o, pnT[0:NB, br, cols], kv_new[:, col:col + P], start=(br == 0), stop=False, skip_group_check=True)
            pe.matmul(o, pcT_s[0:CMP_N, cols], vc_s[0:CMP_N, s, :], start=False, stop=False, skip_group_check=True)
            for c in range(NTILE):
                pr = pT_slc[:, c, cols] if c < 8 else pT_win[:, c - 8, cols]
                ins = pe.matmul(o, pr, v_rows[s][:, c, :], start=False, stop=(c == NTILE - 1), skip_group_check=True)
            ins.then_inc(seq_valued, 1)
        pe.wait_ge(o_rows_taken, 1)
        for s in range(NB):
            ins = pe.transpose(pb(0)[:, NH * s:NH * s + NH], o_rows[0:NH, s, :], ident[0:NH, 0:NH])
        ins.then_inc(o_rows_turned, 1)
        pe.wait_ge(oT_taken, 1)
        for h in range(NH):
            g = h // NR
            ins = pe.transpose(pb(7 - g)[0:NB, DH * h:DH * h + DH], oT_s[DH * g:DH * g + DH, h:64:NH],
                               ident[DH * g:DH * g + DH, DH * g:DH * g + DH])
        ins.then_inc(o_turned, 1)

    def stage3_scalar(act):
        stream_last(act, 0)
        stream_last(act, 1)
        for n in range(1, 3 * NB, 2):
            s, j = n // 3, n % 3
            act.wait_ge(k_tiles_turned, n + 1)
            if s >= 2:
                act.wait_ge(seq_scored, s - 1)
            act.activation(kTs[:, s % 2, 512 * j:512 * j + 512], pb(4 + n % 4), ACT.Copy).then_inc(k_odd, 1)
            if (n + 2) // 3 > s and s + 2 < NB:
                stream_last(act, s + 2)
            if n == 3:
                act.wait_ge(max_s, 1)
                act.activation(s_cmp[0:64, :], s_cmp[0:64, :], ACT.Exp, bias=st_s[0:64, 0:1],
                               accum_out=st_s[0:64, 3:4]).then_inc(exp_s, 1)
        act.wait_ge(max_s, 2)
        act.activation(s_win[0:64, :], s_win[0:64, :], ACT.Exp, bias=st_s[0:64, 1:2], accum_out=st_s[0:64, 4:5])\
           .then_inc(exp_s, 1)
        act.wait_ge(max_s, 3)
        act.activation(s_slc[0:64, :], s_slc[0:64, :], ACT.Exp, bias=st_s[0:64, 2:3], accum_out=st_s[0:64, 5:6])\
           .then_inc(exp_s, 1)
        act.wait_ge(p_turned, 1)
        act.activation(pT_slc, pb(7).rearrange("p (c n) -> p c n", c=8), ACT.Copy).then_inc(pT_taken, 1)

    def stage3_vector(dve, chain):
        link = chain.link
        dve.tensor_copy(q_s2[0:NB].rearrange("p r g d -> p g r d"), q_s.rearrange("p (g r d) -> p g r d", g=NG, r=NR))\
           .then_inc(q_sorted, 1)
        link(dve.memset(q_bd, 0.0))
        dve.wait_ge(kc_ready, NW)
        link(dve.memset(q_pad, 0.0))
        dve.wait_ge(prep_turned, 1)
        t4 = pb(0)[:, 0:32].rearrange("p (r s) -> p s r", r=NR)
        for g in range(NG):
            dve.tensor_copy(q_bd[DH * g:DH * g + DH, :, NR * g:NR * g + NR], t4[DH * g:DH * g + DH])
            a = q_pad[DH * g:DH * g + DH, 0, NR * g:NR * g + 1]
            own = bass.AP(tensor=a.tensor, offset=a.offset, ap=[a.ap[0], [64 + NH, NB], [1, NR]])
            dve.tensor_copy(own, t4[DH * g:DH * g + DH])
        dve.tensor_copy(qTs[0:DH], pb(0)[0:DH, 32:96].rearrange("p (h s) -> p s h", h=NH))
        dve.tensor_copy(knT, pb(0)[:, 96:112].rearrange("p (b s) -> p b s", b=2))
        dve.wait_ge(table_ready, 112)
        link(dve.tensor_tensor(gate_rows[0:64, :], pb(1)[0:64, 0:24], head_pick[0:64, :], ALU.mult))
        dve.tensor_reduce(gates_s[0:64, :], gate_rows[0:64, :].rearrange("p (h c) -> p c h", c=3), AX, ALU.add)\
           .then_inc(prep_taken, 1)
        dve.wait_ge(cmp_scored, 1)
        dve.tensor_copy(scT[0:CMP_N, :], pb(1)[0:CMP_N, 64:128]).then_inc(cmp_cols, 1)

        def take_keys(n):
            s, j = n // 3, n % 3
            dve.wait_ge(k_tiles_turned, n + 1)
            if s >= 2:
                dve.wait_ge(seq_scored, s - 1)
            dve.tensor_copy(kTs[:, s % 2, 512 * j:512 * j + 512], pb(4 + n % 4)).then_inc(k_even, 1)

        def cmp_probs():
            dve.wait_ge(cmp_turned, 1)
            link(dve.tensor_tensor(s_cmp[0:64, :], pb(1)[0:64, 128:128 + CMP_N], t_cmp[0:64, :], ALU.add))
            dve.tensor_reduce(st_s[0:64, 0:1], s_cmp[0:64, :], AX, ALU.max, negate=True).then_inc(max_s, 1)
            dve.wait_ge(exp_s, 1)
            link(dve.reciprocal(st_s[0:64, 6:7], st_s[0:64, 3:4]))
            dve.tensor_scalar(s_cmp[0:64, :], s_cmp[0:64, :], st_s[0:64, 6:7], None, ALU.mult).then_inc(pc_ready, 1)

        def select():
            link(dve.memset(imp_pad[0:64, :], 0.0))
            link(dve.memset(imp_s[0:64, :], 0.0))
            dve.wait_ge(imp_summed, 1)
            link(dve.tensor_copy(imp_pad[0:64, 1:1 + CMP_N], pb(1)[0:64, 192:192 + CMP_N]))
            link(dve.tensor_reduce(imp_s[0:64, 0:NBLK], block_windows(imp_pad[0:64, :]), AX, ALU.add))
            link(dve.tensor_tensor(imp_s[0:64, :], imp_s[0:64, :], imp_add_s[0:64, :], ALU.add))
            link(dve.max(top_s[0:64, :], imp_s[0:64, :]))
            link(dve.match_replace(out=imp_hit[0:64, :], in_to_replace=top_s[0:64, :], in_values=imp_s[0:64, :],
                                   imm_value=PICKED))
            link(dve.tensor_scalar(sel_s[0:64, :], imp_hit[0:64, :], 2e38, NEG, ALU.is_lt, ALU.mult))
            dve.tensor_scalar(s_cmp[0:64, :], s_cmp[0:64, :], gates_s[0:64, 0:1], None, ALU.mult).then_inc(ps_ready, 1)

        for n in range(0, 3 * NB, 2):
            take_keys(n)
            if n == 2:
                cmp_probs()
            if n == 8:
                select()
        dve.wait_ge(seq_scored, NB + 1)
        for br in range(2):
            link(dve.tensor_tensor(p_new[0:64, br, :], pb(1)[0:64, 256 + 8 * br:264 + 8 * br], rows_seq[0:64, :], ALU.mult))
        link(dve.tensor_reduce(s_slc[0:64, PAST:PAST + 1], p_new[0:64, 0, :], AX, ALU.add))
        link(dve.tensor_reduce(s_win[0:64, 512:513], p_new[0:64, 1, :], AX, ALU.add))
        link(dve.tensor_tensor(s_win[0:64, 0:512], pb(0)[0:64, :], t_win[0:64, 0:512], ALU.add))
        dve.tensor_reduce(st_s[0:64, 1:2], s_win[0:64, :], AX, ALU.max, negate=True).then_inc(max_s, 1)
        dve.wait_ge(t_slc_ready, 16)
        link(dve.tensor_tensor(s_slc[0:64, 0:PAST], bank[1][0:64, :], t_slc[0:64, 0:PAST], ALU.add))
        blocks = s_slc[0:64, 0:PAST].rearrange("p (j n) -> p j n", j=NBLK)
        link(dve.tensor_tensor(blocks, blocks, sel_s[0:64, 0:NBLK, None].to_broadcast([64, NBLK, SEL]), ALU.add))
        dve.tensor_reduce(st_s[0:64, 2:3], s_slc[0:64, :], AX, ALU.max, negate=True).then_inc(max_s, 1)
        for br, s in ((1, s_win), (0, s_slc)):
            dve.wait_ge(exp_s, 3 - br)
            w = st_s[0:64, 8 + br:9 + br]
            link(dve.reciprocal(w, st_s[0:64, 5 - br:6 - br]))
            link(dve.tensor_tensor(w, w, gates_s[0:64, 1 + br:2 + br], ALU.mult))
            last = s.shape[1] - 1
            link(dve.tensor_scalar(s[0:64, :], s[0:64, :], w, None, ALU.mult))
            dve.tensor_scalar(p_new[0:64, br, :], rows_seq[0:64, :], s[0:64, last:last + 1], None, ALU.mult)\
               .then_inc(ps_ready, 1)
        dve.wait_ge(p_turned, 1)
        dve.tensor_copy(pT_win, pb(6)[:, 0:256].rearrange("p (c n) -> p c n", c=4)).then_inc(pT_taken, 1)
        dve.tensor_copy(pnT[0:NB], pb(1)[0:NB, 300:428].rearrange("p (b n) -> p b n", b=2)).then_inc(pT_taken, 1)
        dve.tensor_copy(pcT_s[0:CMP_N, :], pb(1)[0:CMP_N, 432:496]).then_inc(pT_taken, 1)
        dve.wait_ge(seq_valued, NB)
        dve.tensor_copy(o_rows[0:NH].rearrange("p s n -> p (s n)"), bank[1][0:NH, :]).then_inc(o_rows_taken, 1)
        dve.wait_ge(o_rows_turned, 1)
        dve.tensor_copy(oT_s, pb(0)[:, 0:64]).then_inc(oT_taken, 1)
        dve.wait_ge(o_turned, 1)
        dve.tensor_copy(ob_s[:, 0:256], pb(7)[0:NB, 0:256]).then_inc(ob_s_ready, 1)
        dve.tensor_copy(ob_s[:, 256:512], pb(6)[0:NB, 256:512]).then_inc(ob_s_ready, 1)

    def block_windows(padded):
        a = padded[:, 0:80] if padded.shape[1] >= 80 else padded
        return bass.AP(tensor=a.tensor, offset=a.offset, ap=[a.ap[0], [4, NBLK], [1, 5]])

    wo = at(0, [KD, D])
    p_buf = [at(8192, [D]), at(9216, [D])]
    pT_buf = [at(10240, [512]), at(10752, [512]), samp[:, 0:512], samp[:, 512:1024]]
    qT = at(11264, [2, NG, 512])
    tmp = at(13312, [512])
    ob = at(0, [512], regC)
    obT = at(512, [4, P], regC)
    pc = at(1024, [NH, 64], regC)
    h2 = at(1536, [D], regC)
    imp_pad2 = at(2560, [NG, 65], regC)
    imp2 = at(2690, [NG, NBLK], regC)
    imp_hit2 = at(2722, [NG, NBLK], regC)
    top2 = at(2754, [NG, 8], regC)
    sel2 = samp[:, 1024:1216].rearrange("p (g n) -> p g n", g=NG)
    ssb, rb = small[:, 36:45], small[:, 45:54]
    ssh, rh = small[:, 54:63], small[:, 63:72]
    ssf, rf = small[:, 72:81], small[:, 81:90]
    neg_max = small[:, 90:94]
    nm_c, sum_c = small[:, 96:104], small[:, 104:112]
    row_sum = {"w": small[:, 112:120], "s": small[:, 120:128]}
    weight = small[:, 128:136]

    def key_tiles(i, kind):
        return list(range(max(0, i - 4), i + 1)) if kind == "w" else list(range(i + 1))

    units = [(i, kind, h) for i in range(NT) for kind, h in
             [("w", h) for h in range(NH)] + [("c", 0)] + [("s", h) for h in range(NH)]]
    NU = 2 * NH + 1
    events = [("QT", 0), ("CS", 0), ("CN", 0)]
    before = {}
    for i in range(NT):
        tail = NT if i == 0 else i - 1
        for place, name in ((3, "OBQ"), (4, "OBN"), (5, "OBT"), (6, "WO"), (8, "H2N"), (10, "H2T")):
            before.setdefault(NU * i + place, []).append((name, tail))
        if i >= 4:
            before.setdefault(NU * i + 8, []).append(("SELT", i))
        if i + 1 < NT:
            before.setdefault(NU * i + 11, []).append(("QT", i + 1))
            before.setdefault(NU * i + 14, []).append(("CS", i + 1))
            before.setdefault(NU * i + 15, []).append(("CN", i + 1))
            before.setdefault(NU * i + 17, []).append(("CI", i + 1))
    for u in range(len(units) + 3):
        events += before.get(u, [])
        if u < len(units) and units[u][1] != "c":
            events.append(("QK", u))
        if 0 <= u - 2 < len(units):
            events.append(("T", u - 2))
        if 0 <= u - 3 < len(units):
            events.append(("PV", u - 3))
    events += [(name, NT - 1) for name in ("OBQ", "OBN", "OBT", "SPLIT", "WO", "H2N")]
    events += [("GU", 0), ("H2T", NT - 1), ("GU", 1)]

    s_at, p_at, pt_at, o_at = {}, {}, {}, {}
    n_pt = 0
    for e in events:
        if e[0] in ("QT", "CS", "QK", "SELT", "OBT", "WO", "H2T"):
            s_at[e] = len(s_at)
        if e[0] == "QK":
            p_at[e[1]] = len(p_at)
        if e[0] == "T":
            i, kind, h = units[e[1]]
            n = 2 if kind == "c" else -(-len(key_tiles(i, kind)) // 4)
            pt_at[e[1]] = (n_pt, n)
            n_pt += n
    for u, (i, kind, h) in enumerate(units):
        o_at[u] = 3 * i + "wcs".index(kind)
    h2T_high = rounded("h2T_high", [P, KD, TOK], "hT")
    h2T_low = [rounded("h2T_low0", [P, 4, TOK], "q_all"), rounded("h2T_low1", [P, 4, TOK], "oaT")]

    qk_by_p = {n: u for u, n in p_at.items()}

    wo_ready, qaug_ready = sem("wo_ready"), [sem("qaug_ready0"), sem("qaug_ready1")]
    s_ready = sem("s_ready")
    s_taken = [sem("s_taken0"), sem("s_taken1")]
    max_ready = sem("max_ready")
    pt_ready, pt_taken = sem("pt_ready"), [sem("pt_taken0"), sem("pt_taken1")]
    pv_done, o_free = sem("pv_done"), sem("o_free")
    cmp_exp, pc_normed = sem("cmp_exp"), sem("pc_normed")
    sel_ready = sem("sel_ready")
    ob_ready, ob_squared, ob_inv, obn_ready = sem("ob_ready"), sem("ob_squared"), sem("ob_inv"), sem("obn_ready")
    x1_squared, x1_inv, h2_ready, h2_high = sem("x1_squared"), sem("x1_inv"), sem("h2_ready"), sem("h2_high")

    def s_pair(e):
        return bank[s_at[e] % 2]

    def wait_s(eng, e):
        eng.wait_ge(s_ready, s_at[e] + 1)

    def taken(ins, e):
        ins.then_inc(s_taken[s_at[e] % 2], 1)

    def wait_taken(eng, e):
        eng.wait_ge(s_taken[s_at[e] % 2], s_at[e] // 2 + 1)

    def tail_order(t):
        return 0 if t == NT else t + 1

    def load_qaug(sp, i):
        if i >= 2:
            last = s_at[("QK", NU * (i - 2) + NU - 1)]
            sp.wait_ge(s_ready, last + 1)
        sp.dma_start(qT[64:KAUG, i % 2].rearrange("p g n -> p (g n)"), C["qaug"][i]).then_inc(qaug_ready[i % 2], 16)

    def stage4_sync(sp):
        sp.wait_ge(ob_s_ready, 2)
        load_qaug(sp, 0)
        load_qaug(sp, 1)
        sp.dma_start(norm_g[:, :], norm_rows(A["norm2_g"][0]).to_broadcast([P, D])).then_inc(wo_ready, 16)
        for k in range(2):
            sp.dma_start(wo[:, 4 * k:4 * k + 4, :], A["w_out"][0, 512 * k:512 * k + 512].rearrange("(k p) n -> p k n", p=P))\
              .then_inc(wo_ready, 16)
        for i in range(2, NT):
            load_qaug(sp, i)

    def stage4_tensor(pe):
        pe.wait_ge(ob_s_ready, 2)
        for e in events:
            name, a = e
            if e in s_at and s_at[e] >= 2:
                pe.wait_ge(s_taken[s_at[e] % 2], s_at[e] // 2)
            if name == "QT":
                for h in range(NH):
                    ins = pe.transpose(s_pair(e)[0:DH, P * h:P * h + P], q_all[:, h // 2, P * a + DH * (h % 2):P * a + DH * (h % 2) + DH], ident[:, :])
                ins.then_inc(s_ready, 1)
            elif name == "CS":
                wait_taken(pe, ("QT", a))
                pe.wait_ge(qaug_ready[a % 2], 16 * (a // 2 + 1))
                out = s_pair(e)[:, 0:512].rearrange("p (h n) -> p h n", h=NH)
                pe.matmul(out, ident_bf[:, :], mask_cmp[:, a, None, :].to_broadcast([P, NH, 64]), start=True, stop=False,
                          skip_group_check=True)
                for h in range(NH):
                    g, r = h // NR, h % NR
                    ins = pe.matmul(out[:, h, 0:CMP_N], qT[0:KAUG, a % 2, g, P * r:P * r + P], kcT_p[0:KAUG, g, 0:CMP_N],
                                    start=False, stop=(h == NH - 1), skip_group_check=True)
                ins.then_inc(s_ready, 1)
            elif name == "QK":
                i, kind, h = units[a]
                g, r = h // NR, h % NR
                tiles = key_tiles(i, kind)
                if kind == "s" and i >= 4:
                    wait_taken(pe, ("SELT", i))
                q = qT[0:KAUG, i % 2, g, P * r:P * r + P]
                for c in range(0, len(tiles), 4):
                    part = tiles[c:c + 4]
                    masks = [(x, m) for x, m in ((i, mask_diag), (i - 4 if kind == "w" else -1, mask_low)) if x in part]
                    ins = pe.matmul(s_pair(e)[:, P * c:P * (c + len(part))], q,
                                    kT[0:KAUG, 2 * (kind == "w") + g, P * part[0]:P * part[-1] + P],
                                    start=True, stop=not masks, skip_group_check=True)
                    for n, (x, m) in enumerate(masks):
                        col = P * (x - tiles[0])
                        ins = pe.matmul(s_pair(e)[:, col:col + P], ident_bf[:, :], m[:, :], start=False,
                                        stop=(n == len(masks) - 1), skip_group_check=True)
                ins.then_inc(s_ready, 1)
            elif name == "SELT":
                pe.wait_ge(sel_ready, a - 3)
                for g in range(NG):
                    ins = pe.transpose(s_pair(e)[0:96, P * g:P * g + P], sel2[:, g, :], ident[:, :])
                ins.then_inc(s_ready, 1)
            elif name == "T":
                turn_probs(pe, a)
            elif name == "PV":
                values(pe, a)
            elif name == "OBT":
                n = rows(a)
                pe.wait_ge(obn_ready, tail_order(a) + 1)
                src = ob if a < NT else ob_s[:, :]
                for k in range(4):
                    ins = pe.transpose(s_pair(e)[:, P * k:P * k + n], src[0:n, P * k:P * k + P], ident[0:n, 0:n])
                ins.then_inc(s_ready, 1)
            elif name == "WO":
                n = rows(a)
                pe.wait_ge(wo_ready, 48)
                wait_taken(pe, ("OBT", a))
                for half in range(2):
                    for k in range(KD):
                        lhs = oaT[:, k, P * a:P * a + n] if k < 4 else obT[:, k - 4, 0:n]
                        ins = pe.matmul(s_pair(e)[0:n, 512 * half:512 * half + 512], lhs, wo[:, k, 512 * half:512 * half + 512],
                                        start=(k == 0), stop=(k == KD - 1))
                ins.then_inc(s_ready, 1)
            elif name == "GU":
                for t in range(NT):
                    if TCH * a < P * t + P and P * t < TCH * (a + 1):
                        wait_taken(pe, ("H2T", t))
                if a == 0:
                    pe.wait_ge(gu_high, 2)
                    pe.wait_ge(gu_low, 2)
                    for x in range(2):
                        pe.wait_ge(pt_taken[x], (n_pt + 1 - x) // 2)
                    pe.wait_ge(o_free, max(o_at.values()) + 1)
                gate_up_chunk(pe, 0, 0, a).then_inc(gu_ready, 1)
            elif name == "H2T":
                n = rows(a)
                pe.wait_ge(h2_ready, tail_order(a) + 1)
                for k in range(KD):
                    ins = pe.transpose(s_pair(e)[:, P * k:P * k + n], h2[0:n, P * k:P * k + P], ident[0:n, 0:n])
                ins.then_inc(s_ready, 1)

    def turn_probs(pe, u):
        i, kind, h = units[u]
        first, n_chunks = pt_at[u]
        if kind == "c":
            pe.wait_ge(pc_normed, i + 1)
        else:
            wait_taken(pe, ("QK", u))
        nk = len(key_tiles(i, kind)) if kind != "c" else NH
        for c in range(n_chunks):
            n = first + c
            if n >= 2:
                pe.wait_ge(pt_taken[n % 2], n // 2)
            for b in range(4 * c, min(4 * c + 4, nk)):
                col = P * (b - 4 * c)
                if kind == "c":
                    ins = pe.transpose(pb(4 + n % 2)[0:64, col:col + P], pc[:, b, :], ident[:, :])
                else:
                    ins = pe.transpose(pb(4 + n % 2)[:, col:col + P], p_buf[p_at[u] % 2][:, P * b:P * b + P], ident[:, :])
            ins.then_inc(pt_ready, 1)

    def values(pe, u):
        i, kind, h = units[u]
        first, n_chunks = pt_at[u]
        bank_o = pb(6 + o_at[u] % 2)
        if h == 0 and o_at[u] >= 2:
            pe.wait_ge(o_free, o_at[u] - 1)
        tiles = key_tiles(i, kind) if kind != "c" else list(range(NH))
        for c in range(n_chunks):
            n = first + c
            pe.wait_ge(pt_taken[n % 2], n // 2 + 1)
            for b in range(4 * c, min(4 * c + 4, len(tiles))):
                col = P * (b - 4 * c)
                if kind == "c":
                    g = b // NR
                    ins = pe.matmul(bank_o[:, DH * b:DH * b + DH], pT_buf[n % 4][0:CMP_N, col:col + P],
                                    vc_p[0:CMP_N, DH * g:DH * g + DH], start=True, stop=True, skip_group_check=True)
                else:
                    g = h // NR
                    ins = pe.matmul(bank_o[:, DH * h:DH * h + DH], pT_buf[n % 4][:, col:col + P],
                                    v_all[:, tiles[b], int(kind == "w"), DH * g:DH * g + DH],
                                    start=(b == 0), stop=(b == len(tiles) - 1), skip_group_check=True)
            ins.then_inc(pv_done, 1)

    def branch_ends(u):
        return units[u][1] == "c" or units[u][2] == NH - 1

    def take_chunks(eng, copy, u, parity):
        i, kind, h = units[u]
        first, n_chunks = pt_at[u]
        nk = len(key_tiles(i, kind)) if kind != "c" else NH
        for c in range(n_chunks):
            n = first + c
            if n % 2 != parity:
                continue
            w = P * min(4, nk - 4 * c)
            r = CMP_N if kind == "c" else P
            eng.wait_ge(pt_ready, n + 1)
            if n >= 4:
                eng.wait_ge(pv_done, n - 3)
            copy(pT_buf[n % 4][0:r, 0:w], pb(4 + n % 2)[0:r, 0:w]).then_inc(pt_taken[n % 2], 1)

    def stage4_scalar(act):
        def copy(dst, src):
            return act.activation(dst, src, ACT.Copy)

        for e in events:
            name, a = e
            if name == "CS":
                wait_taken(act, e)
                act.activation(pc, pc, ACT.Exp).then_inc(cmp_exp, 1)
            elif name == "QK":
                i, kind, h = units[a]
                w = P * len(key_tiles(i, kind))
                n = p_at[a]
                act.wait_ge(max_ready, n + 1)
                if n >= 2:
                    first, n_chunks = pt_at[qk_by_p[n - 2]]
                    act.wait_ge(pt_ready, first + n_chunks)
                taken(act.activation(p_buf[n % 2][:, 0:w], s_pair(e)[:, 0:w], ACT.Exp, bias=neg_max[:, n % 4:n % 4 + 1],
                                     accum_out=row_sum[kind][:, h:h + 1]), e)
            elif name == "T":
                take_chunks(act, copy, a, 1)
            elif name == "OBQ":
                n, k = rows(a), tail_order(a)
                act.wait_ge(ob_ready, k) if k else act.wait_ge(ob_s_ready, 2)
                if k:
                    wait_s(act, ("H2T", NT if k == 1 else a - 1))
                src = ob if a < NT else ob_s[:, :]
                act.activation(h2[0:n, 0:512], src[0:n, :], ACT.Square, accum_out=ssb[0:n, a:a + 1]).then_inc(ob_squared, 1)
            elif name == "WO":
                n, k = rows(a), tail_order(a)
                wait_taken(act, e)
                act.wait_ge(ob_squared, k + 1)
                act.activation(h2[0:n, :], x_all[0:n, a, :], ACT.Square, accum_out=ssh[0:n, a:a + 1]).then_inc(x1_squared, 1)
            elif name == "SPLIT":
                round_gate_up(act, 0, 0)
            elif name == "H2T":
                n = rows(a)
                wait_s(act, e)
                act.activation(h2T_high[:, :, P * a:P * a + n],
                               s_pair(e)[:, :].rearrange("p (k n) -> p k n", k=KD)[:, :, 0:n], ACT.Copy).then_inc(h2_high, 1)

    def stage4_pool(pool, chain):
        for e in events:
            name, a = e
            n = rows(a) if name in ("OBQ", "WO") else 0
            if name == "OBQ":
                pool.wait_ge(ob_squared, tail_order(a) + 1)
                inv_rms(pool, chain.link, ssb[0:n, a:a + 1], rb[0:n, a:a + 1], 512).then_inc(ob_inv, 1)
            elif name == "WO":
                pool.wait_ge(x1_squared, tail_order(a) + 1)
                inv_rms(pool, chain.link, ssh[0:n, a:a + 1], rh[0:n, a:a + 1], D).then_inc(x1_inv, 1)
            elif name == "SPLIT":
                low_gate_up(pool, 0, 0)

    def stage4_vector(dve, chain):
        link = chain.link

        def cmp_softmax(e, i):
            wait_s(dve, e)
            s = s_pair(e)[:, 0:512].rearrange("p (h n) -> p h n", h=NH)
            link(dve.tensor_reduce(nm_c, s, AX, ALU.max, negate=True))
            link(dve.tensor_scalar(nm_c, nm_c, -NEG / 10, None, ALU.min))
            if i:
                first, n_chunks = pt_at[NU * (i - 1) + NH]
                dve.wait_ge(pt_ready, first + n_chunks)
            taken(dve.tensor_tensor(pc, s, nm_c[:, :, None].to_broadcast([P, NH, 64]), ALU.add), e)

        def cmp_normalize(i):
            dve.wait_ge(cmp_exp, i + 1)
            link(dve.tensor_reduce(sum_c, pc, AX, ALU.add))
            link(dve.tensor_scalar(sum_c, sum_c, 1e-30, None, ALU.max))
            link(dve.reciprocal(sum_c, sum_c))
            dve.tensor_tensor(pc, pc, sum_c[:, :, None].to_broadcast([P, NH, 64]), ALU.mult).then_inc(pc_normed, 1)

        def select_blocks(i):
            if i >= 4:
                dve.wait_ge(pc_normed, i + 1)
                pc_g = pc.rearrange("p (g r) n -> p g n r", g=NG)
                for g in range(NG):
                    link(dve.tensor_reduce(imp_pad2[:, g, 1:65], pc_g[:, g], AX, ALU.add))
                for g in range(NG):
                    link(dve.tensor_reduce(imp2[:, g, :], block_windows(imp_pad2[:, g, :]), AX, ALU.add))
                link(dve.tensor_tensor(imp2, imp2, imp_add[:, i, None, :].to_broadcast([P, NG, NBLK]), ALU.add))
                for g in range(NG):
                    link(dve.max(top2[:, g, :], imp2[:, g, :]))
                for g in range(NG):
                    link(dve.match_replace(out=imp_hit2[:, g, :], in_to_replace=top2[:, g, :], in_values=imp2[:, g, :],
                                           imm_value=PICKED))
                dve.tensor_scalar(sel2[:, :, 64:80], imp_hit2, 2e38, NEG, ALU.is_lt, ALU.mult).then_inc(sel_ready, 1)

        def add_branch(u):
            i, kind, h = units[u]
            n = o_at[u]
            gate_h = gate[:, i, :].rearrange("p (h c) -> p c h", c=3)
            if kind == "c":
                w = gate_h[:, 0, :]
            else:
                w = weight
                link(dve.reciprocal(weight, row_sum[kind]))
                link(dve.tensor_tensor(weight, weight, gate_h[:, 1 if kind == "s" else 2, :], ALU.mult))
            dve.wait_ge(pv_done, sum(pt_at[u]))
            first = kind == "w"
            dst = (ob if first else tmp).rearrange("p (h d) -> p h d", h=NH)
            if first and i:
                dve.wait_ge(s_ready, s_at[("OBT", i - 1)] + 1)
            dve.tensor_tensor(dst, pb(6 + n % 2).rearrange("p (h d) -> p h d", h=NH), w[:, :, None].to_broadcast([P, NH, DH]),
                              ALU.mult).then_inc(o_free, 1)
            dve.wait_ge(o_free, n + 1)
            if not first:
                ins = dve.tensor_tensor(ob, ob, tmp, ALU.add)
                if kind == "s":
                    ins.then_inc(ob_ready, 1)
                else:
                    link(ins)

        link(dve.memset(samp[:, 1024:1216], 0.0))
        link(dve.memset(regC[:, 2560:2690], 0.0))
        for e in events:
            name, a = e
            if name == "QT":
                wait_s(dve, e)
                taken(dve.tensor_copy(qT[0:DH, a % 2].rearrange("p g n -> p (g n)"), s_pair(e)[0:DH, :]), e)
            elif name == "CS":
                cmp_softmax(e, a)
            elif name == "CN":
                cmp_normalize(a)
            elif name == "CI":
                select_blocks(a)
            elif name == "QK":
                i, kind, h = units[a]
                w = P * len(key_tiles(i, kind))
                wait_s(dve, e)
                n = p_at[a]
                dve.tensor_reduce(neg_max[:, n % 4:n % 4 + 1], s_pair(e)[:, 0:w], AX, ALU.max, negate=True)\
                   .then_inc(max_ready, 1)
            elif name == "SELT":
                wait_s(dve, e)
                dve.wait_ge(qaug_ready[a % 2], 16 * (a // 2 + 1))
                for g in range(NG):
                    rows_q = qT[64:96, a % 2, g].rearrange("p (r n) -> p r n", r=NR)
                    ins = dve.tensor_tensor(rows_q, rows_q, s_pair(e)[64:96, None, P * g:P * g + P].to_broadcast([32, NR, P]),
                                            ALU.add)
                taken(ins, e)
            elif name == "T":
                take_chunks(dve, dve.tensor_copy, a, 0)
            elif name == "PV" and branch_ends(a):
                add_branch(a)
            elif name == "OBN":
                n, k = rows(a), tail_order(a)
                src = ob if a < NT else ob_s[:, :]
                dve.wait_ge(ob_inv, k + 1)
                dve.scalar_tensor_tensor(out=src[0:n, :], in0=src[0:n, :], scalar=rb[0:n, a:a + 1], in1=normb_g[0:n, :],
                                         op0=ALU.mult, op1=ALU.mult).then_inc(obn_ready, 1)
            elif name == "OBT":
                n, k = rows(a), tail_order(a)
                wait_s(dve, e)
                taken(dve.tensor_copy(obT[:, :, 0:n], s_pair(e)[:, 0:512].rearrange("p (k n) -> p k n", k=4)[:, :, 0:n]), e)
            elif name == "WO":
                n, k = rows(a), tail_order(a)
                wait_s(dve, e)
                taken(dve.tensor_tensor(x_all[0:n, a, :], x_all[0:n, a, :], s_pair(e)[0:n, :], ALU.add), e)
            elif name == "H2N":
                n, k = rows(a), tail_order(a)
                dve.wait_ge(x1_inv, k + 1)
                dve.wait_ge(wo_ready, 48)
                dve.scalar_tensor_tensor(out=h2[0:n, :], in0=x_all[0:n, a, :], scalar=rh[0:n, a:a + 1], in1=norm_g[0:n, :],
                                         op0=ALU.mult, op1=ALU.mult).then_inc(h2_ready, 1)
            elif name == "H2T":
                n = rows(a)
                dve.wait_ge(h2_high, tail_order(a) + 1)
                for half in range(2):
                    ins = dve.tensor_tensor(h2T_low[half][:, :, P * a:P * a + n],
                                            s_pair(e)[:, 512 * half:512 * half + 512].rearrange("p (k n) -> p k n", k=4)[:, :, 0:n],
                                            h2T_high[:, 4 * half:4 * half + 4, P * a:P * a + n].bitcast(F32), ALU.subtract)
                taken(ins, e)

    FG = P
    NJ = FF // FG
    YH = 2 * XT
    TCH = TOK // 3
    w_low_at, w_high_at = [[8192, 9216, 10240], [1024, 2048, 3072]], [[11264, 12288, 0], [4096, 5120, 6144]]
    w_raw = [[at(w_low_at[i][x], [KD, FG]) for x in range(2)] + [at(w_low_at[i][2], [1, D])] for i in range(2)]
    w_low, w_high = ([[rounded(f"{part}{i}_{x}", [P, KD, FG] if x < 2 else [P, 1, D], "arena", word[i][x])[:, :, :]
                       for x in range(3)] for i in range(2)]
                     for part, word in (("w_low", w_low_at), ("w_high", w_high_at)))
    act_raw = [at(TOK * i, [TOK], kT_space) for i in (0, 1)]
    act_low = [rounded(f"act_low{i}", [P, TOK], "kT_space", TOK * i) for i in (0, 1)]
    act_high = [rounded("act_high0", [P, TOK], "kT_space", 2 * TOK), rounded("act_high1", [P, TOK], "v_all")]
    y_out = [at(D * i, [D], regC) for i in range(2)]
    sq_y = at(7168, [D])

    gu_loaded = [sem("gu_loaded0"), sem("gu_loaded1")]
    wd_loaded = [sem("wd_loaded0"), sem("wd_loaded1")]
    gu_high, gu_low, wd_high, wd_low = sem("gu_high"), sem("gu_low"), sem("wd_high"), sem("wd_low")
    gu_ready, silu_ready, act_ready = sem("gu_ready"), sem("silu_ready"), sem("act_ready")
    act_high_ready, act_low_ready = sem("act_high_ready"), sem("act_low_ready")
    y_ready, y_added = sem("y_ready"), sem("y_added")
    final_g_ready, y_squared, y_inv, y_normed = sem("final_g_ready"), sem("y_squared"), sem("y_inv"), sem("y_normed")
    y_stored = [sem("y_stored0"), sem("y_stored1")]

    def load_gate_up(sp, j, s, first):
        if not first:
            sp.wait_ge(gu_ready, j * 3 - 3)
        for x, name in enumerate(("w_gate", "w_up")):
            sp.dma_start(w_raw[s][x], A[name][0].rearrange("(k p) f -> p k f", p=P)[:, :, bass.ds(j * FG, FG)])\
              .then_inc(gu_loaded[s], 16)

    def load_down(sp, j, s, first):
        if not first:
            sp.wait_ge(y_ready, j * YH - YH)
        sp.dma_start(w_raw[s][2], A["w_down"][0].rearrange("(f p) n -> p f n", p=P)[:, bass.ds(j, 1), :])\
          .then_inc(wd_loaded[s], 16)

    def stage5_sync(sp):
        first, n_chunks = pt_at[len(units) - 1]
        sp.wait_ge(pt_ready, first + n_chunks)
        load_gate_up(sp, 0, 0, True)
        sp.wait_ge(pv_done, first + n_chunks)
        load_down(sp, 0, 0, True)
        sp.wait_ge(s_ready, s_at[("WO", NT - 1)] + 1)
        load_gate_up(sp, 1, 1, True)
        load_down(sp, 1, 1, True)
        sp.wait_ge(h2_ready, XT)
        sp.dma_start(norm_g[:, :], norm_rows(A["final_norm_g"]).to_broadcast([P, D])).then_inc(final_g_ready, 16)
        with sp.Fori(0, (NJ - 2) // 2) as i:
            for s in range(2):
                load_gate_up(sp, i * 2 + (2 + s), s, False)
                load_down(sp, i * 2 + (2 + s), s, False)
        for t in range(XT):
            sp.wait_ge(y_normed, t + 1)
            dst = O["y_prompt"][0, P * t:P * t + P] if t < NT else O["y_sample"][:, 0, :]
            sp.dma_start(dst, y_out[t % 2][0:rows(t), :]).then_inc(y_stored[t % 2], 16)

    def gate_bank(j, s, c):
        return 4 + 2 * c if early(j, c) else (s + c) % 2

    def up_bank(j, s, c):
        return gate_bank(j, s, c) + (1 if early(j, c) else 2)

    def early(j, c):
        return isinstance(j, int) and j == 0 and c < 2

    def gate_up_chunk(pe, j, s, c):
        cols = slice(TCH * c, TCH * c + TCH)
        for x, b in enumerate((gate_bank(j, s, c), up_bank(j, s, c))):
            out = pb(b)[:, 0:TCH]
            for k in range(KD):
                high, low = h2T_high[:, k, cols], h2T_low[k // 4][:, k % 4, cols]
                wh, wl = w_high[s][x][:, k, :], w_low[s][x][:, k, :]
                pe.matmul(out, wh, high, start=(k == 0), stop=False)
                pe.matmul(out, wh, low, start=False, stop=False)
                ins = pe.matmul(out, wl, high, start=False, stop=(k == KD - 1))
        return ins

    def stage5_tensor(pe):
        def gate_up(j, s):
            pe.wait_ge(gu_high, j * 2 + 2)
            pe.wait_ge(gu_low, j * 2 + 2)
            for c in range(3):
                pe.wait_ge(act_ready, j * 3 + (c - 1))
                gate_up_chunk(pe, j, s, c).then_inc(gu_ready, 1)

        def down(j, s, first):
            pe.wait_ge(act_high_ready, j * 3 + 3)
            pe.wait_ge(act_low_ready, j * 3 + 3)
            pe.wait_ge(wd_high, j + 1)
            pe.wait_ge(wd_low, j + 1)
            for t in range(XT):
                n = rows(t)
                ah, al = (a[s][:, P * t:P * t + n] for a in (act_high, act_low))
                for half in range(2):
                    if not (first and j == 0 and t < 2):
                        pe.wait_ge(y_added, j * YH + (2 * t + half - 3))
                    cols = slice(512 * half, 512 * half + 512)
                    out = bank[2 + (s + t) % 2][0:n, cols]
                    wh, wl = w_high[s][2][:, 0, cols], w_low[s][2][:, 0, cols]
                    pe.matmul(out, ah, wh, start=True, stop=False)
                    pe.matmul(out, ah, wl, start=False, stop=False)
                    pe.matmul(out, al, wh, start=False, stop=True).then_inc(y_ready, 1)

        wait_taken(pe, ("H2T", NT - 1))
        wait_taken(pe, ("WO", NT - 1))
        gate_up_chunk(pe, 0, 0, 2).then_inc(gu_ready, 1)
        gate_up(1, 1)
        down(0, 0, True)
        with pe.Fori(0, (NJ - 2) // 2) as i:
            gate_up(i * 2 + 2, 0)
            down(i * 2 + 1, 1, False)
            gate_up(i * 2 + 3, 1)
            down(i * 2 + 2, 0, False)
        down(NJ - 1, 1, False)

    def round_gate_up(act, j, s):
        act.wait_ge(gu_loaded[s], (j - s) * 16 + 32)
        for x in range(2):
            act.activation(w_high[s][x], w_raw[s][x], ACT.Copy).then_inc(gu_high, 1)

    def low_gate_up(pool, j, s):
        for x in range(2):
            pool.wait_ge(gu_high, j * 2 + (x + 1))
            pool.tensor_tensor(w_low[s][x], w_raw[s][x], w_high[s][x].bitcast(F32), ALU.subtract).then_inc(gu_low, 1)

    def stage5_scalar(act):
        def round_down(j, s):
            act.wait_ge(wd_loaded[s], (j - s) * 8 + 16)
            act.activation(w_high[s][2], w_raw[s][2], ACT.Copy).then_inc(wd_high, 1)

        def silu(j, s, first):
            if not first:
                act.wait_ge(y_ready, j * YH - YH)
            for c in range(4):
                if c < 3:
                    act.wait_ge(gu_ready, j * 3 + (c + 1))
                    act.activation(act_raw[s][:, TCH * c:TCH * c + TCH], pb(gate_bank(j, s, c))[:, 0:TCH], ACT.Silu)\
                       .then_inc(silu_ready, 1)
                if c >= 1:
                    cols = slice(TCH * (c - 1), TCH * c)
                    act.wait_ge(act_ready, j * 3 + c)
                    act.activation(act_high[s][:, cols], act_raw[s][:, cols], ACT.Copy).then_inc(act_high_ready, 1)

        def step(j, s, first=False, last=False):
            silu(j, s, first)
            if not last:
                round_gate_up(act, j + 1, 1 - s)
            round_down(j, s)

        round_gate_up(act, 1, 1)
        silu(0, 0, True)
        round_down(0, 0)
        step(1, 1, first=True)
        with act.Fori(0, (NJ - 4) // 2) as i:
            step(i * 2 + 2, 0)
            step(i * 2 + 3, 1)
        step(NJ - 2, 0)
        step(NJ - 1, 1, last=True)
        for t in range(XT):
            n = rows(t)
            act.wait_ge(y_added, (NJ - 1) * YH + 2 * t + 2)
            if t:
                act.wait_ge(y_squared, t)
            act.activation(sq_y[0:n, :], x_all[0:n, t, :], ACT.Square, accum_out=ssf[0:n, t:t + 1]).then_inc(y_squared, 1)

    def stage5_pool(pool, chain):
        def low_down(j, s):
            pool.wait_ge(wd_high, j + 1)
            pool.tensor_tensor(w_low[s][2], w_raw[s][2], w_high[s][2].bitcast(F32), ALU.subtract).then_inc(wd_low, 1)

        with pool.Fori(0, (NJ - 2) // 2) as i:
            for s in range(2):
                low_gate_up(pool, i * 2 + (1 + s), 1 - s)
                low_down(i * 2 + s, s)
        low_gate_up(pool, NJ - 1, 1)
        low_down(NJ - 2, 0)
        low_down(NJ - 1, 1)
        for t in range(XT):
            n = rows(t)
            pool.wait_ge(y_squared, t + 1)
            inv_rms(pool, chain.link, ssf[0:n, t:t + 1], rf[0:n, t:t + 1], D).then_inc(y_inv, 1)

    def stage5_vector(dve, chain):
        def gate_mul(j, s):
            for c in range(4):
                if c < 3:
                    a = act_raw[s][:, TCH * c:TCH * c + TCH]
                    dve.wait_ge(silu_ready, j * 3 + (c + 1))
                    dve.tensor_tensor(a, a, pb(up_bank(j, s, c))[:, 0:TCH], ALU.mult).then_inc(act_ready, 1)
                if c >= 1:
                    cols = slice(TCH * (c - 1), TCH * c)
                    dve.wait_ge(act_high_ready, j * 3 + c)
                    dve.tensor_tensor(act_low[s][:, cols], act_raw[s][:, cols], act_high[s][:, cols].bitcast(F32), ALU.subtract)\
                       .then_inc(act_low_ready, 1)

        def add_tile(j, s, t, first):
            n = rows(t)
            for half in range(2):
                x = x_all[0:n, t, 512 * half:512 * half + 512]
                dve.wait_ge(y_ready, j * YH + (2 * t + half + 1))
                if not first:
                    dve.wait_ge(y_added, j * YH + (2 * t + half + 1 - YH))
                dve.tensor_tensor(x, x, bank[2 + (s + t) % 2][0:n, 512 * half:512 * half + 512], ALU.add).then_inc(y_added, 1)

        def add(j, s, first=False):
            for t in range(XT):
                add_tile(j, s, t, first)

        def final_norm(t):
            n = rows(t)
            dve.wait_ge(y_inv, t + 1)
            if t >= 2:
                dve.wait_ge(y_stored[t % 2], 16 * (t // 2))
            dve.scalar_tensor_tensor(out=y_out[t % 2][0:n, :], in0=x_all[0:n, t, :], scalar=rf[0:n, t:t + 1],
                                     in1=norm_g[0:n, :], op0=ALU.mult, op1=ALU.mult).then_inc(y_normed, 1)

        gate_mul(0, 0)
        gate_mul(1, 1)
        add(0, 0, True)
        with dve.Fori(0, (NJ - 2) // 2) as i:
            gate_mul(i * 2 + 2, 0)
            add(i * 2 + 1, 1)
            gate_mul(i * 2 + 3, 1)
            add(i * 2 + 2, 0)
        dve.wait_ge(final_g_ready, 16)
        for t in range(XT + 1):
            if t < XT:
                add_tile(NJ - 1, 1, t, False)
            if t >= 1:
                final_norm(t - 1)

    block = ctx.enter_context(nc.Block())

    @block.sync
    def _(sp):
        stage1_sync(sp)
        stage2_sync(sp)
        stage3_sync(sp)
        stage4_sync(sp)
        stage5_sync(sp)
        for slot in range(2):
            sp.wait_ge(kv_stored[slot], stores_before(2 * NT + slot))
        sp.wait_ge(new_stored, 48)
        sp.wait_ge(gv_stored, 32)
        sp.wait_ge(win_copied, 16)
        sp.wait_ge(y_stored[0], 16 * 5)
        sp.wait_ge(y_stored[1], 16 * 4)

    @block.gpsimd
    def _(pool):
        chain = stage1_pool(pool)
        stage2_pool(pool)
        stage3_pool(pool)
        stage4_pool(pool, chain)
        stage5_pool(pool, chain)

    @block.tensor
    def _(pe):
        stage1_tensor(pe)
        stage2_tensor(pe)
        stage3_tensor(pe)
        stage4_tensor(pe)
        stage5_tensor(pe)

    @block.scalar
    def _(act):
        stage1_scalar(act)
        stage2_scalar(act)
        stage3_scalar(act)
        stage4_scalar(act)
        stage5_scalar(act)

    @block.vector
    def _(dve):
        chain = stage1_vector(dve)
        stage2_vector(dve, chain)
        stage3_vector(dve, chain)
        stage4_vector(dve, chain)
        stage5_vector(dve, chain)

    ctx.close()


def kernel(**inputs):
    import concourse.bacc as bacc
    from concourse.bass_utils import run_bass_kernel_spmd

    nc = bacc.Bacc("TRN2", target_bir_lowering=False, num_devices=1)
    arrays, A, C, O = {}, {}, {}, {}
    for name in RAW_INPUTS:
        a = np.ascontiguousarray(inputs[name])
        arrays["in_" + name] = a
        A[name] = nc.dram_tensor("in_" + name, a.shape, mybir.dt.from_np(a.dtype), kind="ExternalInput").ap()
    for name, a in constants().items():
        arrays["const_" + name] = a
        C[name] = nc.dram_tensor("const_" + name, a.shape, mybir.dt.from_np(a.dtype), kind="ExternalInput").ap()
    for name, shape in OUTPUTS:
        O[name] = nc.dram_tensor("out_" + name, shape, F32, kind="ExternalOutput").ap()
    build_program(nc, A, C, O)
    r = run_bass_kernel_spmd(nc, [arrays], core_ids=[0])
    return tuple(r.results[0]["out_" + name] for name, _ in OUTPUTS)
```
